# Optimizing a Trainium2 kernel written in Bass

```python
import jax, jax.numpy as jnp
from jax import lax
import numpy as np

D_MODEL = 1024
BATCH = 1
SEQ = 1024
DEPTH = 1

SB_HEADS = 8
SB_HEAD_DIM = 64
SB_WIDTH = SB_HEADS * SB_HEAD_DIM
SB_QBLOCK = 128
DN_HEADS = 8
DN_KEY_DIM = 64
DN_VAL_DIM = 128
DN_QK_WIDTH = DN_HEADS * DN_KEY_DIM
DN_V_WIDTH = DN_HEADS * DN_VAL_DIM
DN_CONV_CH = 2 * DN_QK_WIDTH + DN_V_WIDTH
DN_CONV_WIDTH = 4
DN_CHUNK = 64
D_FF = 2816
FFN_CONV_WIDTH = 3
NORM_EPS = 1e-6
L2_EPS = 1e-6
IN_SIZES = (3 * SB_WIDTH, DN_CONV_CH, DN_V_WIDTH, DN_HEADS, DN_HEADS, 2 * D_MODEL)
IN_WIDTH = int(sum(IN_SIZES))
IN_SPLITS = tuple(int(s) for s in np.cumsum(IN_SIZES)[:-1])

kernel_name = "hybrid_stickbreak_gdn_convffn_block"

def rmsnorm(x, w):
    xf = x.astype(jnp.float32)
    y = xf * lax.rsqrt(jnp.mean(xf * xf, axis=-1, keepdims=True) + NORM_EPS)
    return (y * w.astype(jnp.float32)).astype(x.dtype)

def modulate(h, shift, scale):
    return h * (1.0 + scale) + shift

def causal_dwconv(x, w):
    K, C = w.shape
    return lax.conv_general_dilated(
        x, w[:, None, :], window_strides=(1,), padding=[(K - 1, 0)],
        dimension_numbers=("NWC", "WIO", "NWC"), feature_group_count=C)

def stick_breaking_attention(q, k, v):
    S = q.shape[1]
    scale = q.shape[-1] ** -0.5
    outs = []
    for blk in range(S // SB_QBLOCK):
        s0 = blk * SB_QBLOCK
        end = s0 + SB_QBLOCK
        z = jnp.einsum("bthd,bshd->bhts", q[:, s0:end], k[:, :end]).astype(jnp.float32) * scale
        t_pos = s0 + jnp.arange(SB_QBLOCK)
        s_pos = jnp.arange(end)
        causal = s_pos[None, :] < t_pos[:, None]
        log_1m_beta = jnp.where(causal, jax.nn.log_sigmoid(-z), 0.0)
        log_stick = lax.cumsum(log_1m_beta, axis=3, reverse=True) - log_1m_beta
        A = jnp.where(causal, jnp.exp(jax.nn.log_sigmoid(z) + log_stick), 0.0)
        outs.append(jnp.einsum("bhts,bshd->bthd", A.astype(v.dtype), v[:, :end]))
    return jnp.concatenate(outs, axis=1)

def _l2norm(t):
    return t * lax.rsqrt(jnp.sum(t * t, axis=-1, keepdims=True) + L2_EPS)

def gated_delta_rule(q, k, v, g, beta):
    out_dtype = v.dtype
    f32 = jnp.float32
    b, s, h, dk = q.shape
    dv = v.shape[-1]
    C = DN_CHUNK
    n = s // C
    q = _l2norm(q.astype(f32)) * (dk ** -0.5)
    k = _l2norm(k.astype(f32))
    v = v.astype(f32)

    def to_chunks(t):
        return t.reshape(b, n, C, h, t.shape[-1]).transpose(0, 3, 1, 2, 4)

    qc, kc, vc = to_chunks(q), to_chunks(k), to_chunks(v)
    gcum = jnp.cumsum(g.astype(f32).reshape(b, n, C, h).transpose(0, 3, 1, 2), axis=-1)
    bc = beta.astype(f32).reshape(b, n, C, h).transpose(0, 3, 1, 2)[..., None]
    incl = jnp.tril(jnp.ones((C, C), bool))
    strict = jnp.tril(jnp.ones((C, C), bool), -1)
    diff = gcum[..., :, None] - gcum[..., None, :]
    decay = jnp.where(incl, jnp.exp(jnp.where(incl, diff, 0.0)), 0.0)
    kb = kc * bc
    L = jnp.where(strict, jnp.einsum("bhnid,bhnjd->bhnij", kb, kc) * decay, 0.0)
    eye = jnp.eye(C, dtype=f32)
    T = lax.linalg.triangular_solve(eye + L, jnp.broadcast_to(eye, L.shape),
                                    left_side=True, lower=True, unit_diagonal=True)
    u = jnp.einsum("bhnij,bhnjd->bhnid", T, vc * bc)
    w = jnp.einsum("bhnij,bhnjd->bhnid", T, kb * jnp.exp(gcum)[..., None])
    intra = jnp.where(incl, jnp.einsum("bhnid,bhnjd->bhnij", qc, kc) * decay, 0.0)

    def step(state, inp):
        q_i, k_i, u_i, w_i, g_i, a_i = inp
        v_new = u_i - jnp.einsum("bhck,bhkv->bhcv", w_i, state)
        o = (jnp.einsum("bhck,bhkv->bhcv", q_i * jnp.exp(g_i)[..., None], state)
             + jnp.einsum("bhij,bhjv->bhiv", a_i, v_new))
        g_last = g_i[..., -1:]
        k_dec = k_i * jnp.exp(g_last - g_i)[..., None]
        state = state * jnp.exp(g_last)[..., None] + jnp.einsum("bhck,bhcv->bhkv", k_dec, v_new)
        return state, o

    mv = lambda t: jnp.moveaxis(t, 2, 0)
    xs = (mv(qc), mv(kc), mv(u), mv(w), mv(gcum), mv(intra))
    state0 = jnp.zeros((b, h, dk, dv), f32)
    _, o = lax.scan(step, state0, xs)
    o = o.transpose(1, 0, 3, 2, 4).reshape(b, s, h, dv)
    return o.astype(out_dtype)

def setup_inputs(seed: int = 0) -> dict:
    key = jax.random.key(seed)
    ks = jax.random.split(key, 24)
    f32 = jnp.float32
    nrm = lambda k, shape, fan_in: jax.random.normal(k, shape, f32) * (fan_in ** -0.5)
    gain = lambda k, shape: 1.0 + 0.02 * jax.random.normal(k, shape, f32)
    x = jax.random.normal(ks[0], (BATCH, SEQ, D_MODEL), f32)
    c = jax.random.normal(ks[1], (BATCH, D_MODEL), f32)
    w_ada = nrm(ks[2], (DEPTH, D_MODEL, 6 * D_MODEL), D_MODEL)
    b_ada = 0.02 * jax.random.normal(ks[3], (DEPTH, 6 * D_MODEL), f32)
    norm1_w = gain(ks[4], (DEPTH, D_MODEL))
    w_in = nrm(ks[5], (DEPTH, D_MODEL, IN_WIDTH), D_MODEL)
    dn_conv_w = nrm(ks[6], (DEPTH, DN_CONV_WIDTH, DN_CONV_CH), DN_CONV_WIDTH)
    dn_A_log = jnp.log(jax.random.uniform(ks[7], (DEPTH, DN_HEADS), f32, 1.0, 16.0))
    dt = jnp.exp(jax.random.uniform(ks[8], (DEPTH, DN_HEADS), f32, jnp.log(0.001), jnp.log(0.1)))
    dn_dt_bias = dt + jnp.log(-jnp.expm1(-dt))
    dn_norm_w = gain(ks[9], (DEPTH, DN_VAL_DIM))
    w_proj_sb = nrm(ks[10], (DEPTH, SB_WIDTH, D_MODEL), SB_WIDTH)
    w_proj_dn = nrm(ks[11], (DEPTH, DN_V_WIDTH, D_MODEL), DN_V_WIDTH)
    w_out = nrm(ks[12], (DEPTH, D_MODEL, D_MODEL), D_MODEL)
    norm2_w = gain(ks[13], (DEPTH, D_MODEL))
    w_ffn_in = nrm(ks[14], (DEPTH, D_MODEL, 2 * D_FF), D_MODEL)
    ffn_conv_w = nrm(ks[15], (DEPTH, FFN_CONV_WIDTH, 2 * D_FF), FFN_CONV_WIDTH)
    ffn_conv_b = 0.02 * jax.random.normal(ks[16], (DEPTH, 2 * D_FF), f32)
    w_ffn_out = nrm(ks[17], (DEPTH, D_FF, D_MODEL), D_FF)
    final_norm_w = gain(ks[18], (D_MODEL,))
    return {"x": x, "c": c, "w_ada": w_ada, "b_ada": b_ada, "norm1_w": norm1_w, "w_in": w_in,
            "dn_conv_w": dn_conv_w, "dn_A_log": dn_A_log, "dn_dt_bias": dn_dt_bias,
            "dn_norm_w": dn_norm_w, "w_proj_sb": w_proj_sb, "w_proj_dn": w_proj_dn, "w_out": w_out,
            "norm2_w": norm2_w, "w_ffn_in": w_ffn_in, "ffn_conv_w": ffn_conv_w,
            "ffn_conv_b": ffn_conv_b, "w_ffn_out": w_ffn_out, "final_norm_w": final_norm_w}

def reference(x, c, w_ada, b_ada, norm1_w, w_in, dn_conv_w, dn_A_log, dn_dt_bias, dn_norm_w,
              w_proj_sb, w_proj_dn, w_out, norm2_w, w_ffn_in, ffn_conv_w, ffn_conv_b, w_ffn_out,
              final_norm_w):
    B, S, _ = x.shape
    c_act = jax.nn.silu(c)
    for l in range(DEPTH):
        mod = (c_act @ w_ada[l] + b_ada[l])[:, None, :]
        shift1, scale1, gate1, shift2, scale2, gate2 = jnp.split(mod, 6, axis=-1)

        h = modulate(rmsnorm(x, norm1_w[l]), shift1, scale1)
        proj = h @ w_in[l]
        sb_qkv, dn_qkv, dn_z, dn_b, dn_a, br_gates = jnp.split(proj, IN_SPLITS, axis=-1)

        sb_q, sb_k, sb_v = jnp.split(sb_qkv.reshape(B, S, 3, SB_HEADS, SB_HEAD_DIM), 3, axis=2)
        o_a = stick_breaking_attention(sb_q[:, :, 0], sb_k[:, :, 0], sb_v[:, :, 0]).reshape(B, S, SB_WIDTH)

        dn_qkv = jax.nn.silu(causal_dwconv(dn_qkv, dn_conv_w[l]))
        dq, dk_, dv_ = jnp.split(dn_qkv, (DN_QK_WIDTH, 2 * DN_QK_WIDTH), axis=-1)
        dq = dq.reshape(B, S, DN_HEADS, DN_KEY_DIM)
        dk_ = dk_.reshape(B, S, DN_HEADS, DN_KEY_DIM)
        dv_ = dv_.reshape(B, S, DN_HEADS, DN_VAL_DIM)
        beta = jax.nn.sigmoid(dn_b)
        g = -jnp.exp(dn_A_log[l]) * jax.nn.softplus(dn_a + dn_dt_bias[l])
        o_b = gated_delta_rule(dq, dk_, dv_, g, beta)
        o_b = rmsnorm(o_b, dn_norm_w[l]) * jax.nn.silu(dn_z.reshape(B, S, DN_HEADS, DN_VAL_DIM))
        o_b = o_b.reshape(B, S, DN_V_WIDTH)

        gate_a, gate_b = jnp.split(jax.nn.sigmoid(br_gates), 2, axis=-1)
        merged = gate_a * (o_a @ w_proj_sb[l]) + gate_b * (o_b @ w_proj_dn[l])
        x = x + gate1 * (merged @ w_out[l])

        h2 = modulate(rmsnorm(x, norm2_w[l]), shift2, scale2)
        u = causal_dwconv(h2 @ w_ffn_in[l], ffn_conv_w[l]) + ffn_conv_b[l]
        u_gate, u_up = jnp.split(u, 2, axis=-1)
        x = x + gate2 * ((jax.nn.silu(u_gate) * u_up) @ w_ffn_out[l])
    return rmsnorm(x, final_norm_w)


_drawn_inputs = setup_inputs


def setup_inputs(seed=0):
    import zlib

    import numpy as np

    out = dict(_drawn_inputs(seed))
    spreads = {}
    factors = {'norm1_w': 4.805,
     'dn_norm_w': 8.0,
     'norm2_w': 12.351,
     'ffn_conv_b': 15.165,
     'final_norm_w': 8.489}
    for name, (base, spread) in spreads.items():
        noise = np.random.default_rng([zlib.crc32(name.encode()), seed]).standard_normal(out[name].shape)
        drawn = base * np.exp(spread * noise) if base else spread * noise
        out[name] = __import__('jax').numpy.asarray(drawn.astype(out[name].dtype))
    for name, factor in factors.items():
        out[name] = (out[name] * factor).astype(out[name].dtype)
    return out
```

```python
import concourse.bass as bass
from concourse import mybir
from contextlib import ExitStack

F32 = mybir.dt.float32
F32R = mybir.dt.float32r
BF16 = mybir.dt.bfloat16
ALU = mybir.AluOpType
ACT = mybir.ActivationFunctionType
AX = mybir.AxisListType

P = 128
D = 1024
S = 1024
KD = D // P
HALF = 512
EPS = 1e-6
HEADS = 8
N_PROJ = 53
SB_BLOCKS, CONV_END, Z_END, GATE_END = 12, 28, 36, 52
W_EXTRA = 4
BLK = KD * P + W_EXTRA
D_FF = 2816
KF = D_FF // P
NEG = -1e30

C_IDENT, C_ONES, C_ONES64, C_INCL, C_STRICT, C_SEL = 0, 128, 256, 384, 512, 640
C_NEG = 640 + 512
C_EVEN, C_ODD = C_NEG + 128, C_NEG + 256
C_RESET = C_NEG + 384
C_END = C_RESET + 1024


def three(hi_w, lo_w, hi_x, lo_x):
    return ((hi_w, hi_x), (hi_w, lo_x), (lo_w, hi_x))


def as_f32(ap):
    return ap.bitcast(F32)


class Scope:

    def __init__(self, nc, name, side="left"):
        self.nc, self.name, self.side, self.stack = nc, name, side, ExitStack()
        self.signals = []

    def sb(self, name, shape, dt=F32):
        return self.stack.enter_context(self.nc.sbuf_tensor(f"{self.name}_{name}", shape, dt, side=self.side))

    def ps(self, name, shape, dt=F32):
        return self.stack.enter_context(self.nc.psum_tensor(f"{self.name}_ps_{name}", shape, dt))

    def sem(self, name):
        signal = self.stack.enter_context(self.nc.semaphore(f"{self.name}_{name}"))
        self.signals.append(signal)
        return signal

    def sems(self, name, n):
        return [self.sem(f"{name}{i}") for i in range(n)]

    def close(self):
        self.stack.close()
        for signal in self.signals:
            self.nc.sync.sem_clear(signal)


def condition(nc, g, d):
    ph = Scope(nc, "cond")
    PIECE = 4
    xT = ph.sb("xT", [P, KD, S])
    wa = ph.sb("wa", [P, 2, PIECE, D])
    acc = ph.sb("acc", [P, 2, D])
    sq = ph.sb("sq", [P, 2, S])
    std = ph.sb("std", [P, S])
    rstd = ph.sb("rstd", [P, S])
    hf = ph.sb("hf", [P, 2, S])
    c_in = ph.sb("c_in", [P, KD])
    ps_ss = ph.ps("ss", [P, S])
    ps_mod = ph.ps("mod", [P, 2 * KD])
    ld_small, ld_c = ph.sem("ld_small"), ph.sem("ld_c")
    ld_x = ph.sems("ld_x", KD)
    ld_w = ph.sems("ld_w", 2)
    c_done, acc_free, acc_done = ph.sem("c_done"), ph.sem("acc_free"), ph.sem("acc_done")
    sq_done, ss_done, std_done, rstd_done = (ph.sem(n) for n in ("sq_done", "ss_done", "std_done", "rstd_done"))
    mod_done, mod_copied, step, xn_done = (ph.sem(n) for n in ("mod_done", "mod_copied", "step", "xn_done"))
    eps_set = ph.sem("eps_set")
    h_done, hi_done, lo_done = ph.sem("h_done"), ph.sem("hi_done"), ph.sem("lo_done")
    block = ph.stack.enter_context(nc.Block())

    @block.sync
    def _(sp):
        sp.dma_start(c_in[:], d["c"]).then_inc(ld_c, 16)
        sp.dma_start(g.const[:], d["const"]).then_inc(ld_small, 16)
        for name in ("b_ada", "norms", "dn_norm", "dn_head"):
            sp.dma_start(g.small[name][:], d[name]).then_inc(ld_small, 16)
        for k in range(KD):
            sp.dma_start(xT[:, k, :], d["xT"][k]).then_inc(ld_x[k], 16)
        for n in range(4):
            if n >= 2:
                sp.wait_ge(acc_free, n - 1)
            sp.dma_start(wa[:, n % 2], d["w_ada"][n // 2, n % 2]).then_inc(ld_w[n % 2], 16)

    @block.scalar
    def _(act):
        act.wait_ge(ld_c, 16)
        act.activation(g.c_act[:], c_in[:], ACT.Silu).then_inc(c_done, 1)
        for k in range(KD):
            act.wait_ge(ld_x[k], 16)
            if k >= 2:
                act.wait_ge(ss_done, k - 1)
            act.activation(sq[:, k % 2], xT[:, k], ACT.Square).then_inc(sq_done, 1)
        act.wait_ge(ss_done, KD)
        act.wait_ge(eps_set, 1)
        act.activation(std[:], ps_ss[:], ACT.Sqrt, scale=1.0 / D, bias=g.eps[:]).then_inc(std_done, 1)
        for k in range(KD):
            act.wait_ge(xn_done, k + 1)
            act.wait_ge(step, 2)
            if k >= 2:
                act.wait_ge(lo_done, k - 1)
            act.activation(hf[:, k % 2], xT[:, k], ACT.Identity, scale=g.mod[:, KD + k:KD + k + 1],
                           bias=g.mod[:, k:k + 1]).then_inc(h_done, 1)
            act.wait_ge(h_done, k + 1)
            act.activation(g.h_hi[:, k], hf[:, k % 2], ACT.Copy).then_inc(hi_done, 1)

    @block.gpsimd
    def _(pool):
        pool.memset(g.eps[:], EPS).then_inc(eps_set, 1)
        pool.wait_ge(rstd_done, 1)
        for k in range(KD):
            pool.tensor_tensor(xT[:, k], xT[:, k], rstd[:], ALU.mult).then_inc(xn_done, 1)

    @block.vector
    def _(dve):
        dve.wait_ge(c_done, 1)
        for n in range(4):
            dve.wait_ge(ld_w[n % 2], 16 * (n // 2 + 1))
            for k in range(PIECE):
                kk = n % 2 * PIECE + k
                c_k = g.c_act[:, kk:kk + 1]
                dst = acc[:, n // 2]
                if kk == 0:
                    ins = dve.tensor_scalar(dst, wa[:, 0, 0], c_k, None, ALU.mult)
                else:
                    dve.wait_ge(acc_done, n // 2 * KD + kk)
                    ins = dve.scalar_tensor_tensor(dst, wa[:, n % 2, k], c_k, dst, ALU.mult, ALU.add)
                ins.then_inc(acc_done, 1)
            dve.wait_ge(acc_done, 4 * n + 4)
            dve.sem_inc(acc_free, 1)
        dve.wait_ge(std_done, 1)
        dve.reciprocal(rstd[:], std[:]).then_inc(rstd_done, 1)
        dve.wait_ge(ld_small, 16 * 5)
        dve.wait_ge(mod_done, 2)
        dve.tensor_tensor(g.mod[:, 0:2 * KD], ps_mod[:], g.small["b_ada"][:, 0:2 * KD], ALU.add).then_inc(step, 1)
        dve.wait_ge(step, 1)
        dve.scalar_tensor_tensor(g.mod[:, KD:2 * KD], g.mod[:, KD:2 * KD], 1.0, g.small["norms"][:, 0:KD],
                                 ALU.add, ALU.mult).then_inc(step, 1)
        for k in range(KD):
            dve.wait_ge(hi_done, k + 1)
            dve.tensor_tensor(g.h_lo[:, k], hf[:, k % 2], as_f32(g.h_hi[:, k]), ALU.subtract).then_inc(lo_done, 1)

    @block.tensor
    def _(pe):
        ones = g.const[:, C_ONES:C_ONES + P]
        pe.wait_ge(ld_small, 16 * 5)
        for k in range(KD):
            pe.wait_ge(sq_done, k + 1)
            for t in range(2):
                mm = pe.matmul(ps_ss[:, t * HALF:(t + 1) * HALF], ones, sq[:, k % 2, t * HALF:(t + 1) * HALF],
                               start=k == 0, stop=k == KD - 1)
            mm.then_inc(ss_done, 1)
        for grp in range(2):
            pe.wait_ge(acc_done, KD * (grp + 1))
            for m in range(KD):
                mm = pe.matmul(ps_mod[:, grp * KD + m:grp * KD + m + 1], acc[:, grp, m * P:(m + 1) * P],
                               ones[:, 0:1], start=True, stop=True)
            mm.then_inc(mod_done, 1)

    ph.close()


def project(nc, g, d):
    ph = Scope(nc, "proj")
    raw = ph.sb("raw", [P, 2, BLK])
    w_hi = ph.sb("w_hi", [P, 2, KD, P], F32R)
    w_lo = ph.sb("w_lo", [P, 2, KD, P], F32R)
    taps = ph.sb("taps", [P, 2, W_EXTRA])
    stage = ph.sb("stage", [P, 2, S])
    wa = ph.sb("wa", [P, 2, 4, D])
    acc = ph.sb("acc", [P, 2, D])
    ps = [ph.ps(f"ps{i}", [P, S]) for i in range(2)]
    ps_mod = ph.ps("mod", [P, 4 * KD])
    ld = ph.sems("ld", 2)
    st = ph.sems("st", 2)
    ld_a = ph.sems("ld_a", 2)
    hi_done, lo_done, mm_done, out_done = (ph.sem(n) for n in ("hi_done", "lo_done", "mm_done", "out_done"))
    scaled, conv, acc_done, acc_free = (ph.sem(n) for n in ("scaled", "conv", "acc_done", "acc_free"))
    mod_done, step = ph.sem("mod_done"), ph.sem("step")
    block = ph.stack.enter_context(nc.Block())
    LAST = N_PROJ - 1

    def rows(n):
        return d["proj"][n] if isinstance(n, int) else d["proj"][bass.ds(n, 1)].rearrange("o p n -> p (o n)")

    def wrows(n):
        return d["w_in"][n] if isinstance(n, int) else d["w_in"][bass.ds(n, 1)].rearrange("o p n -> p (o n)")

    @block.sync
    def _(sp):
        def block_io(j, s, load=True):
            n = 2 * j + s
            if load:
                sp.wait_ge(lo_done, n + 1)
                sp.dma_start(raw[:, s], wrows(n + 2)).then_inc(ld[s], 16)
            sp.wait_ge(out_done, n + 1)
            sp.dma_start(rows(n), stage[:, s]).then_inc(st[s], 16)

        for s in range(2):
            sp.dma_start(raw[:, s], wrows(s)).then_inc(ld[s], 16)
        for j in range(SB_BLOCKS // 2):
            for s in range(2):
                n = 2 * j + s
                if n < 8:
                    if n >= 2:
                        sp.wait_ge(acc_free, n - 1)
                    sp.dma_start(wa[:, n % 2], d["w_ada"][2 + n // 2, n % 2]).then_inc(ld_a[n % 2], 16)
                block_io(j, s)
        with sp.Fori(SB_BLOCKS // 2, LAST // 2 - 1) as j:
            for s in range(2):
                block_io(j, s)
        block_io(LAST // 2 - 1, 0)
        block_io(LAST // 2 - 1, 1, load=False)
        block_io(LAST // 2, 0, load=False)
        sp.wait_ge(st[0], 16 * (LAST // 2 + 1))
        sp.wait_ge(st[1], 16 * (LAST // 2))

    @block.scalar
    def _(act):
        def split(j, s):
            n = 2 * j + s
            act.wait_ge(ld[s], 16 * (j + 1))
            if not (isinstance(n, int) and n < 2):
                act.wait_ge(mm_done, n - 1)
            act.activation(w_hi[:, s], raw[:, s, 0:KD * P].rearrange("p (k m) -> p k m", k=KD), ACT.Copy)\
               .then_inc(hi_done, 1)

        def evacuate(j, s, kind, nconv=None):
            n = 2 * j + s
            act.wait_ge(mm_done, n + 1)
            if not (isinstance(n, int) and n < 2):
                act.wait_ge(st[s], 16 * j)
            if kind == "conv":
                act.activation(stage[:, s], ps[s][:], ACT.Copy, scale=taps[:, s, 3:4]).then_inc(scaled, 1)
                act.wait_ge(conv, 3 * (n - SB_BLOCKS) + 3)
                act.activation(stage[:, s], stage[:, s], ACT.Silu).then_inc(out_done, 1)
            else:
                act.activation(stage[:, s], ps[s][:], kind).then_inc(out_done, 1)

        def step_blocks(j, kind):
            split(j, 1)
            evacuate(j, 0, kind)
            split(j + 1, 0)
            evacuate(j, 1, kind)

        split(0, 0)
        for j in range(SB_BLOCKS // 2):
            step_blocks(j, ACT.Copy)
        with act.Fori(SB_BLOCKS // 2, CONV_END // 2) as j:
            step_blocks(j, "conv")
        with act.Fori(CONV_END // 2, Z_END // 2) as j:
            step_blocks(j, ACT.Silu)
        with act.Fori(Z_END // 2, GATE_END // 2) as j:
            step_blocks(j, ACT.Sigmoid)
        evacuate(LAST // 2, 0, ACT.Copy)

    @block.gpsimd
    def _(pool):
        def low(j, s):
            n = 2 * j + s
            pool.wait_ge(hi_done, n + 1)
            if not (isinstance(n, int) and n < 2):
                pool.wait_ge(out_done, n - 1)
            pool.tensor_tensor(w_lo[:, s], raw[:, s, 0:KD * P].rearrange("p (k m) -> p k m", k=KD),
                               as_f32(w_hi[:, s]), ALU.subtract)
            pool.tensor_copy(taps[:, s], raw[:, s, KD * P:BLK]).then_inc(lo_done, 1)

        low(0, 0)
        low(0, 1)
        with pool.Fori(1, LAST // 2) as j:
            for s in range(2):
                low(j, s)
        low(LAST // 2, 0)

    @block.vector
    def _(dve):
        for n in range(8):
            dve.wait_ge(ld_a[n % 2], 16 * (n // 2 + 1))
            if n % 2 == 0 and n >= 4:
                dve.wait_ge(mod_done, n // 2 - 1)
            for k in range(4):
                kk = n % 2 * 4 + k
                dst, c_k = acc[:, n // 2 % 2], g.c_act[:, kk:kk + 1]
                if kk == 0:
                    ins = dve.tensor_scalar(dst, wa[:, 0, 0], c_k, None, ALU.mult)
                else:
                    dve.wait_ge(acc_done, n // 2 * KD + kk)
                    ins = dve.scalar_tensor_tensor(dst, wa[:, n % 2, k], c_k, dst, ALU.mult, ALU.add)
                ins.then_inc(acc_done, 1)
            dve.wait_ge(acc_done, 4 * n + 4)
            dve.sem_inc(acc_free, 1)
        dve.wait_ge(mod_done, 4)
        dve.tensor_tensor(g.mod[:, 2 * KD:6 * KD], ps_mod[:], g.small["b_ada"][:, 2 * KD:6 * KD], ALU.add)\
           .then_inc(step, 1)
        dve.wait_ge(step, 1)
        dve.scalar_tensor_tensor(g.mod[:, 4 * KD:5 * KD], g.mod[:, 4 * KD:5 * KD], 1.0,
                                 g.small["norms"][:, KD:2 * KD], ALU.add, ALU.mult).then_inc(step, 1)
        with dve.Fori(SB_BLOCKS // 2, CONV_END // 2) as j:
            for s in range(2):
                i = 2 * j + s - SB_BLOCKS
                dve.wait_ge(scaled, i + 1)
                for back in (1, 2, 3):
                    if back > 1:
                        dve.wait_ge(conv, 3 * i + back - 1)
                    dve.scalar_tensor_tensor(stage[:, s, back:S], ps[s][:, 0:S - back], taps[:, s, 3 - back:4 - back],
                                             stage[:, s, back:S], ALU.mult, ALU.add).then_inc(conv, 1)

    @block.tensor
    def _(pe):
        def product(j, s):
            n = 2 * j + s
            pe.wait_ge(lo_done, n + 1)
            if not (isinstance(n, int) and n < 2):
                pe.wait_ge(out_done, n - 1)
            for k in range(KD):
                hi, lo = w_hi[:, s, k], w_lo[:, s, k]
                for i, (w, x) in enumerate(three(hi, lo, g.h_hi[:, k], g.h_lo[:, k])):
                    for t in range(2):
                        mm = pe.matmul(ps[s][:, t * HALF:(t + 1) * HALF], w, x[:, t * HALF:(t + 1) * HALF],
                                       start=k == 0 and i == 0, stop=k == KD - 1 and i == 2)
            mm.then_inc(mm_done, 1)

        ones = g.const[:, C_ONES:C_ONES + 1]
        for j in range(SB_BLOCKS // 2):
            for s in range(2):
                product(j, s)
                n = 2 * j + s
                if n >= 4 and n % 2 == 0:
                    grp = n // 2 - 2
                    pe.wait_ge(acc_done, KD * (grp + 1))
                    for m in range(KD):
                        mm = pe.matmul(ps_mod[:, grp * KD + m:grp * KD + m + 1],
                                       acc[:, grp % 2, m * P:(m + 1) * P], ones, start=True, stop=True)
                    mm.then_inc(mod_done, 1)
        with pe.Fori(SB_BLOCKS // 2, LAST // 2) as j:
            for s in range(2):
                product(j, s)
        product(LAST // 2, 0)

    ph.close()


def stick(nc, g, d):
    ph = Scope(nc, "stick")
    PAIRS, TILES, UNITS = HEADS // 2, S // P, 16
    q_raw, k_raw = ph.sb("q_raw", [P, 2, S]), ph.sb("k_raw", [P, 2, S])
    v_raw = ph.sb("v_raw", [P, S])
    q_both = ph.sb("q_both", [P, 2, S], F32R)
    k_hi, k_lo = ph.sb("k_hi", [P, 2, S], F32R), ph.sb("k_lo", [P, 2, S], F32R)
    v_hi, v_lo = (ph.sb(n, [P, TILES, 2, P], F32R) for n in ("v_hi", "v_lo"))
    a_hi, a_lo = (ph.sb(n, [P, 2, TILES, HALF], F32R) for n in ("a_hi", "a_lo"))
    beta, rest, weight = (ph.sb(n, [P, 2, S]) for n in ("beta", "rest", "weight"))
    stick_left = ph.sb("stick_left", [P, 2, S + 1])
    o_out = ph.sb("o_out", [P, PAIRS, S])
    ident_b, mask_b = ph.sb("ident_b", [P, P], BF16), ph.sb("mask_b", [P, P], BF16)
    ps_z = [ph.ps(f"z{i}", [P, S]) for i in range(2)]
    ps_t = [ph.ps(f"t{i}", [P, 4, P]) for i in range(2)]
    ps_o = [ph.ps(f"o{i}", [P, HALF]) for i in range(2)]
    ld_qk, ld_v, st = ph.sem("ld_qk"), ph.sem("ld_v"), ph.sem("st")
    setup, q_hi_done, prep_done, q_done = (ph.sem(n) for n in ("setup", "q_hi_done", "prep_done", "q_done"))
    z_done, rest_done, beta_done, scan_done, w_done = (ph.sem(n) for n in ("z_done", "rest_done", "beta_done", "scan_done", "w_done"))
    t_done, hi_done, lo_done, av_done, o_done = (ph.sem(n) for n in ("t_done", "hi_done", "lo_done", "av_done", "o_done"))
    block = ph.stack.enter_context(nc.Block())
    SCALE = 64 ** -0.5
    ident = g.const[:, C_IDENT:C_IDENT + P]

    tile_of = [4 * (u // 8) + u % 4 for u in range(UNITS)]
    groups = [(u, j0) for u in range(UNITS) for j0 in range(0, tile_of[u] + 1, 4)]
    VG = 2
    first_group = [VG + groups.index((u, 0)) for u in range(UNITS)] + [VG + len(groups)]
    GROUPS = VG + len(groups)

    def start(u):
        return S - (tile_of[u] + 1) * P

    @block.sync
    def _(sp):
        def pair_rows(n):
            return d["proj"][n] if isinstance(n, int) else d["proj"][bass.ds(n, 1)].rearrange("o p n -> p (o n)")

        def load(p):
            for raw, b in ((q_raw, p), (k_raw, p + PAIRS)):
                rows = pair_rows(b)
                for h in range(2):
                    for copy in range(2):
                        sp.dma_start(raw[copy * 64:copy * 64 + 64, h], rows[h * 64:h * 64 + 64]).then_inc(ld_qk, 16)
            sp.dma_start(v_raw[:], pair_rows(p + 2 * PAIRS)).then_inc(ld_v, 16)

        def store(p):
            for half in range(2):
                sp.wait_ge(o_done, 2 * p + half + 1)
                cols = slice(half * HALF, half * HALF + HALF)
                sp.dma_start(d["o_a"][p][:, cols], o_out[:, p, cols]).then_inc(st, 16)

        load(0)
        for p in range(PAIRS):
            if p + 1 < PAIRS:
                sp.wait_ge(prep_done, 3 * p + 3)
                sp.wait_ge(t_done, GROUPS * p + VG)
                load(p + 1)
            store(p)
        sp.wait_ge(st, 32 * PAIRS)

    @block.scalar
    def _(act):
        def sigmoids(p, u):
            s, o = u % 2, start(u)
            act.wait_ge(z_done, UNITS * p + u + 1)
            if u >= 2:
                act.wait_ge(w_done, UNITS * p + u - 1)
            z = ps_z[s][:, 0:S - o]
            act.activation(rest[:, s, o:S], z, ACT.Sigmoid, scale=-SCALE).then_inc(rest_done, 1)
            act.activation(beta[:, s, o:S], z, ACT.Sigmoid, scale=SCALE).then_inc(beta_done, 1)

        def high(p, u):
            h, t0 = u // 4 % 2, u % 4 * P
            if u // 8 == 1 and u % 4 == 0:
                act.wait_ge(av_done, 4 * p + h + 1)
            for j0 in range(0, tile_of[u] + 1, 4):
                n = first_group[u] + j0 // 4
                w = min(4, tile_of[u] + 1 - j0)
                act.wait_ge(t_done, GROUPS * p + n + 1)
                act.activation(a_hi[:, h, j0:j0 + w, t0:t0 + P], ps_t[n % 2][:, 0:w], ACT.Copy).then_inc(hi_done, 1)

        def out(p, half):
            act.wait_ge(av_done, 4 * p + 2 * half + 2)
            dst = o_out[:, p] if isinstance(p, int) else o_out[:, bass.ds(p, 1)].rearrange("q o n -> q (o n)")
            act.activation(dst[:, half * HALF:half * HALF + HALF], ps_o[half][:], ACT.Copy).then_inc(o_done, 1)

        with act.Fori(0, PAIRS) as p:
            act.wait_ge(ld_qk, 128 * p + 128)
            act.activation(q_both[:], q_raw[:], ACT.Copy).then_inc(q_hi_done, 1)
            act.activation(k_hi[:], k_raw[:], ACT.Copy).then_inc(q_hi_done, 1)
            for n in range(VG):
                act.wait_ge(t_done, GROUPS * p + n + 1)
                if n == 0:
                    act.wait_ge(setup, 3)
                for h in range(2):
                    cols = slice(h * 64, h * 64 + 64)
                    ins = act.activation(v_hi[:, 4 * n:4 * n + 4, h, cols], ps_t[n % 2][:, :, cols], ACT.Copy)
                ins.then_inc(hi_done, 1)
            sigmoids(p, 0)
            sigmoids(p, 1)
            for u in range(UNITS):
                high(p, u)
                if u + 2 < UNITS:
                    sigmoids(p, u + 2)
                if u == 10:
                    out(p, 0)
            out(p, 1)

    @block.gpsimd
    def _(pool):
        pool.memset(as_f32(v_hi[:]), 0.0).then_inc(setup, 1)
        pool.memset(as_f32(v_lo[:]), 0.0).then_inc(setup, 1)
        pool.memset(stick_left[:, :, S:S + 1], 1.0).then_inc(setup, 1)
        pool.wait_ge(setup, 3)
        with pool.Fori(0, PAIRS) as p:
            for u in range(UNITS):
                s, o = u % 2, start(u)
                pool.wait_ge(beta_done, UNITS * p + u + 1)
                pool.wait_ge(scan_done, UNITS * p + u + 1)
                if u >= 2:
                    pool.wait_ge(t_done, GROUPS * p + first_group[u - 1])
                pool.tensor_tensor(weight[:, s, o:S], beta[:, s, o:S], stick_left[:, s, o + 1:S + 1], ALU.mult)\
                    .then_inc(w_done, 1)
            pool.wait_ge(t_done, GROUPS * p + GROUPS)

    @block.vector
    def _(dve):
        def scan(p, u):
            s, o = u % 2, start(u)
            dve.wait_ge(rest_done, UNITS * p + u + 1)
            if u >= 2:
                dve.wait_ge(w_done, UNITS * p + u - 1)
            factor = rest[:, s, o:S][:, ::-1]
            dve.tensor_tensor_scan(stick_left[:, s, o:S][:, ::-1], factor, factor, 1.0, ALU.mult, ALU.bypass)\
               .then_inc(scan_done, 1)

        def low(p, u):
            h, t0 = u // 4 % 2, u % 4 * P
            for j0 in range(0, tile_of[u] + 1, 4):
                n = first_group[u] + j0 // 4
                w = min(4, tile_of[u] + 1 - j0)
                dve.wait_ge(hi_done, GROUPS * p + n + 1)
                dve.tensor_tensor(a_lo[:, h, j0:j0 + w, t0:t0 + P], ps_t[n % 2][:, 0:w],
                                  as_f32(a_hi[:, h, j0:j0 + w, t0:t0 + P]), ALU.subtract).then_inc(lo_done, 1)

        dve.tensor_copy(ident_b[:], ident).then_inc(q_done, 1)
        dve.tensor_copy(mask_b[:], g.const[:, C_NEG:C_NEG + P]).then_inc(q_done, 1)
        dve.wait_ge(setup, 3)
        with dve.Fori(0, PAIRS) as p:
            dve.wait_ge(q_hi_done, 2 * p + 1)
            dve.tensor_tensor(q_both[64:P], q_raw[64:P], as_f32(q_both[64:P]), ALU.subtract).then_inc(prep_done, 1)
            dve.wait_ge(q_hi_done, 2 * p + 2)
            dve.tensor_tensor(k_lo[:], k_raw[:], as_f32(k_hi[:]), ALU.subtract).then_inc(prep_done, 1)
            for n in range(VG):
                dve.wait_ge(hi_done, GROUPS * p + n + 1)
                for h in range(2):
                    cols = slice(h * 64, h * 64 + 64)
                    ins = dve.tensor_tensor(v_lo[:, 4 * n:4 * n + 4, h, cols], ps_t[n % 2][:, :, cols],
                                            as_f32(v_hi[:, 4 * n:4 * n + 4, h, cols]), ALU.subtract)
                ins.then_inc(lo_done, 1)
            dve.wait_ge(lo_done, GROUPS * p + VG)
            dve.sem_inc(prep_done, 1)
            scan(p, 0)
            scan(p, 1)
            for u in range(UNITS):
                low(p, u)
                if u + 2 < UNITS:
                    scan(p, u + 2)
            dve.wait_ge(av_done, 4 * p + 4)

    @block.tensor
    def _(pe):
        def logits(p, u):
            s, h, i = u % 2, u // 4 % 2, tile_of[u]
            if u >= 2:
                pe.wait_ge(beta_done, UNITS * p + u - 1)
            w = (i + 1) * P
            q_t = q_both[:, h, i * P:i * P + P]
            for c0 in range(0, w, HALF):
                c1 = min(w, c0 + HALF)
                pe.matmul(ps_z[s][:, c0:c1], q_t, k_hi[:, h, c0:c1], start=True, stop=False)
                mm = pe.matmul(ps_z[s][:, c0:c1], q_t, k_lo[:, h, c0:c1], start=False, stop=c1 < w)
            mm = pe.matmul(ps_z[s][:, w - P:w], ident_b[:], mask_b[:], start=False, stop=True)
            mm.then_inc(z_done, 1)

        def transposes(p, u):
            s, o = u % 2, start(u)
            pe.wait_ge(w_done, UNITS * p + u + 1)
            for j0 in range(0, tile_of[u] + 1, 4):
                n = first_group[u] + j0 // 4
                pe.wait_ge(lo_done, GROUPS * p + n - 1)
                for j in range(j0, min(tile_of[u] + 1, j0 + 4)):
                    mm = pe.transpose(ps_t[n % 2][:, j - j0], weight[:, s, o + j * P:o + j * P + P], ident)
                mm.then_inc(t_done, 1)

        def values(p, a):
            half, h = a // 2, a % 2
            pe.wait_ge(lo_done, GROUPS * p + first_group[4 * a + 4])
            if a == 2:
                pe.wait_ge(o_done, 2 * p + 1)
            last = 4 * half + 3
            for j in range(last + 1):
                t0 = max(0, j - 4 * half) * P
                for i, (w, x) in enumerate(three(v_hi[:, j, h], v_lo[:, j, h], a_hi[:, h, j, t0:HALF],
                                                 a_lo[:, h, j, t0:HALF])):
                    mm = pe.matmul(ps_o[half][:, t0:HALF], w, x, start=h == 0 and j == 0 and i == 0,
                                   stop=h == 1 and j == last and i == 2)
            mm.then_inc(av_done, 1)

        with pe.Fori(0, PAIRS) as p:
            pe.wait_ge(ld_v, 16 * p + 16)
            for n in range(VG):
                for j in range(4):
                    mm = pe.transpose(ps_t[n % 2][:, j], v_raw[:, (4 * n + j) * P:(4 * n + j) * P + P], ident)
                mm.then_inc(t_done, 1)
            pe.wait_ge(q_done, 2)
            pe.wait_ge(prep_done, 3 * p + 2)
            logits(p, 0)
            logits(p, 1)
            for u in range(UNITS):
                transposes(p, u)
                if u + 2 < UNITS:
                    logits(p, u + 2)
                if u % 4 == 0 and u:
                    values(p, u // 4 - 1)
            values(p, 3)
            pe.wait_ge(o_done, 2 * p + 1)

    ph.close()


CHUNK = 64
TILES = S // P
DK, DV = 64, 128
SOLVES = HEADS * S // CHUNK


def delta_decay(nc, g, d, dn):
    ph = Scope(nc, "dec")
    row = lambda name: ph.sb(name, [HEADS, S])
    a, b, reset = row("a"), row("b"), row("reset")
    mag, e, u, lnu, resid, rec, gl, gcum = (row(n) for n in ("mag", "e", "u", "lnu", "resid", "rec", "gl", "gcum"))
    beta = row("beta")
    neg_a = ph.sb("neg_a", [HEADS, 1])
    tok = ph.sb("tok", [P, 3, TILES * HEADS])
    eg_tok = ph.sb("eg_tok", [P, TILES * HEADS])
    ps_tok = ph.ps("tok", [P, 3, TILES * HEADS])
    ps_sum = ph.ps("sum", [P, 3, TILES * HEADS])
    ld, a_step, v_step, tr_done, sum_done = (ph.sem(n) for n in ("ld", "a_step", "v_step", "tr_done", "sum_done"))
    block = ph.stack.enter_context(nc.Block())

    @block.sync
    def _(sp):
        ab = d["proj"][N_PROJ - 1]
        sp.dma_start(b[:], ab[0:HEADS]).then_inc(ld, 16)
        sp.dma_start(a[:], ab[HEADS:2 * HEADS]).then_inc(ld, 16)
        sp.dma_start(dn.beta_sys[:], ab[0:HEADS].rearrange("h (c i) -> (h c) i", i=CHUNK)).then_inc(ld, 16)
        sp.dma_start(reset[:], d["reset"]).then_inc(ld, 16)

    @block.scalar
    def _(act):
        act.wait_ge(ld, 64)
        act.activation(beta[:], b[:], ACT.Sigmoid).then_inc(a_step, 1)
        act.activation(dn.beta_sys[:], dn.beta_sys[:], ACT.Sigmoid).then_inc(a_step, 1)
        act.wait_ge(v_step, 1)
        act.activation(mag[:], a[:], ACT.Abs).then_inc(a_step, 1)
        act.wait_ge(a_step, 3)
        act.activation(e[:], mag[:], ACT.Exp, scale=-1.0).then_inc(a_step, 1)
        act.activation(neg_a[:], g.small["dn_head"][:, 0:1], ACT.Exp).then_inc(a_step, 1)
        act.wait_ge(v_step, 2)
        act.activation(lnu[:], u[:], ACT.Ln).then_inc(a_step, 1)
        act.wait_ge(v_step, 10)
        act.activation(dn.eg_row[:], gcum[:], ACT.Exp).then_inc(a_step, 1)
        act.wait_ge(v_step, 11)
        act.activation(eg_tok[:], tok[:, 2], ACT.Exp).then_inc(a_step, 1)
        act.wait_ge(sum_done, 1)
        act.activation(dn.rest_tok[:], ps_sum[:, 0], ACT.Exp).then_inc(a_step, 1)
        for par in range(2):
            rows = slice(par * DK, (par + 1) * DK)
            src = ps_sum[rows, 1:3].rearrange("p c (t h) -> p c t h", h=HEADS)[:, :, :, par::2]
            act.activation(dn.chunk_decay[rows], src, ACT.Exp).then_inc(a_step, 1)

    @block.vector
    def _(dve):
        n = [0]

        def then(ins):
            n[0] += 1
            ins.then_inc(v_step, 1)
            dve.wait_ge(v_step, n[0])

        dve.wait_ge(ld, 64)
        then(dve.tensor_scalar(a[:], a[:], g.small["dn_head"][:, 1:2], None, ALU.add))
        dve.wait_ge(a_step, 5)
        then(dve.tensor_scalar(u[:], e[:], 1.0, None, ALU.add))
        then(dve.tensor_scalar(resid[:], u[:], -1.0, None, ALU.add))
        then(dve.tensor_tensor(resid[:], e[:], resid[:], ALU.subtract))
        then(dve.reciprocal(rec[:], u[:]))
        then(dve.tensor_tensor(resid[:], resid[:], rec[:], ALU.mult))
        dve.wait_ge(a_step, 6)
        then(dve.tensor_tensor(resid[:], resid[:], lnu[:], ALU.add))
        then(dve.scalar_tensor_tensor(gl[:], a[:], 0.0, resid[:], ALU.max, ALU.add))
        then(dve.tensor_scalar(gl[:], gl[:], neg_a[:], -1.0, ALU.mult, ALU.mult))
        then(dve.tensor_tensor_scan(gcum[:], reset[:], gl[:], 0.0, ALU.mult, ALU.add))
        dve.wait_ge(tr_done, 1)
        then(dve.tensor_copy(tok[:], ps_tok[:]))
        dve.tensor_copy(dn.g_tok[:], tok[:, 0]).then_inc(v_step, 1)
        dve.tensor_copy(dn.beta_tok[:], tok[:, 1]).then_inc(v_step, 1)
        dve.wait_ge(a_step, 8)
        dve.tensor_tensor(dn.beta_eg_tok[:], tok[:, 1], eg_tok[:], ALU.mult).then_inc(v_step, 1)

    @block.tensor
    def _(pe):
        pe.wait_ge(a_step, 1)
        pe.wait_ge(v_step, 10)
        ident8 = g.const[0:HEADS, C_IDENT:C_IDENT + HEADS]
        for n, src in enumerate((gl, beta, gcum)):
            for t in range(TILES):
                mm = pe.transpose(ps_tok[:, n, t * HEADS:(t + 1) * HEADS], src[:, t * P:(t + 1) * P], ident8)
        mm.then_inc(tr_done, 1)
        pe.wait_ge(v_step, 11)
        for n, c in enumerate((C_STRICT, C_EVEN, C_ODD)):
            mm = pe.matmul(ps_sum[:, n], g.const[:, c:c + P], tok[:, 0], start=True, stop=True)
        mm.then_inc(sum_done, 1)

    ph.close()


def delta_prepare(nc, g, d, dn):
    ph = Scope(nc, "prep")
    XR = 4
    x = ph.sb("x", [P, XR, S])
    sq, norm, rn = ph.sb("sq", [P, 2, S]), ph.sb("norm", [P, S]), ph.sb("rn", [P, S])
    q_n, k_n = ph.sb("q_n", [P, 4, S]), ph.sb("k_n", [P, 4, S])
    gu, decay, system = ph.sb("gu", [P, HEADS, P]), ph.sb("decay", [P, HEADS, P]), ph.sb("system", [P, 2, HEADS, P])
    ps_a, ps_b, ps_c = (ph.ps(n, [P, S]) for n in ("a", "b", "c"))
    ld = ph.sems("ld", XR)
    st = ph.sems("st", 2)
    sq_done, ss_done, norm_done, rn_done, n_done = (ph.sem(n) for n in ("sq_done", "ss_done", "norm_done", "rn_done", "n_done"))
    bc_done, qg_done, kt_done, k_used = (ph.sem(n) for n in ("bc_done", "qg_done", "kt_done", "k_used"))
    vt_done, v_used = ph.sem("vt_done"), ph.sem("v_used")
    gu_done, diff_done, exp_done, mask_done, prod_done, tile_done = (
        ph.sem(n) for n in ("gu_done", "diff_done", "exp_done", "mask_done", "prod_done", "tile_done"))
    block = ph.stack.enter_context(nc.Block())
    ident = g.const[:, C_IDENT:C_IDENT + P]
    NQK = 8
    order = [SB_BLOCKS + n // 2 + 4 * (n % 2) for n in range(NQK)] + [SB_BLOCKS + 8 + h for h in range(HEADS)]

    def systems(t, c):
        return d["systems"].rearrange("(h t c) j i -> t c j h i", h=HEADS, c=2)[t, c]

    @block.sync
    def _(sp):
        for n, b in enumerate(order):
            if n >= XR:
                m = n - XR
                if m < NQK:
                    sp.wait_ge(n_done, m + 1)
                else:
                    sp.wait_ge(vt_done, m - NQK + 1)
            sp.dma_start(x[:, n % XR], d["proj"][b]).then_inc(ld[n % XR], 16)
        for t in range(TILES):
            sp.wait_ge(tile_done, 4 * t + 4)
            for c in range(2):
                rows = slice(c * CHUNK, (c + 1) * CHUNK)
                sp.dma_start(systems(t, c), system[rows, t % 2, :, rows]).then_inc(st[t % 2], 16)
        for s in range(2):
            sp.wait_ge(st[s], 32 * TILES // 2)

    @block.scalar
    def _(act):
        def square(n):
            act.wait_ge(ld[n % XR], 16 * (n // XR + 1))
            if n >= 2:
                act.wait_ge(ss_done, n - 1)
            act.activation(sq[:, n % 2], x[:, n % XR], ACT.Square).then_inc(sq_done, 1)

        square(0)
        for n in range(NQK):
            if n + 1 < NQK:
                square(n + 1)
            act.wait_ge(ss_done, n + 1)
            if n:
                act.wait_ge(rn_done, n)
            act.activation(norm[:], ps_a[:], ACT.Sqrt, bias=g.eps[:]).then_inc(norm_done, 1)
        for t in range(TILES):
            act.wait_ge(diff_done, t + 1)
            if t:
                act.wait_ge(tile_done, 4 * t)
            act.activation(decay[:].rearrange("p h i -> p (h i)"), ps_a[:], ACT.Exp).then_inc(exp_done, 1)

    @block.gpsimd
    def _(pool):
        incl = g.const[:, C_INCL:C_INCL + P]
        incl_h = incl.unsqueeze(1).to_broadcast([P, HEADS, P])
        for t in range(TILES):
            g_t = dn.g_tok[:, t * HEADS:(t + 1) * HEADS]
            if t:
                pool.wait_ge(diff_done, t)
            pool.tensor_tensor(gu[:], incl_h, g_t.unsqueeze(2).to_broadcast([P, HEADS, P]), ALU.mult)\
                .then_inc(gu_done, 1)
            pool.wait_ge(exp_done, t + 1)
            pool.tensor_tensor(decay[:], decay[:], incl_h, ALU.mult).then_inc(mask_done, 1)

    @block.vector
    def _(dve):
        for n in range(NQK):
            b = n // 2
            dve.wait_ge(norm_done, n + 1)
            if n:
                dve.wait_ge(n_done, n)
            dve.reciprocal(rn[:], norm[:]).then_inc(rn_done, 1)
            dve.wait_ge(rn_done, n + 1)
            if n % 2 == 0:
                dve.scalar_tensor_tensor(q_n[:, b], x[:, n % XR], DK ** -0.5, rn[:], ALU.mult, ALU.mult)\
                   .then_inc(n_done, 1)
                dve.wait_ge(n_done, n + 1)
                dve.wait_ge(bc_done, b + 1)
                dve.tensor_tensor(dn.q_decayed[:, b], q_n[:, b], ps_b[:], ALU.mult).then_inc(qg_done, 1)
            else:
                dve.tensor_tensor(k_n[:, b], x[:, n % XR], rn[:], ALU.mult).then_inc(n_done, 1)
                dve.wait_ge(kt_done, b + 1)
                k_tok = ps_c[:].rearrange("p (t h k) -> p t h k", t=TILES, h=2)
                for dst, by in ((dn.k_beta, dn.beta_eg_tok), (dn.k_rest, dn.rest_tok)):
                    by = by[:].rearrange("p (t h) -> p t h", h=HEADS)[:, :, 2 * b:2 * b + 2]
                    dve.tensor_tensor(dst[:, :, b * P:(b + 1) * P].rearrange("p t (h k) -> p t h k", h=2), k_tok,
                                      by.unsqueeze(3).to_broadcast([P, TILES, 2, DK]), ALU.mult).then_inc(k_used, 1)
        for h in range(HEADS):
            dve.wait_ge(vt_done, h + 1)
            by = dn.beta_tok[:].rearrange("p (t h) -> p t h", h=HEADS)[:, :, h:h + 1]
            v_tok = (ps_b, ps_c)[h % 2][:].rearrange("p (t v) -> p t v", t=TILES)
            dve.tensor_tensor(dn.value[:, :, h * DV:(h + 1) * DV], v_tok, by.to_broadcast([P, TILES, DV]), ALU.mult)\
               .then_inc(v_used, 1)
        for t in range(TILES):
            dve.wait_ge(mask_done, t + 1)
            dve.wait_ge(prod_done, t + 1)
            if t >= 2:
                dve.wait_ge(st[t % 2], 32 * (t // 2))
            for par in range(2):
                kk = ps_b[:, par * HALF:(par + 1) * HALF].rearrange("p (h i) -> p h i", h=4)
                qk = ps_c[:, par * HALF:(par + 1) * HALF].rearrange("p (h i) -> p h i", h=4)
                dve.tensor_tensor(system[:, t % 2, par::2], kk, decay[:, par::2], ALU.mult).then_inc(tile_done, 1)
                dve.tensor_tensor(dn.intra[:, t, par::2], qk, decay[:, par::2], ALU.mult).then_inc(tile_done, 1)

    @block.tensor
    def _(pe):
        ones64 = g.const[:, C_ONES64:C_ONES64 + P]
        for n in range(NQK):
            b = n // 2
            pe.wait_ge(sq_done, n + 1)
            if n:
                pe.wait_ge(norm_done, n)
            for t in range(2):
                cols = slice(t * HALF, (t + 1) * HALF)
                mm = pe.matmul(ps_a[:, cols], ones64, sq[:, n % 2, cols], start=True, stop=True)
            mm.then_inc(ss_done, 1)
            if n % 2 == 0:
                if b:
                    pe.wait_ge(qg_done, b)
                for t in range(2):
                    cols = slice(t * HALF, (t + 1) * HALF)
                    mm = pe.matmul(ps_b[:, cols], g.const[0:HEADS, C_SEL + b * P:C_SEL + (b + 1) * P],
                                   dn.eg_row[:, cols], start=True, stop=True)
                mm.then_inc(bc_done, 1)
            else:
                pe.wait_ge(n_done, n + 1)
                if b:
                    pe.wait_ge(k_used, 2 * b)
                for t in range(TILES):
                    mm = pe.transpose(ps_c[:, t * P:(t + 1) * P], k_n[:, b, t * P:(t + 1) * P], ident)
                mm.then_inc(kt_done, 1)
        for h in range(HEADS):
            n = NQK + h
            pe.wait_ge(ld[n % XR], 16 * (n // XR + 1))
            pe.wait_ge(*((v_used, h - 1) if h >= 2 else ((qg_done, 4), (k_used, 8))[h]))
            for t in range(TILES):
                mm = pe.transpose((ps_b, ps_c)[h % 2][:, t * P:(t + 1) * P], x[:, n % XR, t * P:(t + 1) * P], ident)
            mm.then_inc(vt_done, 1)
        for t in range(TILES):
            pe.wait_ge(gu_done, t + 1)
            pe.wait_ge(*((exp_done, t) if t else (norm_done, NQK)))
            for i in range(2):
                mm = pe.matmul(ps_a[:, i * HALF:(i + 1) * HALF], g.const[:, C_STRICT:C_STRICT + P],
                               gu[:, 4 * i:4 * i + 4], start=True, stop=True)
            mm.then_inc(diff_done, 1)
            pe.wait_ge(*((tile_done, 4 * t) if t else (v_used, HEADS)))
            tok = slice(t * P, (t + 1) * P)
            for b in range(4):
                for par in range(2):
                    rows = slice(par * DK, (par + 1) * DK)
                    col = par * HALF + b * P
                    pe.matmul(ps_b[:, col:col + P], k_n[rows, b, tok], k_n[rows, b, tok], start=True, stop=True)
            for b in range(4):
                for par in range(2):
                    rows = slice(par * DK, (par + 1) * DK)
                    col = par * HALF + b * P
                    mm = pe.matmul(ps_c[:, col:col + P], k_n[rows, b, tok], q_n[rows, b, tok], start=True, stop=True)
            mm.then_inc(prod_done, 1)

    ph.close()


def delta_solve(nc, g, d, dn):
    ph = Scope(nc, "solve")
    lt = ph.sb("lt", [P, CHUNK, CHUNK])
    r = ph.sb("r", [P, CHUNK, CHUNK])
    part = ph.sb("part", [P, CHUNK * CHUNK // 4])
    ld, st, step = ph.sem("ld"), ph.sem("st"), ph.sem("step")
    block = ph.stack.enter_context(nc.Block())
    steps = 3 + 2 * (CHUNK - 1)

    @block.sync
    def _(sp):
        sp.dma_start(lt[:], d["systems"]).then_inc(ld, 16)
        sp.wait_ge(step, steps)
        sp.dma_start(d["solved"], r[:]).then_inc(st, 16)
        sp.wait_ge(st, 16)

    @block.vector
    def _(dve):
        n = [0]

        def then(ins):
            n[0] += 1
            ins.then_inc(step, 1)
            dve.wait_ge(step, n[0])

        then(dve.memset(r[:], 0.0))
        then(dve.memset(r[:].rearrange("p c i -> p (c i)")[:, 0:CHUNK * CHUNK:CHUNK + 1], 1.0))
        dve.wait_ge(ld, 16)
        then(dve.tensor_tensor(lt[:], lt[:], dn.beta_sys[:].unsqueeze(1).to_broadcast([P, CHUNK, CHUNK]), ALU.mult))
        for j in range(CHUNK - 1):
            c, i = j + 1, CHUNK - 1 - j
            out = part[:, 0:c * i].rearrange("p (c i) -> p c i", c=c)
            then(dve.tensor_tensor(out, r[:, 0:c, j:j + 1].to_broadcast([P, c, i]),
                                   lt[:, j:j + 1, j + 1:CHUNK].to_broadcast([P, c, i]), ALU.mult))
            then(dve.tensor_tensor(r[:, 0:c, j + 1:CHUNK], r[:, 0:c, j + 1:CHUNK], out, ALU.subtract))

    ph.close()


def delta_scan(nc, g, d, dn):
    ph = Scope(nc, "scan")
    inv = ph.sb("inv", [P, 2, HEADS, P])
    w_t = ph.sb("w_t", [P, 2, 4, P])
    u = dn.value
    state = ph.sb("state", [P, 4, 2 * DV])
    kept = ph.sb("kept", [P, 4, 2 * DV])
    v_new = ph.sb("v_new", [P, 2, HEADS * DV])
    o, o_sq = ph.sb("o", [P, 2, HEADS * DV]), ph.sb("o_sq", [P, HEADS * DV])
    ss, std, rstd = ph.sb("ss", [P, HEADS]), ph.sb("std", [P, HEADS]), ph.sb("rstd", [P, HEADS])
    z = ph.sb("z", [P, 2, HEADS, P])
    o_t = ph.sb("o_t", [P, 2, HEADS, P])
    ps_ws, ps_o, ps_kv, ps_m = (ph.ps(n, [P, S]) for n in ("ws", "o", "kv", "m"))
    ld_i, ld_z, st = ph.sems("ld_i", 2), ph.sems("ld_z", 2), ph.sems("st", 2)
    zeroed, m_filled, m_free = ph.sem("zeroed"), ph.sem("m_filled"), ph.sem("m_free")
    ws_done, vn_done, kept_done, kv_done, s_done = (ph.sem(n) for n in ("ws_done", "vn_done", "kept_done", "kv_done", "s_done"))
    o_done, o_copied, sum_done, std_done, rstd_done, on_done = (
        ph.sem(n) for n in ("o_done", "o_copied", "sum_done", "std_done", "rstd_done", "on_done"))
    block = ph.stack.enter_context(nc.Block())
    ident = g.const[:, C_IDENT:C_IDENT + P]
    uses = [("u", 0), ("w", 0)]
    for t in range(TILES):
        uses += [("u", t + 1), ("w", t + 1)] if t + 1 < TILES else []
        uses += [("o", t - 1)] if t else []
    uses += [("o", TILES - 1)]
    use = {key: n for n, key in enumerate(uses)}
    even, odd = slice(0, DK), slice(DK, P)

    @block.sync
    def _(sp):
        def load_inv(t):
            if t >= 2:
                sp.wait_ge(m_filled, use["w", t - 2] + 1)
            for c in range(2):
                rows = slice(c * CHUNK, (c + 1) * CHUNK)
                src = d["solved"].rearrange("(h t c) j i -> t c j h i", h=HEADS, c=2)[t, c]
                sp.dma_start(inv[rows, t % 2, :, rows], src).then_inc(ld_i[t % 2], 16)

        sp.wait_ge(zeroed, 3)
        load_inv(0)
        load_inv(1)
        for t in range(TILES):
            s = t % 2
            if t >= 2:
                sp.wait_ge(m_free, use["o", t - 2] + 1)
                sp.dma_start(d["o_b"].rearrange("h v n -> v h n")[:, :, (t - 2) * P:(t - 1) * P], o_t[:, s])\
                  .then_inc(st[s], 16)
            src = d["proj"][CONV_END:Z_END].rearrange("h v n -> v h n")[:, :, t * P:(t + 1) * P]
            sp.dma_start(z[:, s], src).then_inc(ld_z[s], 16)
            if t + 2 < TILES:
                load_inv(t + 2)
        for t in range(TILES - 2, TILES):
            sp.wait_ge(m_free, use["o", t] + 1)
            sp.dma_start(d["o_b"].rearrange("h v n -> v h n")[:, :, t * P:(t + 1) * P], o_t[:, t % 2])\
              .then_inc(st[t % 2], 16)
        for s in range(2):
            sp.wait_ge(st[s], 16 * TILES // 2)

    @block.scalar
    def _(act):
        def take_uw(t):
            act.wait_ge(m_filled, use["u", t] + 1)
            act.activation(u[:, t], ps_m[:], ACT.Copy).then_inc(m_free, 1)
            act.wait_ge(m_filled, use["w", t] + 1)
            act.activation(w_t[:, t % 2], ps_m[:, 0:HALF].rearrange("p (b n) -> p b n", b=4), ACT.Copy)\
               .then_inc(m_free, 1)

        def root(t):
            act.wait_ge(sum_done, t + 1)
            act.activation(std[:], ss[:], ACT.Sqrt, scale=1.0 / DV, bias=g.eps[:]).then_inc(std_done, 1)

        take_uw(0)
        for t in range(TILES):
            if t + 1 < TILES:
                take_uw(t + 1)
            if t:
                root(t - 1)
            act.wait_ge(o_done, t + 1)
            if t >= 2:
                act.wait_ge(on_done, t - 1)
            act.activation(o[:, t % 2], ps_o[:], ACT.Copy).then_inc(o_copied, 1)
            act.activation(o_sq[:], ps_o[:], ACT.Square).then_inc(o_copied, 1)
        root(TILES - 1)

    @block.gpsimd
    def _(pool):
        pool.memset(inv[:, 0], 0.0).then_inc(zeroed, 1)
        pool.memset(inv[:, 1], 0.0).then_inc(zeroed, 1)
        pool.memset(state[:], 0.0).then_inc(zeroed, 1)
        pool.wait_ge(zeroed, 3)

        def normalise(t):
            pool.wait_ge(rstd_done, t + 1)
            o_h = o[:, t % 2].rearrange("p (h v) -> p h v", h=HEADS)
            pool.tensor_tensor(o_h, o_h, rstd[:].unsqueeze(2).to_broadcast([P, HEADS, DV]), ALU.mult)\
                .then_inc(on_done, 1)

        for n in range(2 * TILES):
            t, c = n // 2, n % 2
            if n:
                pool.wait_ge(s_done, 2 * n)
            pool.tensor_tensor(kept[:], state[:], dn.chunk_decay[:, c, t].unsqueeze(2).to_broadcast([P, 4, 2 * DV]),
                               ALU.mult).then_inc(kept_done, 1)
            if c and t:
                normalise(t - 1)
        normalise(TILES - 1)

    @block.vector
    def _(dve):
        def sums(t):
            dve.wait_ge(o_copied, 2 * t + 2)
            dve.tensor_reduce(ss[:], o_sq[:].rearrange("p (h v) -> p h v", h=HEADS), AX.X, ALU.add)\
               .then_inc(sum_done, 1)
            dve.wait_ge(std_done, t + 1)
            if t:
                dve.wait_ge(on_done, t)
            dve.reciprocal(rstd[:], std[:]).then_inc(rstd_done, 1)

        def gate(t):
            s = t % 2
            dve.wait_ge(m_filled, use["o", t] + 1)
            dve.wait_ge(ld_z[s], 16 * (t // 2 + 1))
            if t >= 2:
                dve.wait_ge(st[s], 16 * (t // 2))
            dve.scalar_tensor_tensor(o_t[:, s], ps_m[:].rearrange("p (h n) -> p h n", h=HEADS),
                                     g.small["dn_norm"][:], z[:, s], ALU.mult, ALU.mult).then_inc(m_free, 1)

        dve.wait_ge(zeroed, 3)
        for n in range(2 * TILES):
            t, c = n // 2, n % 2
            rows = slice(c * CHUNK, (c + 1) * CHUNK)
            dve.wait_ge(ws_done, n + 1)
            if t >= 2:
                dve.wait_ge(o_done, t - 1)
            dve.tensor_tensor(v_new[rows, t % 2], u[rows, t], ps_ws[rows], ALU.subtract).then_inc(vn_done, 1)
            dve.wait_ge(kv_done, n + 1)
            dve.wait_ge(kept_done, n + 1)
            for par, rows in ((0, even), (1, odd)):
                dve.tensor_tensor(state[rows, :, par * DV:(par + 1) * DV], kept[rows, :, par * DV:(par + 1) * DV],
                                  ps_kv[rows].rearrange("p (b x) -> p b x", b=4)[:, :, par * DV:(par + 1) * DV],
                                  ALU.add).then_inc(s_done, 1)
            if t:
                (gate if c else sums)(t - 1)
        sums(TILES - 1)
        gate(TILES - 1)

    @block.tensor
    def _(pe):
        def fill(kind, t):
            n = use[kind, t]
            if n:
                pe.wait_ge(m_free, n)
            if kind == "u":
                pe.wait_ge(ld_i[t % 2], 32 * (t // 2 + 1))
                for h in range(HEADS):
                    mm = pe.matmul(ps_m[:, h * DV:(h + 1) * DV], inv[:, t % 2, h], u[:, t, h * DV:(h + 1) * DV],
                                   start=True, stop=True)
            elif kind == "w":
                for h in range(HEADS):
                    rows = odd if h % 2 else even
                    mm = pe.matmul(ps_m[rows, h // 2 * P:(h // 2 + 1) * P], dn.k_beta[:, t, h * DK:(h + 1) * DK],
                                   inv[:, t % 2, h], start=True, stop=True)
            else:
                pe.wait_ge(on_done, t + 1)
                for h in range(HEADS):
                    mm = pe.transpose(ps_m[:, h * P:(h + 1) * P], o[:, t % 2, h * DV:(h + 1) * DV], ident)
            mm.then_inc(m_filled, 1)

        pe.wait_ge(zeroed, 3)
        fill("u", 0)
        fill("w", 0)
        for n in range(2 * TILES):
            t, c = n // 2, n % 2
            rows = slice(c * CHUNK, (c + 1) * CHUNK)
            pe.wait_ge(m_free, use["w", t] + 1)
            if n:
                pe.wait_ge(s_done, 2 * n)
            for b in range(4):
                mm = pe.matmul(ps_ws[rows, b * 256:(b + 1) * 256], w_t[:, t % 2, b, rows], state[:, b],
                               start=True, stop=True)
            mm.then_inc(ws_done, 1)
            if t:
                pe.wait_ge(o_copied, 2 * t)
            tok = slice(t * P + c * CHUNK, t * P + (c + 1) * CHUNK)
            for b in range(4):
                pe.matmul(ps_o[rows, b * 256:(b + 1) * 256], dn.q_decayed[:, b, tok], state[:, b],
                          start=b % 2 == 0, stop=False, skip_group_check=True)
            if c == 0 and t + 1 < TILES:
                fill("u", t + 1)
                fill("w", t + 1)
            if c == 1 and t:
                fill("o", t - 1)
            pe.wait_ge(vn_done, n + 1)
            for b in range(4):
                mm = pe.matmul(ps_kv[:, b * 256:(b + 1) * 256], dn.k_rest[rows, t, b * P:(b + 1) * P],
                               v_new[rows, t % 2, b * 256:(b + 1) * 256], start=True, stop=True)
            mm.then_inc(kv_done, 1)
            if c == 1:
                for h in range(HEADS):
                    cols = slice(h * DV, (h + 1) * DV)
                    mm = pe.matmul(ps_o[:, cols], dn.intra[:, t, h], v_new[:, t % 2, cols],
                                   start=False, stop=True, skip_group_check=True)
                mm.then_inc(o_done, 1)
        fill("o", TILES - 1)

    ph.close()


def delta(nc, g, d):
    dn = Scope(nc, "dn")
    TH = TILES * HEADS
    dn.beta_sys = dn.sb("beta_sys", [P, CHUNK])
    dn.eg_row = dn.sb("eg_row", [HEADS, S])
    dn.g_tok, dn.beta_tok, dn.beta_eg_tok, dn.rest_tok = (
        dn.sb(n, [P, TH]) for n in ("g_tok", "beta_tok", "beta_eg_tok", "rest_tok"))
    dn.chunk_decay = dn.sb("chunk_decay", [P, 2, TILES, 4])
    delta_decay(nc, g, d, dn)
    dn.q_decayed = dn.sb("q_decayed", [P, 4, S])
    dn.k_beta, dn.k_rest = dn.sb("k_beta", [P, TILES, 4 * P]), dn.sb("k_rest", [P, TILES, 4 * P])
    dn.value = dn.sb("value", [P, TILES, HEADS * DV])
    dn.intra = dn.sb("intra", [P, TILES, HEADS, P])
    delta_prepare(nc, g, d, dn)
    delta_solve(nc, g, d, dn)
    delta_scan(nc, g, d, dn)
    dn.close()


def merge(nc, g, d):
    ph = Scope(nc, "merge")
    KA, KB = SB_BLOCKS // 3, KD
    K = KA + KB
    raw = ph.sb("raw", [P, 2, K * P])
    w_hi, w_lo = ph.sb("w_hi", [P, 2, K, P], F32R), ph.sb("w_lo", [P, 2, K, P], F32R)
    o_raw = ph.sb("o_raw", [P, 2, S])
    o_hi, o_lo = ph.sb("o_hi", [P, K, S], F32R), ph.sb("o_lo", [P, K, S], F32R)
    gates = ph.sb("gates", [P, 2, 2, S])
    ps = [[ph.ps(f"s{s}_{i}", [P, S]) for i in range(2)] for s in range(2)]
    ld, ld_g, ld_o = ph.sems("ld", 2), ph.sems("ld_g", 2), ph.sems("ld_o", 2)
    oh_done, ol_done, hi_done, lo_done, mm_done, part_done, out_done = (
        ph.sem(n) for n in ("oh_done", "ol_done", "hi_done", "lo_done", "mm_done", "part_done", "out_done"))
    block = ph.stack.enter_context(nc.Block())

    @block.sync
    def _(sp):
        def load_w(m):
            if m >= 2:
                sp.wait_ge(lo_done, m - 1)
            sp.dma_start(raw[:, m % 2], d["w_merge"][m]).then_inc(ld[m % 2], 16)

        def load_gates(m):
            if m >= 2:
                sp.wait_ge(out_done, m - 1)
            for i in range(2):
                sp.dma_start(gates[:, m % 2, i], d["proj"][Z_END + i * KD + m]).then_inc(ld_g[m % 2], 16)

        load_w(0)
        for k in range(K):
            if k >= 2:
                sp.wait_ge(ol_done, k - 1)
            src = d["o_a"][k] if k < KA else d["o_b"][k - KA]
            sp.dma_start(o_raw[:, k % 2], src).then_inc(ld_o[k % 2], 16)
        load_w(1)
        load_gates(0)
        load_gates(1)
        for m in range(2, KD):
            load_w(m)
            load_gates(m)

    @block.scalar
    def _(act):
        def split(m):
            act.wait_ge(ld[m % 2], 16 * (m // 2 + 1))
            if m >= 2:
                act.wait_ge(mm_done, m - 1)
            act.activation(w_hi[:, m % 2].rearrange("p k n -> p (k n)"), raw[:, m % 2], ACT.Copy).then_inc(hi_done, 1)

        split(0)
        for k in range(K):
            act.wait_ge(ld_o[k % 2], 16 * (k // 2 + 1))
            act.activation(o_hi[:, k], o_raw[:, k % 2], ACT.Copy).then_inc(oh_done, 1)
        for m in range(1, KD):
            split(m)

    @block.gpsimd
    def _(pool):
        def low(m):
            pool.wait_ge(hi_done, m + 1)
            pool.tensor_tensor(w_lo[:, m % 2].rearrange("p k n -> p (k n)"), raw[:, m % 2],
                               as_f32(w_hi[:, m % 2].rearrange("p k n -> p (k n)")), ALU.subtract).then_inc(lo_done, 1)

        low(0)
        for m in range(1, KD):
            low(m)
            pool.wait_ge(part_done, 2 * m)
            pool.tensor_tensor(g.merged[:, m - 1], gates[:, (m - 1) % 2, 0], gates[:, (m - 1) % 2, 1], ALU.add)\
                .then_inc(out_done, 1)
        pool.wait_ge(part_done, 2 * KD)
        pool.tensor_tensor(g.merged[:, KD - 1], gates[:, (KD - 1) % 2, 0], gates[:, (KD - 1) % 2, 1], ALU.add)\
            .then_inc(out_done, 1)

    @block.vector
    def _(dve):
        for k in range(K):
            dve.wait_ge(oh_done, k + 1)
            dve.tensor_tensor(o_lo[:, k], o_raw[:, k % 2], as_f32(o_hi[:, k]), ALU.subtract).then_inc(ol_done, 1)
        for m in range(KD):
            dve.wait_ge(mm_done, m + 1)
            dve.wait_ge(ld_g[m % 2], 32 * (m // 2 + 1))
            for i in range(2):
                gate = gates[:, m % 2, i]
                dve.tensor_tensor(gate, ps[m % 2][i][:], gate, ALU.mult).then_inc(part_done, 1)

    @block.tensor
    def _(pe):
        for m in range(KD):
            s = m % 2
            pe.wait_ge(lo_done, m + 1)
            if m >= 2:
                pe.wait_ge(part_done, 2 * (m - 1))
            for k in range(K):
                if m == 0:
                    pe.wait_ge(ol_done, k + 1)
                branch, first, last = (0, 0, KA - 1) if k < KA else (1, KA, K - 1)
                for i, (w, x) in enumerate(three(w_hi[:, s, k], w_lo[:, s, k], o_hi[:, k], o_lo[:, k])):
                    for t in range(2):
                        cols = slice(t * HALF, (t + 1) * HALF)
                        mm = pe.matmul(ps[s][branch][:, cols], w, x[:, cols], start=k == first and i == 0,
                                       stop=k == last and i == 2)
            mm.then_inc(mm_done, 1)

    ph.close()


def output(nc, g, d):
    ph = Scope(nc, "out")
    raw = ph.sb("raw", [P, 2, KD * P])
    w_hi, w_lo = ph.sb("w_hi", [P, 2, KD, P], F32R), ph.sb("w_lo", [P, 2, KD, P], F32R)
    hi, lo = g.h_hi, g.h_lo
    x2 = ph.sb("x2", [P, KD, S])
    sq, total = ph.sb("sq", [P, S]), ph.sb("total", [P, S])
    hf = ph.sb("hf", [P, 2, S])
    ps = [ph.ps(f"s{s}", [P, S]) for s in range(2)]
    ps_ss = ph.ps("ss", [P, S])
    ld, ld_x, st = ph.sems("ld", 2), ph.sems("ld_x", KD), ph.sem("st")
    mh_done, ml_done, hi_done, lo_done, mm_done, x2_done = (
        ph.sem(n) for n in ("mh_done", "ml_done", "hi_done", "lo_done", "mm_done", "x2_done"))
    sq_done, add_done, ss_done, std_done, rstd_done = (
        ph.sem(n) for n in ("sq_done", "add_done", "ss_done", "std_done", "rstd_done"))
    xn_done, h_done, hh_done, hl_done = (ph.sem(n) for n in ("xn_done", "h_done", "hh_done", "hl_done"))
    block = ph.stack.enter_context(nc.Block())

    @block.sync
    def _(sp):
        for m in range(KD):
            if m >= 2:
                sp.wait_ge(lo_done, m - 1)
            sp.dma_start(raw[:, m % 2], d["w_out"][m]).then_inc(ld[m % 2], 16)
            sp.dma_start(x2[:, m], d["xT"][m]).then_inc(ld_x[m], 16)
        for m in range(KD):
            sp.wait_ge(x2_done, m + 1)
            sp.dma_start(d["x2"][m], x2[:, m]).then_inc(st, 16)
        sp.wait_ge(st, 16 * KD)

    @block.scalar
    def _(act):
        def split(m):
            act.wait_ge(ld[m % 2], 16 * (m // 2 + 1))
            if m >= 2:
                act.wait_ge(mm_done, m - 1)
            act.activation(w_hi[:, m % 2].rearrange("p k n -> p (k n)"), raw[:, m % 2], ACT.Copy).then_inc(hi_done, 1)

        split(0)
        for k in range(KD):
            act.activation(hi[:, k], g.merged[:, k], ACT.Copy).then_inc(mh_done, 1)
        for m in range(KD):
            if m + 1 < KD:
                split(m + 1)
            act.wait_ge(x2_done, m + 1)
            if m:
                act.wait_ge(add_done, m + 1)
            act.activation(sq[:], x2[:, m], ACT.Square).then_inc(sq_done, 1)
        act.wait_ge(ss_done, 1)
        act.activation(sq[:], ps_ss[:], ACT.Sqrt, scale=1.0 / D, bias=g.eps[:]).then_inc(std_done, 1)
        for k in range(KD):
            act.wait_ge(xn_done, k + 1)
            if k >= 2:
                act.wait_ge(hl_done, k - 1)
            act.activation(hf[:, k % 2], hf[:, k % 2], ACT.Identity, scale=g.mod[:, 4 * KD + k:4 * KD + k + 1],
                           bias=g.mod[:, 3 * KD + k:3 * KD + k + 1]).then_inc(h_done, 1)
            act.wait_ge(h_done, k + 1)
            act.activation(g.h_hi[:, k], hf[:, k % 2], ACT.Copy).then_inc(hh_done, 1)

    @block.gpsimd
    def _(pool):
        def low(m):
            pool.wait_ge(hi_done, m + 1)
            pool.tensor_tensor(w_lo[:, m % 2].rearrange("p k n -> p (k n)"), raw[:, m % 2],
                               as_f32(w_hi[:, m % 2].rearrange("p k n -> p (k n)")), ALU.subtract).then_inc(lo_done, 1)

        pool.memset(total[:], 0.0).then_inc(add_done, 1)
        low(0)
        for m in range(KD):
            if m + 1 < KD:
                low(m + 1)
            pool.wait_ge(sq_done, m + 1)
            pool.wait_ge(add_done, m + 1)
            pool.tensor_tensor(total[:], total[:], sq[:], ALU.add).then_inc(add_done, 1)
        pool.wait_ge(rstd_done, 1)
        for k in range(KD):
            if k >= 2:
                pool.wait_ge(hl_done, k - 1)
            pool.tensor_tensor(hf[:, k % 2], x2[:, k], total[:], ALU.mult).then_inc(xn_done, 1)

    @block.vector
    def _(dve):
        for k in range(KD):
            dve.wait_ge(mh_done, k + 1)
            dve.tensor_tensor(lo[:, k], g.merged[:, k], as_f32(hi[:, k]), ALU.subtract).then_inc(ml_done, 1)
        for m in range(KD):
            dve.wait_ge(mm_done, m + 1)
            dve.wait_ge(ld_x[m], 16)
            dve.scalar_tensor_tensor(x2[:, m], ps[m % 2][:], g.mod[:, 2 * KD + m:2 * KD + m + 1], x2[:, m],
                                     ALU.mult, ALU.add).then_inc(x2_done, 1)
        dve.wait_ge(std_done, 1)
        dve.reciprocal(total[:], sq[:]).then_inc(rstd_done, 1)
        for k in range(KD):
            dve.wait_ge(hh_done, k + 1)
            dve.tensor_tensor(g.h_lo[:, k], hf[:, k % 2], as_f32(g.h_hi[:, k]), ALU.subtract).then_inc(hl_done, 1)

    @block.tensor
    def _(pe):
        for m in range(KD):
            s = m % 2
            pe.wait_ge(lo_done, m + 1)
            if m >= 2:
                pe.wait_ge(x2_done, m - 1)
            for k in range(KD):
                if m == 0:
                    pe.wait_ge(ml_done, k + 1)
                for i, (w, x) in enumerate(three(w_hi[:, s, k], w_lo[:, s, k], hi[:, k], lo[:, k])):
                    for t in range(2):
                        cols = slice(t * HALF, (t + 1) * HALF)
                        mm = pe.matmul(ps[s][:, cols], w, x[:, cols], start=k == 0 and i == 0,
                                       stop=k == KD - 1 and i == 2)
            mm.then_inc(mm_done, 1)
        pe.wait_ge(add_done, KD + 1)
        for t in range(2):
            cols = slice(t * HALF, (t + 1) * HALF)
            mm = pe.matmul(ps_ss[:, cols], g.const[:, C_ONES:C_ONES + P], total[:, cols], start=True, stop=True)
        mm.then_inc(ss_done, 1)

    ph.close()


def ffn_up(nc, g, d):
    ph = Scope(nc, "up")
    raw = ph.sb("raw", [P, 2, BLK])
    w_hi, w_lo = ph.sb("w_hi", [P, 2, KD, P], F32R), ph.sb("w_lo", [P, 2, KD, P], F32R)
    taps = ph.sb("taps", [P, 2, W_EXTRA])
    u = ph.sb("u", [P, 2, S])
    ps = [ph.ps(f"s{s}", [P, S]) for s in range(2)]
    ld = ph.sems("ld", 2)
    hi_done, lo_done, mm_done, scaled, conv, gate_done, y_done = (
        ph.sem(n) for n in ("hi_done", "lo_done", "mm_done", "scaled", "conv", "gate_done", "y_done"))
    block = ph.stack.enter_context(nc.Block())

    @block.sync
    def _(sp):
        def load(n, s):
            src = d["w_up"][n] if isinstance(n, int) else d["w_up"][bass.ds(n, 1)].rearrange("o p n -> p (o n)")
            sp.dma_start(raw[:, s], src).then_inc(ld[s], 16)

        load(0, 0)
        load(1, 1)
        with sp.Fori(0, KF - 1) as j:
            for s in range(2):
                sp.wait_ge(lo_done, 2 * j + s + 1)
                load(2 * j + s + 2, s)

    @block.scalar
    def _(act):
        def split(j, s, first=False):
            act.wait_ge(ld[s], 16 * j + 16)
            if not first:
                act.wait_ge(mm_done, 2 * j + s - 1)
            act.activation(w_hi[:, s], raw[:, s, 0:KD * P].rearrange("p (k m) -> p k m", k=KD), ACT.Copy)\
               .then_inc(hi_done, 1)

        def scale(j, s, first=False):
            act.wait_ge(mm_done, 2 * j + s + 1)
            if not first:
                act.wait_ge(y_done, j)
            act.activation(u[:, s], ps[s][:], ACT.Identity, scale=taps[:, s, 2:3], bias=taps[:, s, 3:4])\
               .then_inc(scaled, 1)

        def silu(j):
            act.wait_ge(conv, 4 * j + 2)
            act.activation(u[:, 0], u[:, 0], ACT.Silu).then_inc(gate_done, 1)

        split(0, 0, True)
        split(0, 1, True)
        scale(0, 0, True)
        split(1, 0)
        silu(0)
        scale(0, 1, True)
        with act.Fori(1, KF - 1) as j:
            split(j, 1)
            scale(j, 0)
            split(j + 1, 0)
            silu(j)
            scale(j, 1)
        split(KF - 1, 1)
        scale(KF - 1, 0)
        silu(KF - 1)
        scale(KF - 1, 1)

    @block.gpsimd
    def _(pool):
        def low(j, s, first=False):
            pool.wait_ge(hi_done, 2 * j + s + 1)
            if not first:
                pool.wait_ge(conv, 4 * (j - 1) + 2 * s + 2)
            pool.tensor_tensor(w_lo[:, s], raw[:, s, 0:KD * P].rearrange("p (k m) -> p k m", k=KD),
                               as_f32(w_hi[:, s]), ALU.subtract)
            pool.tensor_copy(taps[:, s], raw[:, s, KD * P:BLK]).then_inc(lo_done, 1)

        low(0, 0, True)
        low(0, 1, True)
        with pool.Fori(1, KF) as j:
            low(j, 0)
            low(j, 1)

    @block.vector
    def _(dve):
        with dve.Fori(0, KF) as j:
            for s in range(2):
                dve.wait_ge(scaled, 2 * j + s + 1)
                for back in (1, 2):
                    if back == 2:
                        dve.wait_ge(conv, 4 * j + 2 * s + 1)
                    dve.scalar_tensor_tensor(u[:, s, back:S], ps[s][:, 0:S - back], taps[:, s, 2 - back:3 - back],
                                             u[:, s, back:S], ALU.mult, ALU.add).then_inc(conv, 1)
            dve.wait_ge(conv, 4 * j + 4)
            dve.wait_ge(gate_done, j + 1)
            dve.tensor_tensor(g.y[:, bass.ds(j, 1)], u[:, 0:1], u[:, 1:2], ALU.mult).then_inc(y_done, 1)

    @block.tensor
    def _(pe):
        def product(j, s, first=False):
            pe.wait_ge(lo_done, 2 * j + s + 1)
            if not first:
                pe.wait_ge(conv, 4 * (j - 1) + 2 * s + 2)
            for k in range(KD):
                for i, (w, x) in enumerate(three(w_hi[:, s, k], w_lo[:, s, k], g.h_hi[:, k], g.h_lo[:, k])):
                    for t in range(2):
                        cols = slice(t * HALF, (t + 1) * HALF)
                        mm = pe.matmul(ps[s][:, cols], w, x[:, cols], start=k == 0 and i == 0,
                                       stop=k == KD - 1 and i == 2)
            mm.then_inc(mm_done, 1)

        product(0, 0, True)
        product(0, 1, True)
        with pe.Fori(1, KF) as j:
            product(j, 0)
            product(j, 1)

    ph.close()


def ffn_down(nc, g, d):
    ph = Scope(nc, "down")
    MB = 4
    W = MB * P
    raw = ph.sb("raw", [P, 2, W])
    w_hi, w_lo = ph.sb("w_hi", [P, 2, W], F32R), ph.sb("w_lo", [P, 2, W], F32R)
    y_hi, y_lo = ph.sb("y_hi", [P, 2, S], F32R), ph.sb("y_lo", [P, 2, S], F32R)
    x3 = ph.sb("x3", [P, KD, S])
    sq, total, rstd = ph.sb("sq", [P, S]), ph.sb("total", [P, S]), ph.sb("rstd", [P, S])
    ps = [ph.ps(f"m{m}", [P, S]) for m in range(MB)]
    ld, ld_x, st = ph.sems("ld", 2), ph.sem("ld_x"), ph.sem("st")
    wh_done, wl_done, yh_done, yl_done, mm_done, last_done, x3_done = (
        ph.sem(n) for n in ("wh_done", "wl_done", "yh_done", "yl_done", "mm_done", "last_done", "x3_done"))
    sq_done, add_done, ss_done, std_done, rstd_done, out_done = (
        ph.sem(n) for n in ("sq_done", "add_done", "ss_done", "std_done", "rstd_done", "out_done"))
    block = ph.stack.enter_context(nc.Block())
    STEPS = 2 * KF

    @block.sync
    def _(sp):
        w = d["w_down"].rearrange("g k p n -> (g k) p n")

        def load(n, s):
            src = w[n] if isinstance(n, int) else w[bass.ds(n, 1)].rearrange("o p n -> p (o n)")
            sp.dma_start(raw[:, s], src).then_inc(ld[s], 16)

        load(0, 0)
        load(1, 1)
        sp.dma_start(x3[:], d["x2"].rearrange("m p n -> p m n")).then_inc(ld_x, 16)
        with sp.Fori(0, KF - 1) as j:
            for s in range(2):
                sp.wait_ge(wl_done, 2 * j + s + 1)
                load(2 * j + s + 2, s)
        for m in range(KD):
            sp.wait_ge(out_done, m + 1)
            sp.dma_start(d["out"][m], x3[:, m]).then_inc(st, 16)
        sp.wait_ge(st, 16 * KD)

    @block.scalar
    def _(act):
        def split(n, s, y_n, read=None):
            act.wait_ge(ld[s], 8 * (n - s) + 16)
            if read:
                act.wait_ge(*read)
            act.activation(w_hi[:, s], raw[:, s], ACT.Copy).then_inc(wh_done, 1)
            act.activation(y_hi[:, s:s + 1], g.y[:, bass.ds(y_n, 1)], ACT.Copy).then_inc(yh_done, 1)

        def square(m):
            act.wait_ge(x3_done, m + 1)
            if m:
                act.wait_ge(add_done, m + 1)
            act.activation(sq[:], x3[:, m], ACT.Square).then_inc(sq_done, 1)

        split(0, 0, 0)
        split(1, 1, 1)
        with act.Fori(1, KF // 2) as j:
            for s in range(2):
                split(2 * j + s, s, 2 * j + s, (mm_done, 2 * j + s - 1))
        split(KF, 0, 0, (mm_done, KF - 1))
        split(KF + 1, 1, 1, (last_done, MB))
        with act.Fori(KF // 2 + 1, KF) as j:
            for s in range(2):
                split(2 * j + s, s, 2 * j + s - KF, (mm_done, 2 * j + s - 2))
        for m in range(KD):
            square(m)
        act.wait_ge(ss_done, 1)
        act.activation(sq[:], ps[0][:], ACT.Sqrt, scale=1.0 / D, bias=g.eps[:]).then_inc(std_done, 1)

    @block.gpsimd
    def _(pool):
        pool.memset(total[:], 0.0).then_inc(add_done, 1)
        with pool.Fori(0, KF) as j:
            for s in range(2):
                pool.wait_ge(wh_done, 2 * j + s + 1)
                pool.tensor_tensor(w_lo[:, s], raw[:, s], as_f32(w_hi[:, s]), ALU.subtract).then_inc(wl_done, 1)
        for m in range(KD):
            pool.wait_ge(sq_done, m + 1)
            pool.wait_ge(add_done, m + 1)
            pool.tensor_tensor(total[:], total[:], sq[:], ALU.add).then_inc(add_done, 1)

    @block.vector
    def _(dve):
        def low(n, s, y_n):
            dve.wait_ge(yh_done, n + 1)
            dve.tensor_tensor(y_lo[:, s:s + 1], g.y[:, bass.ds(y_n, 1)], as_f32(y_hi[:, s:s + 1]), ALU.subtract)\
               .then_inc(yl_done, 1)

        def residual(grp):
            for m in range(MB):
                n = grp * MB + m
                dve.wait_ge(last_done, n + 1)
                if n == 0:
                    dve.wait_ge(ld_x, 16)
                dve.scalar_tensor_tensor(x3[:, n], ps[m][:], g.mod[:, 5 * KD + n:5 * KD + n + 1], x3[:, n],
                                         ALU.mult, ALU.add).then_inc(x3_done, 1)

        with dve.Fori(0, KF // 2) as j:
            for s in range(2):
                low(2 * j + s, s, 2 * j + s)
        low(KF, 0, 0)
        residual(0)
        low(KF + 1, 1, 1)
        with dve.Fori(KF // 2 + 1, KF) as j:
            for s in range(2):
                low(2 * j + s, s, 2 * j + s - KF)
        residual(1)
        dve.wait_ge(std_done, 1)
        dve.reciprocal(rstd[:], sq[:]).then_inc(rstd_done, 1)
        dve.wait_ge(rstd_done, 1)
        for m in range(KD):
            dve.scalar_tensor_tensor(x3[:, m], x3[:, m], g.small["norms"][:, 2 * KD + m:2 * KD + m + 1], rstd[:],
                                     ALU.mult, ALU.mult).then_inc(out_done, 1)

    @block.tensor
    def _(pe):
        def step(n, s, grp, first=False, last=False):
            pe.wait_ge(wl_done, n + 1)
            pe.wait_ge(yl_done, n + 1)
            for m in range(MB):
                if first and grp:
                    pe.wait_ge(x3_done, m + 1)
                cut = slice(m * P, (m + 1) * P)
                for i, (w, x) in enumerate(three(w_hi[:, s, cut], w_lo[:, s, cut], y_hi[:, s], y_lo[:, s])):
                    for t in range(2):
                        cols = slice(t * HALF, (t + 1) * HALF)
                        mm = pe.matmul(ps[m][:, cols], w, x[:, cols], start=first and i == 0, stop=last and i == 2)
                if last:
                    mm.then_inc(last_done, 1)
                elif m == MB - 1:
                    mm.then_inc(mm_done, 1)

        for grp in range(2):
            n0 = grp * KF
            step(n0, 0, grp, first=True)
            step(n0 + 1, 1, grp)
            with pe.Fori(grp * KF // 2 + 1, (grp + 1) * KF // 2 - 1) as j:
                for s in range(2):
                    step(2 * j + s, s, grp)
            step(n0 + KF - 2, 0, grp)
            step(n0 + KF - 1, 1, grp, last=True)
        pe.wait_ge(add_done, KD + 1)
        for t in range(2):
            cols = slice(t * HALF, (t + 1) * HALF)
            mm = pe.matmul(ps[0][:, cols], g.const[:, C_ONES:C_ONES + P], total[:, cols], start=True, stop=True)
        mm.then_inc(ss_done, 1)

    ph.close()

SCRATCH = {"proj": (N_PROJ, P, S), "systems": (SOLVES, CHUNK, CHUNK), "solved": (SOLVES, CHUNK, CHUNK),
           "o_a": (HEADS // 2, P, S), "o_b": (HEADS, P, S), "x2": (KD, P, S), "out": (KD, P, S)}
OUT = ("out",)


def finish(r):
    return r["out"].reshape(D, S).T.reshape(1, S, D)


class Shared:
    pass


def build(nc, d):
    with ExitStack() as stack:
        sb = lambda name, shape, dt=F32: stack.enter_context(nc.sbuf_tensor(name, shape, dt))
        g = Shared()
        g.const = sb("const", [P, C_RESET])
        g.eps = sb("eps", [P, 1])
        g.c_act = sb("c_act", [P, KD])
        g.mod = sb("mod", [P, 6 * KD])
        g.small = {"b_ada": sb("b_ada", [P, 6 * KD]), "norms": sb("norms", [P, 3 * KD]),
                   "dn_norm": sb("dn_norm", [P, 1]), "dn_head": sb("dn_head", [HEADS, 2])}
        def hidden(scope, n):
            g.h_hi = scope.sb(f"{n}_hi", [P, KD, S], F32R)
            g.h_lo = scope.sb(f"{n}_lo", [P, KD, S], F32R)

        scope = Scope(nc, "h1")
        hidden(scope, "h1")
        condition(nc, g, d)
        project(nc, g, d)
        scope.close()
        delta(nc, g, d)
        stick(nc, g, d)
        merged = Scope(nc, "merged")
        g.merged = merged.sb("merged", [P, KD, S])
        merge(nc, g, d)
        h2 = Scope(nc, "h2", side="right")
        hidden(h2, "h2")
        output(nc, g, d)
        merged.close()
        mlp = Scope(nc, "mlp")
        g.y = mlp.sb("y", [P, KF, S])
        ffn_up(nc, g, d)
        h2.close()
        ffn_down(nc, g, d)
        mlp.close()


def constants():
    import numpy as np

    t = np.zeros((P, C_END), np.float32)
    i, j = np.arange(P)[:, None], np.arange(P)[None]
    chunk = i // 64 == j // 64
    t[:, C_IDENT:C_IDENT + P] = i == j
    t[:, C_ONES:C_ONES + P] = 1
    t[:, C_ONES64:C_ONES64 + P] = chunk
    t[:, C_INCL:C_INCL + P] = chunk & (j >= i)
    t[:, C_STRICT:C_STRICT + P] = chunk & (i > j)
    for h in range(HEADS):
        t[h, C_SEL + h // 2 * P + h % 2 * 64:C_SEL + h // 2 * P + h % 2 * 64 + 64] = 1
    t[:, C_NEG:C_NEG + P] = np.where(j >= i, NEG, 0)
    t[:64, C_EVEN:C_EVEN + P] = 1
    t[64:, C_ODD:C_ODD + P] = 1
    t[:, C_RESET:C_RESET + S] = (np.arange(S) % 64 != 0)[None]
    return t


def kernel(x, c, w_ada, b_ada, norm1_w, w_in, dn_conv_w, dn_A_log, dn_dt_bias, dn_norm_w,
           w_proj_sb, w_proj_dn, w_out, norm2_w, w_ffn_in, ffn_conv_w, ffn_conv_b, w_ffn_out,
           final_norm_w):
    import numpy as np
    import concourse.bacc as bacc
    from concourse.bass_utils import run_bass_kernel_spmd

    def column(v):
        return np.asarray(v).reshape(-1, P).T

    def blocks(w, cols, extra=None, pad=0):
        out = []
        for b, c0 in enumerate(cols):
            part = w[:, c0:c0 + P].reshape(-1, P, P).transpose(1, 0, 2).reshape(P, -1)
            tail = np.zeros((P, pad), np.float32) if extra is None or extra[b] is None else extra[b]
            out.append(np.concatenate([part, tail], 1))
        return np.stack(out)

    ab = SB_BLOCKS * P + 24 * P
    cols = [b * P for b in range(36)] + [ab + 16 + b * P for b in range(16)] + [ab]
    conv = np.asarray(dn_conv_w)[0].T.reshape(16, P, W_EXTRA)
    taps = [None] * SB_BLOCKS + list(conv) + [None] * (N_PROJ - SB_BLOCKS - 16)
    ffn_cols, ffn_taps = [], []
    fcw = np.asarray(ffn_conv_w)[0].T.reshape(2 * KF, P, 3)
    fcb = np.asarray(ffn_conv_b)[0].reshape(2 * KF, P, 1)
    for b in range(KF):
        for half in range(2):
            ffn_cols.append((half * KF + b) * P)
            ffn_taps.append(np.concatenate([fcw[half * KF + b], fcb[half * KF + b]], 1))
    m_cols = [b * P for b in range(KD)]
    ins = {
        "xT": np.asarray(x)[0].T.reshape(KD, P, S),
        "c": column(c[0]),
        "w_ada": np.asarray(w_ada)[0].reshape(2, 4, P, 6, D).transpose(3, 0, 2, 1, 4),
        "b_ada": column(b_ada[0]),
        "norms": np.concatenate([column(norm1_w[0]), column(norm2_w[0]), column(final_norm_w)], 1),
        "w_in": blocks(np.asarray(w_in)[0], cols, taps, W_EXTRA),
        "dn_norm": np.asarray(dn_norm_w)[0].reshape(P, 1),
        "dn_head": np.stack([np.asarray(dn_A_log)[0], np.asarray(dn_dt_bias)[0]], 1),
        "w_merge": np.concatenate([blocks(np.asarray(w_proj_sb)[0], m_cols),
                                   blocks(np.asarray(w_proj_dn)[0], m_cols)], 2),
        "w_out": blocks(np.asarray(w_out)[0], m_cols),
        "w_up": blocks(np.asarray(w_ffn_in)[0], ffn_cols, ffn_taps, W_EXTRA),
        "w_down": np.asarray(w_ffn_out)[0].reshape(KF, P, 2, 4 * P).transpose(2, 0, 1, 3),
        "const": constants(),
    }
    ins = {k + "_dram": np.ascontiguousarray(v) for k, v in ins.items()}
    nc = bacc.Bacc("TRN2", target_bir_lowering=False, num_devices=1)
    d = {k[:-5]: nc.dram_tensor(k, v.shape, F32, kind="ExternalInput").ap() for k, v in ins.items()}
    d["reset"] = d["const"][0:HEADS, C_RESET:C_END]
    d["const"] = d["const"][:, 0:C_RESET]
    for name, shape in SCRATCH.items():
        d[name] = nc.dram_tensor(name + "_dram", shape, F32, kind="ExternalOutput" if name in OUT else "Internal").ap()
    build(nc, d)
    r = run_bass_kernel_spmd(nc, [ins], core_ids=[0])
    return finish({name: r.results[0][name + "_dram"] for name in OUT})
```

```python
import concourse.bass as bass
from concourse import mybir
from contextlib import ExitStack

F32 = mybir.dt.float32
F32R = mybir.dt.float32r
BF16 = mybir.dt.bfloat16
ALU = mybir.AluOpType
ACT = mybir.ActivationFunctionType
AX = mybir.AxisListType

P = 128
D = 1024
S = 1024
KD = D // P
HALF = 512
EPS = 1e-6
HEADS = 8
N_PROJ = 53
B_DN, B_Z, B_SB, B_GATE = 1, 17, 25, 37
W_EXTRA = 4
BLK = KD * P + W_EXTRA
D_FF = 2816
KF = D_FF // P
NEG = -1e30

C_IDENT, C_ONES, C_ONES64, C_INCL, C_STRICT, C_SEL = 0, 128, 256, 384, 512, 640
C_NEG = 640 + 512
C_EVEN, C_ODD = C_NEG + 128, C_NEG + 256
C_RESET = C_NEG + 384
C_END = C_RESET + 1024


def three(hi_w, lo_w, hi_x, lo_x):
    return ((hi_w, hi_x), (hi_w, lo_x), (lo_w, hi_x))


def as_f32(ap):
    return ap.bitcast(F32)


class Scope:

    def __init__(self, nc, name, side="left"):
        self.nc, self.name, self.side, self.stack = nc, name, side, ExitStack()
        self.signals = []

    def sb(self, name, shape, dt=F32):
        return self.stack.enter_context(self.nc.sbuf_tensor(f"{self.name}_{name}", shape, dt, side=self.side))

    def ps(self, name, shape, dt=F32):
        return self.stack.enter_context(self.nc.psum_tensor(f"{self.name}_ps_{name}", shape, dt))

    def sem(self, name):
        signal = self.stack.enter_context(self.nc.semaphore(f"{self.name}_{name}"))
        self.signals.append(signal)
        return signal

    def sems(self, name, n):
        return [self.sem(f"{name}{i}") for i in range(n)]

    def close(self):
        self.stack.close()
        for signal in self.signals:
            self.nc.sync.sem_clear(signal)


def project_a(nc, g, d):
    ph = Scope(nc, "pa")
    PIECE = 4
    xT = ph.sb("xT", [P, KD, S])
    wa, acc = ph.sb("wa", [P, 2, PIECE, D]), ph.sb("acc", [P, 2, D])
    sq, std, rstd = ph.sb("sq", [P, 2, S]), ph.sb("std", [P, S]), ph.sb("rstd", [P, S])
    hf = ph.sb("hf", [P, 2, S])
    c_in = ph.sb("c_in", [P, KD])
    raw = ph.sb("raw", [P, 2, BLK])
    w_hi = ph.sb("w_hi", [P, 2, KD, P], F32R)
    w_lo = ph.sb("w_lo", [P, 2, KD, P], F32R)
    taps = ph.sb("taps", [P, 2, W_EXTRA])
    stage = ph.sb("stage", [P, 2, S])
    ps = [ph.ps(f"s{i}", [P, S]) for i in range(2)]
    ps_ss, ps_mod = ph.ps("ss", [P, S]), ph.ps("mod", [P, 3 * KD])
    ld_small, ld_c, ld_x, ld_a = ph.sem("ld_small"), ph.sem("ld_c"), ph.sems("ld_x", KD), ph.sems("ld_a", 2)
    ld, st = ph.sems("ld", 2), ph.sems("st", 2)
    c_done, acc_free, acc_done, eps_set = (ph.sem(n) for n in ("c_done", "acc_free", "acc_done", "eps_set"))
    sq_done, ss_done, std_done, rstd_done = (ph.sem(n) for n in ("sq_done", "ss_done", "std_done", "rstd_done"))
    mod_done, step, xn_done = (ph.sem(n) for n in ("mod_done", "step", "xn_done"))
    act_h, dve_h, hh_done, hl_done = (ph.sem(n) for n in ("act_h", "dve_h", "hh_done", "hl_done"))
    hi_done, lo_done, mm_done, out_done = (ph.sem(n) for n in ("hi_done", "lo_done", "mm_done", "out_done"))
    scaled, conv = ph.sem("scaled"), ph.sem("conv")
    block = ph.stack.enter_context(nc.Block())
    N = B_Z
    PEEL = 9

    def at(tensor, n):
        return tensor[n] if isinstance(n, int) else tensor[bass.ds(n, 1)].rearrange("o p n -> p (o n)")


    @block.sync
    def _(sp):
        def load_piece(n):
            if n >= 2:
                sp.wait_ge(acc_free, n - 1)
            sp.dma_start(wa[:, n % 2], d["w_ada"][n // 2, n % 2]).then_inc(ld_a[n % 2], 16)

        def block_io(j, s, load=True):
            n = 2 * j + s
            if load:
                sp.wait_ge(lo_done, n + 1)
                sp.dma_start(raw[:, s], at(d["w_in"], n + 2)).then_inc(ld[s], 16)
            sp.wait_ge(out_done, n + 1)
            sp.dma_start(at(d["proj"], n), stage[:, s]).then_inc(st[s], 16)

        sp.dma_start(c_in[:], d["c"]).then_inc(ld_c, 16)
        sp.dma_start(g.const[:], d["const"]).then_inc(ld_small, 16)
        for name in ("b_ada", "norms", "dn_norm", "dn_head"):
            sp.dma_start(g.small[name][:], d[name]).then_inc(ld_small, 16)
        for k in range(KD):
            sp.dma_start(xT[:, k, :], d["xT"][k]).then_inc(ld_x[k], 16)
        load_piece(0)
        load_piece(1)
        for s in range(2):
            sp.dma_start(raw[:, s], d["w_in"][s]).then_inc(ld[s], 16)
        load_piece(2)
        load_piece(3)
        for n in range(PEEL + 1):
            block_io(n // 2, n % 2)
            if n in (0, 4):
                load_piece(4 + n // 4)
        with sp.Fori((PEEL + 1) // 2, N // 2 - 1) as j:
            for s in range(2):
                block_io(j, s)
        block_io(N // 2 - 1, 0)
        block_io(N // 2 - 1, 1, load=False)
        block_io(N // 2, 0, load=False)
        sp.wait_ge(st[0], 16 * (N // 2 + 1))
        sp.wait_ge(st[1], 16 * (N // 2))

    @block.scalar
    def _(act):
        def split(j, s):
            n = 2 * j + s
            act.wait_ge(ld[s], 16 * (j + 1))
            if not (isinstance(n, int) and n < 2):
                act.wait_ge(mm_done, n - 1)
            act.activation(w_hi[:, s], raw[:, s, 0:KD * P].rearrange("p (k m) -> p k m", k=KD), ACT.Copy)\
               .then_inc(hi_done, 1)

        def evacuate(j, s):
            n = 2 * j + s
            act.wait_ge(mm_done, n + 1)
            if not (isinstance(n, int) and n < 2):
                act.wait_ge(st[s], 16 * j)
            act.activation(stage[:, s], ps[s][:], ACT.Copy, scale=taps[:, s, 3:4]).then_inc(scaled, 1)
            act.wait_ge(conv, 3 * n)
            act.activation(stage[:, s], stage[:, s], ACT.Silu).then_inc(out_done, 1)

        act.wait_ge(ld_c, 16)
        act.activation(g.c_act[:], c_in[:], ACT.Silu).then_inc(c_done, 1)
        for k in range(KD):
            act.wait_ge(ld_x[k], 16)
            if k >= 2:
                act.wait_ge(ss_done, k - 1)
            act.activation(sq[:, k % 2], xT[:, k], ACT.Square).then_inc(sq_done, 1)
        act.wait_ge(ss_done, KD)
        act.wait_ge(eps_set, 1)
        act.activation(std[:], ps_ss[:], ACT.Sqrt, scale=1.0 / D, bias=g.eps[:]).then_inc(std_done, 1)
        split(0, 0)
        split(0, 1)
        act.wait_ge(step, 2)
        for k in range(KD):
            if k % 2 == 0:
                act.wait_ge(xn_done, k + 1)
                if k >= 2:
                    act.wait_ge(hl_done, k - 1)
                act.activation(hf[:, 0], xT[:, k], ACT.Identity, scale=g.mod[:, KD + k:KD + k + 1],
                               bias=g.mod[:, k:k + 1]).then_inc(act_h, 1)
            act.wait_ge((act_h, dve_h)[k % 2], k // 2 + 1)
            act.activation(g.h_hi[:, k], hf[:, k % 2], ACT.Copy).then_inc(hh_done, 1)
        act.wait_ge(mm_done, 1)
        act.activation(stage[:, 0], ps[0][:], ACT.Copy).then_inc(out_done, 1)
        split(1, 0)
        evacuate(0, 1)
        with act.Fori(1, N // 2) as j:
            split(j, 1)
            evacuate(j, 0)
            split(j + 1, 0)
            evacuate(j, 1)
        evacuate(N // 2, 0)

    @block.gpsimd
    def _(pool):
        def low(j, s):
            n = 2 * j + s
            pool.wait_ge(hi_done, n + 1)
            if not (isinstance(n, int) and n < 2):
                pool.wait_ge(out_done, n - 1)
            pool.tensor_tensor(w_lo[:, s], raw[:, s, 0:KD * P].rearrange("p (k m) -> p k m", k=KD),
                               as_f32(w_hi[:, s]), ALU.subtract)
            pool.tensor_copy(taps[:, s], raw[:, s, KD * P:BLK]).then_inc(lo_done, 1)

        pool.memset(g.eps[:], EPS).then_inc(eps_set, 1)
        pool.wait_ge(rstd_done, 1)
        for k in range(KD):
            pool.tensor_tensor(xT[:, k], xT[:, k], rstd[:], ALU.mult).then_inc(xn_done, 1)
        low(0, 0)
        low(0, 1)
        with pool.Fori(1, N // 2) as j:
            for s in range(2):
                low(j, s)
        low(N // 2, 0)

    @block.vector
    def _(dve):
        def condition(grp, k):
            n = 2 * grp + k // PIECE
            dst, c_k = acc[:, grp % 2], g.c_act[:, k:k + 1]
            if k % PIECE == 0:
                dve.wait_ge(ld_a[n % 2], 16 * (n // 2 + 1))
            if k == 0:
                if grp == 2:
                    dve.wait_ge(mod_done, 1)
                ins = dve.tensor_scalar(dst, wa[:, 0, 0], c_k, None, ALU.mult)
            else:
                dve.wait_ge(acc_done, grp * KD + k)
                ins = dve.scalar_tensor_tensor(dst, wa[:, n % 2, k % PIECE], c_k, dst, ALU.mult, ALU.add)
            ins.then_inc(acc_done, 1)
            if k % PIECE == PIECE - 1:
                dve.wait_ge(acc_done, PIECE * n + PIECE)
                dve.sem_inc(acc_free, 1)

        def convolve(n, s):
            dve.wait_ge(scaled, n)
            for back in (1, 2, 3):
                if back > 1:
                    dve.wait_ge(conv, 3 * (n - 1) + back - 1)
                dve.scalar_tensor_tensor(stage[:, s, back:S], ps[s][:, 0:S - back], taps[:, s, 3 - back:4 - back],
                                         stage[:, s, back:S], ALU.mult, ALU.add).then_inc(conv, 1)

        dve.wait_ge(c_done, 1)
        for k in range(PIECE):
            condition(0, k)
        dve.wait_ge(std_done, 1)
        dve.reciprocal(rstd[:], std[:]).then_inc(rstd_done, 1)
        for k in range(PIECE, KD):
            condition(0, k)
        for k in range(KD):
            condition(1, k)
        dve.wait_ge(ld_small, 16 * 5)
        dve.wait_ge(mod_done, 2)
        dve.tensor_tensor(g.mod[:, 0:2 * KD], ps_mod[:, 0:2 * KD], g.small["b_ada"][:, 0:2 * KD], ALU.add)\
           .then_inc(step, 1)
        dve.wait_ge(step, 1)
        dve.scalar_tensor_tensor(g.mod[:, KD:2 * KD], g.mod[:, KD:2 * KD], 1.0, g.small["norms"][:, 0:KD],
                                 ALU.add, ALU.mult).then_inc(step, 1)
        dve.wait_ge(step, 2)
        for k in range(KD):
            if k % 2 == 0:
                dve.wait_ge(xn_done, k + 2)
                if k >= 2:
                    dve.wait_ge(hl_done, k)
                dve.tensor_scalar(hf[:, 1], xT[:, k + 1], g.mod[:, KD + k + 1:KD + k + 2], g.mod[:, k + 1:k + 2],
                                  ALU.mult, ALU.add).then_inc(dve_h, 1)
            dve.wait_ge(hh_done, k + 1)
            dve.tensor_tensor(g.h_lo[:, k], hf[:, k % 2], as_f32(g.h_hi[:, k]), ALU.subtract).then_inc(hl_done, 1)
        for n in range(1, PEEL):
            convolve(n, n % 2)
            condition(2, n - 1)
        with dve.Fori(PEEL // 2, N // 2) as j:
            for s in (1, 2):
                convolve(2 * j + s, s % 2)
        dve.wait_ge(mod_done, 3)
        dve.tensor_tensor(g.mod[:, 2 * KD:3 * KD], ps_mod[:, 2 * KD:3 * KD], g.small["b_ada"][:, 2 * KD:3 * KD], ALU.add)\
           .then_inc(step, 1)

    @block.tensor
    def _(pe):
        ones = g.const[:, C_ONES:C_ONES + P]

        def product(n, s, first=False):
            pe.wait_ge(lo_done, n + 1)
            if not first:
                pe.wait_ge(out_done, n - 1)
            for k in range(KD):
                if isinstance(n, int) and n == 0:
                    pe.wait_ge(hl_done, k + 1)
                hi, lo = w_hi[:, s, k], w_lo[:, s, k]
                for i, (w, x) in enumerate(three(hi, lo, g.h_hi[:, k], g.h_lo[:, k])):
                    for t in range(2):
                        mm = pe.matmul(ps[s][:, t * HALF:(t + 1) * HALF], w, x[:, t * HALF:(t + 1) * HALF],
                                       start=k == 0 and i == 0, stop=k == KD - 1 and i == 2)
            mm.then_inc(mm_done, 1)

        def columns(grp):
            pe.wait_ge(acc_done, KD * (grp + 1))
            for m in range(KD):
                mm = pe.matmul(ps_mod[:, grp * KD + m:grp * KD + m + 1], acc[:, grp % 2, m * P:(m + 1) * P],
                               ones[:, 0:1], start=True, stop=True)
            mm.then_inc(mod_done, 1)

        pe.wait_ge(ld_small, 16 * 5)
        for k in range(KD):
            pe.wait_ge(sq_done, k + 1)
            for t in range(2):
                mm = pe.matmul(ps_ss[:, t * HALF:(t + 1) * HALF], ones, sq[:, k % 2, t * HALF:(t + 1) * HALF],
                               start=k == 0, stop=k == KD - 1)
            mm.then_inc(ss_done, 1)
        columns(0)
        columns(1)
        for n in range(PEEL):
            product(n, n % 2, first=n < 2)
        product(PEEL, PEEL % 2)
        product(PEEL + 1, (PEEL + 1) % 2)
        columns(2)
        with pe.Fori(PEEL // 2 + 1, N // 2) as j:
            for s in (1, 2):
                product(2 * j + s, s % 2)

    ph.close()


def stick(nc, g, d):
    ph = Scope(nc, "stick")
    PAIRS, TILES, UNITS = HEADS // 2, S // P, 16
    q_raw, k_raw = ph.sb("q_raw", [P, 2, S]), ph.sb("k_raw", [P, 2, S])
    v_raw = ph.sb("v_raw", [P, S])
    q_both = ph.sb("q_both", [P, 2, S], F32R)
    k_hi, k_lo = ph.sb("k_hi", [P, 2, S], F32R), ph.sb("k_lo", [P, 2, S], F32R)
    v_hi, v_lo = (ph.sb(n, [P, TILES, 2, P], F32R) for n in ("v_hi", "v_lo"))
    a_hi, a_lo = (ph.sb(n, [P, 2, TILES, HALF], F32R) for n in ("a_hi", "a_lo"))
    beta, rest, weight = (ph.sb(n, [P, 2, S]) for n in ("beta", "rest", "weight"))
    stick_left = ph.sb("stick_left", [P, 2, S + 1])
    o_out = ph.sb("o_out", [P, PAIRS, S])
    ident_b, mask_b = ph.sb("ident_b", [P, P], BF16), ph.sb("mask_b", [P, P], BF16)
    ps_z = [ph.ps(f"z{i}", [P, S]) for i in range(2)]
    ps_t = [ph.ps(f"t{i}", [P, 4, P]) for i in range(2)]
    ps_o = [ph.ps(f"o{i}", [P, HALF]) for i in range(2)]
    ld_qk, ld_v, st = ph.sem("ld_qk"), ph.sem("ld_v"), ph.sem("st")
    setup, q_hi_done, prep_done, q_done = (ph.sem(n) for n in ("setup", "q_hi_done", "prep_done", "q_done"))
    z_done, rest_done, beta_done, scan_done, w_done = (ph.sem(n) for n in ("z_done", "rest_done", "beta_done", "scan_done", "w_done"))
    t_done, hi_done, lo_done, av_done, o_done = (ph.sem(n) for n in ("t_done", "hi_done", "lo_done", "av_done", "o_done"))
    block = ph.stack.enter_context(nc.Block())
    SCALE = 64 ** -0.5
    ident = g.const[:, C_IDENT:C_IDENT + P]

    tile_of = [4 * (u // 8) + u % 4 for u in range(UNITS)]
    groups = [(u, j0) for u in range(UNITS) for j0 in range(0, tile_of[u] + 1, 4)]
    VG = 2
    first_group = [VG + groups.index((u, 0)) for u in range(UNITS)] + [VG + len(groups)]
    GROUPS = VG + len(groups)

    def start(u):
        return S - (tile_of[u] + 1) * P

    @block.sync
    def _(sp):
        def pair_rows(n):
            return d["proj"][n] if isinstance(n, int) else d["proj"][bass.ds(n, 1)].rearrange("o p n -> p (o n)")

        def load(p):
            for raw, b in ((q_raw, B_SB + p), (k_raw, B_SB + PAIRS + p)):
                rows = pair_rows(b)
                for h in range(2):
                    for copy in range(2):
                        sp.dma_start(raw[copy * 64:copy * 64 + 64, h], rows[h * 64:h * 64 + 64]).then_inc(ld_qk, 16)
            sp.dma_start(v_raw[:], pair_rows(B_SB + 2 * PAIRS + p)).then_inc(ld_v, 16)

        def store(p):
            for half in range(2):
                sp.wait_ge(o_done, 2 * p + half + 1)
                cols = slice(half * HALF, half * HALF + HALF)
                sp.dma_start(d["o_a"][p][:, cols], o_out[:, p, cols]).then_inc(st, 16)

        load(0)
        for p in range(PAIRS):
            if p + 1 < PAIRS:
                sp.wait_ge(prep_done, 3 * p + 3)
                sp.wait_ge(t_done, GROUPS * p + VG)
                load(p + 1)
            store(p)
        sp.wait_ge(st, 32 * PAIRS)

    @block.scalar
    def _(act):
        def sigmoids(p, u):
            s, o = u % 2, start(u)
            act.wait_ge(z_done, UNITS * p + u + 1)
            if u >= 2:
                act.wait_ge(w_done, UNITS * p + u - 1)
            z = ps_z[s][:, 0:S - o]
            act.activation(rest[:, s, o:S], z, ACT.Sigmoid, scale=-SCALE).then_inc(rest_done, 1)
            act.activation(beta[:, s, o:S], z, ACT.Sigmoid, scale=SCALE).then_inc(beta_done, 1)

        def high(p, u):
            h, t0 = u // 4 % 2, u % 4 * P
            if u // 8 == 1 and u % 4 == 0:
                act.wait_ge(av_done, 4 * p + h + 1)
            for j0 in range(0, tile_of[u] + 1, 4):
                n = first_group[u] + j0 // 4
                w = min(4, tile_of[u] + 1 - j0)
                act.wait_ge(t_done, GROUPS * p + n + 1)
                act.activation(a_hi[:, h, j0:j0 + w, t0:t0 + P], ps_t[n % 2][:, 0:w], ACT.Copy).then_inc(hi_done, 1)

        def out(p, half):
            act.wait_ge(av_done, 4 * p + 2 * half + 2)
            dst = o_out[:, p] if isinstance(p, int) else o_out[:, bass.ds(p, 1)].rearrange("q o n -> q (o n)")
            act.activation(dst[:, half * HALF:half * HALF + HALF], ps_o[half][:], ACT.Copy).then_inc(o_done, 1)

        with act.Fori(0, PAIRS) as p:
            act.wait_ge(ld_qk, 128 * p + 128)
            act.activation(q_both[:], q_raw[:], ACT.Copy).then_inc(q_hi_done, 1)
            act.activation(k_hi[:], k_raw[:], ACT.Copy).then_inc(q_hi_done, 1)
            for n in range(VG):
                act.wait_ge(t_done, GROUPS * p + n + 1)
                if n == 0:
                    act.wait_ge(setup, 3)
                for h in range(2):
                    cols = slice(h * 64, h * 64 + 64)
                    ins = act.activation(v_hi[:, 4 * n:4 * n + 4, h, cols], ps_t[n % 2][:, :, cols], ACT.Copy)
                ins.then_inc(hi_done, 1)
            sigmoids(p, 0)
            sigmoids(p, 1)
            for u in range(UNITS):
                high(p, u)
                if u + 2 < UNITS:
                    sigmoids(p, u + 2)
                if u == 10:
                    out(p, 0)
            out(p, 1)

    @block.gpsimd
    def _(pool):
        pool.memset(as_f32(v_hi[:]), 0.0).then_inc(setup, 1)
        pool.memset(as_f32(v_lo[:]), 0.0).then_inc(setup, 1)
        pool.memset(stick_left[:, :, S:S + 1], 1.0).then_inc(setup, 1)
        pool.wait_ge(setup, 3)
        with pool.Fori(0, PAIRS) as p:
            for u in range(UNITS):
                s, o = u % 2, start(u)
                pool.wait_ge(beta_done, UNITS * p + u + 1)
                pool.wait_ge(scan_done, UNITS * p + u + 1)
                if u >= 2:
                    pool.wait_ge(t_done, GROUPS * p + first_group[u - 1])
                pool.tensor_tensor(weight[:, s, o:S], beta[:, s, o:S], stick_left[:, s, o + 1:S + 1], ALU.mult)\
                    .then_inc(w_done, 1)
            pool.wait_ge(t_done, GROUPS * p + GROUPS)

    @block.vector
    def _(dve):
        def scan(p, u):
            s, o = u % 2, start(u)
            dve.wait_ge(rest_done, UNITS * p + u + 1)
            if u >= 2:
                dve.wait_ge(w_done, UNITS * p + u - 1)
            factor = rest[:, s, o:S][:, ::-1]
            dve.tensor_tensor_scan(stick_left[:, s, o:S][:, ::-1], factor, factor, 1.0, ALU.mult, ALU.bypass)\
               .then_inc(scan_done, 1)

        def low(p, u):
            h, t0 = u // 4 % 2, u % 4 * P
            for j0 in range(0, tile_of[u] + 1, 4):
                n = first_group[u] + j0 // 4
                w = min(4, tile_of[u] + 1 - j0)
                dve.wait_ge(hi_done, GROUPS * p + n + 1)
                dve.tensor_tensor(a_lo[:, h, j0:j0 + w, t0:t0 + P], ps_t[n % 2][:, 0:w],
                                  as_f32(a_hi[:, h, j0:j0 + w, t0:t0 + P]), ALU.subtract).then_inc(lo_done, 1)

        dve.tensor_copy(ident_b[:], ident).then_inc(q_done, 1)
        dve.tensor_copy(mask_b[:], g.const[:, C_NEG:C_NEG + P]).then_inc(q_done, 1)
        dve.wait_ge(setup, 3)
        with dve.Fori(0, PAIRS) as p:
            dve.wait_ge(q_hi_done, 2 * p + 1)
            dve.tensor_tensor(q_both[64:P], q_raw[64:P], as_f32(q_both[64:P]), ALU.subtract).then_inc(prep_done, 1)
            dve.wait_ge(q_hi_done, 2 * p + 2)
            dve.tensor_tensor(k_lo[:], k_raw[:], as_f32(k_hi[:]), ALU.subtract).then_inc(prep_done, 1)
            for n in range(VG):
                dve.wait_ge(hi_done, GROUPS * p + n + 1)
                for h in range(2):
                    cols = slice(h * 64, h * 64 + 64)
                    ins = dve.tensor_tensor(v_lo[:, 4 * n:4 * n + 4, h, cols], ps_t[n % 2][:, :, cols],
                                            as_f32(v_hi[:, 4 * n:4 * n + 4, h, cols]), ALU.subtract)
                ins.then_inc(lo_done, 1)
            dve.wait_ge(lo_done, GROUPS * p + VG)
            dve.sem_inc(prep_done, 1)
            scan(p, 0)
            scan(p, 1)
            for u in range(UNITS):
                low(p, u)
                if u + 2 < UNITS:
                    scan(p, u + 2)
            dve.wait_ge(av_done, 4 * p + 4)

    @block.tensor
    def _(pe):
        def logits(p, u):
            s, h, i = u % 2, u // 4 % 2, tile_of[u]
            if u >= 2:
                pe.wait_ge(beta_done, UNITS * p + u - 1)
            w = (i + 1) * P
            q_t = q_both[:, h, i * P:i * P + P]
            for c0 in range(0, w, HALF):
                c1 = min(w, c0 + HALF)
                pe.matmul(ps_z[s][:, c0:c1], q_t, k_hi[:, h, c0:c1], start=True, stop=False)
                mm = pe.matmul(ps_z[s][:, c0:c1], q_t, k_lo[:, h, c0:c1], start=False, stop=c1 < w)
            mm = pe.matmul(ps_z[s][:, w - P:w], ident_b[:], mask_b[:], start=False, stop=True)
            mm.then_inc(z_done, 1)

        def transposes(p, u):
            s, o = u % 2, start(u)
            pe.wait_ge(w_done, UNITS * p + u + 1)
            for j0 in range(0, tile_of[u] + 1, 4):
                n = first_group[u] + j0 // 4
                pe.wait_ge(lo_done, GROUPS * p + n - 1)
                for j in range(j0, min(tile_of[u] + 1, j0 + 4)):
                    mm = pe.transpose(ps_t[n % 2][:, j - j0], weight[:, s, o + j * P:o + j * P + P], ident)
                mm.then_inc(t_done, 1)

        def values(p, a):
            half, h = a // 2, a % 2
            pe.wait_ge(lo_done, GROUPS * p + first_group[4 * a + 4])
            if a == 2:
                pe.wait_ge(o_done, 2 * p + 1)
            last = 4 * half + 3
            for j in range(last + 1):
                t0 = max(0, j - 4 * half) * P
                for i, (w, x) in enumerate(three(v_hi[:, j, h], v_lo[:, j, h], a_hi[:, h, j, t0:HALF],
                                                 a_lo[:, h, j, t0:HALF])):
                    mm = pe.matmul(ps_o[half][:, t0:HALF], w, x, start=h == 0 and j == 0 and i == 0,
                                   stop=h == 1 and j == last and i == 2)
            mm.then_inc(av_done, 1)

        with pe.Fori(0, PAIRS) as p:
            pe.wait_ge(ld_v, 16 * p + 16)
            for n in range(VG):
                for j in range(4):
                    mm = pe.transpose(ps_t[n % 2][:, j], v_raw[:, (4 * n + j) * P:(4 * n + j) * P + P], ident)
                mm.then_inc(t_done, 1)
            pe.wait_ge(q_done, 2)
            pe.wait_ge(prep_done, 3 * p + 2)
            logits(p, 0)
            logits(p, 1)
            for u in range(UNITS):
                transposes(p, u)
                if u + 2 < UNITS:
                    logits(p, u + 2)
                if u % 4 == 0 and u:
                    values(p, u // 4 - 1)
            values(p, 3)
            pe.wait_ge(o_done, 2 * p + 1)

    ph.close()


CHUNK = 64
TILES = S // P
DK, DV = 64, 128
SOLVES = HEADS * S // CHUNK
NQK = 8
SLICES = 2 * KD


def schedule():
    order, ticks = [], iter([(n, q) for n in range(N_PROJ - B_Z) for q in range(SLICES)])

    def dense(count):
        for _, (n, q) in zip(range(count), ticks):
            order.append(("dense", n, q))

    def side(kind, *index):
        order.append((kind, *index))

    dense(2)
    for i, count in enumerate((6, 8, 6, 8, 6, 4)):
        side("decay", i)
        dense(count)
    side("square", 0)
    side("square", 1)
    for n in range(NQK):
        side("norm", n)
        dense(3)
        if n:
            side("ship", n - 1)
            if n + 1 < NQK:
                side("square", n + 1)
        side("value", n)
        dense(5)
        side("turn", n)
        dense(6)
    side("ship", NQK - 1)
    for t in range(TILES):
        side("diff", t)
        dense(4)
        if t:
            side("ship_tile", t - 1)
        side("weights", t)
        side("ada", t)
        dense(5)
    side("ship_tile", TILES - 1)
    side("solve")
    dense(SOLVE_TICKS)
    for j in range(LATE, CHUNK - 1):
        side("solve_late", j)
        dense(3)
    side("solved")
    dense(8)
    side("mod", 0)
    dense(10)
    side("u", 0, 0)
    dense(2)
    side("u", 0, 1)
    dense(2)
    side("w", 0)
    dense(2)
    for t in range(TILES):
        side("read", 2 * t)
        dense(2)
        side("write", 2 * t)
        side("ada", KD + 2 * t)
        dense(3)
        if t:
            side("root", t - 1)
            dense(2)
            side("scale", t - 1)
            dense(1)
        side("read", 2 * t + 1)
        dense(1)
        if t:
            side("out", t - 1, 0)
            dense(1)
        side("write", 2 * t + 1)
        side("ada", KD + 2 * t + 1)
        dense(1)
        if t + 2 < TILES:
            side("load", t + 2)
        if t:
            side("out", t - 1, 1)
            dense(1)
            side("ship_out", t - 1)
        if t + 1 < TILES:
            dense(1)
            for step in (("u", t + 1, 0), ("u", t + 1, 1), ("w", t + 1)):
                side(*step)
                dense(2)
        if t == TILES // 2 - 1:
            side("mod", 1)
            dense(1)
    dense(2)
    side("mod", 2)
    side("root", TILES - 1)
    dense(2)
    side("scale", TILES - 1)
    dense(4)
    side("out", TILES - 1, 0)
    dense(2)
    side("out", TILES - 1, 1)
    dense(2)
    side("ship_out", TILES - 1)
    dense(1 << 20)
    return order


SOLVE_TICKS = 42
LATE = 26


def project_b(nc, g, d):
    ph = Scope(nc, "pb")
    BLOCKS = N_PROJ - B_Z
    ORDER = schedule()
    TH = TILES * HEADS
    raw = ph.sb("raw", [P, 2, KD * P])
    w_hi = ph.sb("w_hi", [P, 2, KD, P], F32R)
    w_lo = ph.sb("w_lo", [P, 2, KD, P], F32R)
    stage = ph.sb("stage", [P, 2, HALF])
    ps = [ph.ps(f"s{i}", [P, HALF]) for i in range(2)]
    ld, st = ph.sems("ld", 2), ph.sems("st", 2)
    hi_done, lo_done, mm_done, out_done = (ph.sem(n) for n in ("hi_done", "lo_done", "mm_done", "out_done"))

    beta_sys = ph.sb("beta_sys", [P, CHUNK])
    eg_row = ph.sb("eg_row", [HEADS, S])
    g_tok, beta_tok, beta_eg_tok, rest_tok = (ph.sb(n, [P, TH]) for n in ("g_tok", "beta_tok", "beta_eg_tok", "rest_tok"))
    chunk_decay = ph.sb("chunk_decay", [P, 2, TILES, 4])
    neg_a = ph.sb("neg_a", [HEADS, 1])
    AREAS = 22
    arena = ph.sb("arena", [P, AREAS * S])

    def area(first, pattern=None, count=1, **dims):
        cols = arena[:, int(first * S):int((first + count) * S)]
        return cols.rearrange(pattern, **dims) if pattern else cols

    rows = {name: area(8 + i)[0:HEADS] for i, name in enumerate(
        ("a", "b", "reset", "mag", "e", "u", "lnu", "resid", "rec", "gl", "gcum", "beta"))}
    tok = area(20, "p (k n) -> p k n", k=4, count=0.25)[:, 0:3]
    eg_tok = area(20.25)[:, 0:TH]
    XR, RING = 4, 4
    x = area(0, "p (s n) -> p s n", count=XR, s=XR)
    sq = area(4, "p (s n) -> p s n", count=2, s=2)
    norm, rn = area(6), area(7)
    q_n, k_n = (area(a, "p (b n) -> p b n", count=4, b=4) for a in (8, 12))
    ring = area(16, "p (s n) -> p s n", count=RING, s=RING)
    gu, decay = (area(a, "p (h n) -> p h n", h=HEADS) for a in (20, 21))
    lt = area(8, "p (j i) -> p j i", count=4, j=CHUNK)
    r = area(12, "p (c i) -> p c i", count=4, c=CHUNK)
    part, part_late = area(20), area(21)
    inv = area(0, "p (s h n) -> p s h n", count=2, s=2, h=HEADS)
    w_t = area(2, "p (s b n) -> p s b n", s=2, b=4)
    u = area(3, "p (s n) -> p s n", count=2, s=2)
    k_beta, k_rest = (area(a, "p (s n) -> p s n", s=2) for a in (5, 6))
    q_decayed = area(7, "p (s b n) -> p s b n", s=2, b=4)
    intra = area(16, "p (s h n) -> p s h n", count=2, s=2, h=HEADS)
    state, kept = (area(a, "p (b v) -> p b v", count=0.5, b=4) for a in (10, 10.5))
    v_new = area(11, "p (s n) -> p s n", count=2, s=2)
    o = area(13, "p (s n) -> p s n", count=2, s=2)
    o_sq = area(15)
    z = area(18, "p (s h n) -> p s h n", count=2, s=2, h=HEADS)
    o_t = area(8, "p (s h n) -> p s h n", count=2, s=2, h=HEADS)
    wa, acc = ph.sb("wa", [P, 2, D]), ph.sb("acc", [P, D])
    ss, std, rstd = ph.sb("ss", [P, HEADS]), ph.sb("std", [P, HEADS]), ph.sb("rstd", [P, HEADS])

    side_ps = ph.ps("side", [P, 3, S])
    ps_a, ps_b, ps_c = (side_ps[:, i] for i in range(3))
    ps_tok = side_ps[:, 0, 0:4 * TH].rearrange("p (k n) -> p k n", k=4)[:, 0:3]
    ps_sum = side_ps[:, 1, 0:4 * TH].rearrange("p (k n) -> p k n", k=4)[:, 0:3]
    ps_ws, ps_o = side_ps[:, 0], side_ps[:, 1]
    by_head = "p (r b v) -> p b r v"
    head_at = lambda h: slice(h % 2 * HALF + h // 2 * DV, h % 2 * HALF + h // 2 * DV + DV)
    ps_kv, ps_m = side_ps[:, 2, 0:HALF], side_ps[:, 2, HALF:S]

    ld_d, a_step, v_step, tr_done, total_done = (ph.sem(n) for n in ("ld_d", "a_step", "v_step", "tr_done", "total_done"))
    ld_x, st_r = ph.sems("ld_x", XR), ph.sems("st_r", RING)
    sq_done, ss_done, norm_done, rn_done, n_done = (ph.sem(n) for n in ("sq_done", "ss_done", "norm_done", "rn_done", "n_done"))
    bc_done, kt_done, vt_done, b_used, c_used, ring_full = (
        ph.sem(n) for n in ("bc_done", "kt_done", "vt_done", "b_used", "c_used", "ring_full"))
    gu_done, diff_done, exp_done, mask_done, prod_done, tile_done = (
        ph.sem(n) for n in ("gu_done", "diff_done", "exp_done", "mask_done", "prod_done", "tile_done"))
    ld_s, st_s, solve_step, late_step = (ph.sem(n) for n in ("ld_s", "st_s", "solve_step", "late_step"))
    ld_a, ada_done, mod_step = ph.sems("ld_a", 2), ph.sem("ada_done"), ph.sem("mod_step")
    ld_t, ld_z, st_o = ph.sems("ld_t", 2), ph.sems("ld_z", 2), ph.sems("st_o", 2)
    zeroed, m_filled, m_free = ph.sem("zeroed"), ph.sem("m_filled"), ph.sem("m_free")
    ws_done, vn_done, kept_done, kv_done, s_done = (ph.sem(n) for n in ("ws_done", "vn_done", "kept_done", "kv_done", "s_done"))
    o_done, o_copied, sum_done, std_done, rstd_done, on_done = (
        ph.sem(n) for n in ("o_done", "o_copied", "sum_done", "std_done", "rstd_done", "on_done"))
    block = ph.stack.enter_context(nc.Block())
    ident = g.const[:, C_IDENT:C_IDENT + P]
    SOLVE_STEPS, LATE_STEPS = 3 + 2 * (CHUNK - 1), 2 * (CHUNK - 1 - LATE)

    ring_uses = []
    for n in range(NQK):
        ring_uses += [("value", n)] + ([("k_beta", n // 2), ("k_rest", n // 2)] if n % 2 else [("q", n // 2)])
    for t in range(TILES):
        ring_uses += [("system", t), ("intra", t)]
    ring_no = {key: n for n, key in enumerate(ring_uses)}

    def stored(slot, before):
        return sum(32 if key[0] == "system" else 16 for n, key in enumerate(ring_uses) if n < before and n % RING == slot)

    m_no = {key: n for n, key in enumerate([s for s in ORDER if s[0] in ("u", "w", "out", "mod")])}

    @block.sync
    def _(sp):
        def load_x(i):
            n = i // 2
            b = B_DN + 8 + n if i % 2 else B_DN + n // 2 + 4 * (n % 2)
            sp.dma_start(x[:, i % XR], d["proj"][b]).then_inc(ld_x[i % XR], 16)

        def ship(kind, n):
            no = ring_no[kind, n]
            src = ring[:, no % RING]
            sp.wait_ge(ring_full, no + 1)
            if kind == "system":
                dst = d["systems"].rearrange("(h t c) j i -> t c j h i", h=HEADS, c=2)[n]
                src = src.rearrange("p (h i) -> p h i", h=HEADS)
                for c in range(2):
                    half = slice(c * CHUNK, (c + 1) * CHUNK)
                    sp.dma_start(dst[c], src[half, :, half]).then_inc(st_r[no % RING], 16)
                return
            if kind == "q":
                dst = d["q_decayed"][n]
            elif kind == "intra":
                dst = d["intra"][n]
            else:
                dst = d[kind][:, :, n * P:(n + 1) * P]
                src = src.rearrange("p (t k) -> p t k", t=TILES)
            sp.dma_start(dst, src).then_inc(st_r[no % RING], 16)

        def load_inv(t):
            for c in range(2):
                half = slice(c * CHUNK, (c + 1) * CHUNK)
                src = d["solved"].rearrange("(h t c) j i -> t c j h i", h=HEADS, c=2)[t, c]
                sp.dma_start(inv[half, t % 2, :, half], src).then_inc(ld_t[t % 2], 16)

        def load_tile(t):
            s = t % 2
            sp.dma_start(u[:, s], d["value"][:, t]).then_inc(ld_t[s], 16)
            sp.dma_start(k_beta[:, s], d["k_beta"][:, t]).then_inc(ld_t[s], 16)
            sp.dma_start(k_rest[:, s], d["k_rest"][:, t]).then_inc(ld_t[s], 16)
            src = d["q_decayed"].rearrange("b p n -> p b n")[:, :, t * P:(t + 1) * P]
            sp.dma_start(q_decayed[:, s], src).then_inc(ld_t[s], 16)
            src = d["intra"][t].rearrange("p (h n) -> p h n", h=HEADS)
            sp.dma_start(intra[:, s], src).then_inc(ld_t[s], 16)

        def load_z(t):
            src = d["proj"][B_Z:B_SB].rearrange("h v n -> v h n")[:, :, t * P:(t + 1) * P]
            sp.dma_start(z[:, t % 2], src).then_inc(ld_z[t % 2], 16)

        def store_half(n, half):
            sp.wait_ge(out_done, 2 * n + half + 1)
            sp.dma_start(d["proj"][B_Z + n][:, half * HALF:(half + 1) * HALF], stage[:, half]).then_inc(st[half], 16)

        def load_ada(i):
            if i >= 2:
                sp.wait_ge(ada_done, i - 1)
            sp.dma_start(wa[:, i % 2], d["w_ada"][3 + i // KD, i % KD // 4][:, i % 4]).then_inc(ld_a[i % 2], 16)

        ab = d["proj"][0]
        sp.dma_start(raw[:, 0], d["w_in"][B_Z][:, 0:KD * P]).then_inc(ld[0], 16)
        for dst, src in ((rows["b"], ab[0:HEADS]), (rows["a"], ab[HEADS:2 * HEADS]),
                         (beta_sys[:], ab[0:HEADS].rearrange("h (c i) -> (h c) i", i=CHUNK)), (rows["reset"], d["reset"])):
            sp.dma_start(dst, src).then_inc(ld_d, 16)
        sp.dma_start(raw[:, 1], d["w_in"][B_Z + 1][:, 0:KD * P]).then_inc(ld[1], 16)
        for i in range(XR):
            load_x(i)
        load_ada(0)
        load_ada(1)
        for kind, *index in ORDER:
            if kind == "dense":
                n, q = index
                if q == 0:
                    if n:
                        store_half(n - 1, 1)
                    if n + 2 < BLOCKS:
                        sp.wait_ge(lo_done, n + 1)
                        sp.dma_start(raw[:, n % 2], d["w_in"][B_Z + n + 2][:, 0:KD * P]).then_inc(ld[n % 2], 16)
                elif q == KD:
                    store_half(n, 0)
            elif kind == "ship":
                n, = index
                if 2 * n + XR < 2 * NQK:
                    sp.wait_ge(n_done, n + 1)
                    load_x(2 * n + XR)
                    sp.wait_ge(vt_done, n + 1)
                    load_x(2 * n + XR + 1)
                ship("value", n)
                for name in ("k_beta", "k_rest") if n % 2 else ("q",):
                    ship(name, n // 2)
            elif kind == "ada":
                if index[0] >= 1 and index[0] + 1 < 3 * KD:
                    load_ada(index[0] + 1)
            elif kind == "ship_tile":
                ship("system", *index)
                ship("intra", *index)
            elif kind == "solve":
                for s in range(RING):
                    sp.wait_ge(st_r[s], stored(s, len(ring_uses)))
                sp.wait_ge(tile_done, TILES)
                sp.dma_start(lt, d["systems"]).then_inc(ld_s, 16)
                for s in range(2):
                    sp.wait_ge(st[s], 16 * (B_SB - B_Z))
                for t in range(2):
                    load_tile(t)
                    load_z(t)
            elif kind == "solved":
                sp.wait_ge(solve_step, SOLVE_STEPS)
                sp.wait_ge(late_step, LATE_STEPS)
                sp.dma_start(d["solved"], r).then_inc(st_s, 16)
                sp.wait_ge(zeroed, 2)
                sp.wait_ge(st_s, 16)
                for t in range(2):
                    load_inv(t)
            elif kind == "load":
                t, = index
                sp.wait_ge(o_done, t - 1)
                load_inv(t)
                load_tile(t)
            elif kind == "ship_out":
                t, = index
                sp.wait_ge(m_free, m_no["out", t, 1] + 1)
                sp.dma_start(d["o_b"].rearrange("h v n -> v h n")[:, :, t * P:(t + 1) * P], o_t[:, t % 2])\
                  .then_inc(st_o[t % 2], 16)
                if t + 2 < TILES:
                    load_z(t + 2)
        store_half(BLOCKS - 1, 1)
        for s in range(2):
            sp.wait_ge(st_o[s], 16 * TILES // 2)
            sp.wait_ge(st[s], 16 * BLOCKS)

    @block.scalar
    def _(act):
        def split(n):
            act.wait_ge(ld[n % 2], 16 * (n // 2 + 1))
            if n >= 2:
                act.wait_ge(mm_done, 2 * (n - 1))
            act.activation(w_hi[:, n % 2], raw[:, n % 2].rearrange("p (k m) -> p k m", k=KD), ACT.Copy)\
               .then_inc(hi_done, 1)

        def evacuate(n, half):
            func = ACT.Silu if n < B_SB - B_Z else ACT.Copy if n < B_GATE - B_Z else ACT.Sigmoid
            act.wait_ge(mm_done, 2 * n + half + 1)
            if n:
                act.wait_ge(st[half], 16 * n)
            act.activation(stage[:, half], ps[half][:], func).then_inc(out_done, 1)

        def decay_part(i):
            if i == 0:
                act.wait_ge(ld_d, 64)
                act.activation(rows["beta"], rows["b"], ACT.Sigmoid).then_inc(a_step, 1)
                act.activation(beta_sys[:], beta_sys[:], ACT.Sigmoid).then_inc(a_step, 1)
            elif i == 1:
                act.wait_ge(v_step, 1)
                act.activation(rows["mag"], rows["a"], ACT.Abs).then_inc(a_step, 1)
                act.wait_ge(a_step, 3)
                act.activation(rows["e"], rows["mag"], ACT.Exp, scale=-1.0).then_inc(a_step, 1)
                act.activation(neg_a[:], g.small["dn_head"][:, 0:1], ACT.Exp).then_inc(a_step, 1)
            elif i == 2:
                act.wait_ge(v_step, 2)
                act.activation(rows["lnu"], rows["u"], ACT.Ln).then_inc(a_step, 1)
            elif i == 4:
                act.wait_ge(v_step, 10)
                act.activation(eg_row[:], rows["gcum"], ACT.Exp).then_inc(a_step, 1)
            elif i == 5:
                act.wait_ge(v_step, 11)
                act.activation(eg_tok, tok[:, 2], ACT.Exp).then_inc(a_step, 1)
                act.wait_ge(total_done, 1)
                act.activation(rest_tok[:], ps_sum[:, 0], ACT.Exp).then_inc(a_step, 1)
                for par in range(2):
                    half = slice(par * DK, (par + 1) * DK)
                    src = ps_sum[half, 1:3].rearrange("p c (t h) -> p c t h", h=HEADS)[:, :, :, par::2]
                    act.activation(chunk_decay[half], src, ACT.Exp).then_inc(a_step, 1)

        split(0)
        for kind, *index in ORDER:
            if kind == "dense":
                n, q = index
                if q == 0:
                    if n:
                        evacuate(n - 1, 1)
                    if n + 1 < BLOCKS:
                        split(n + 1)
                elif q == KD:
                    evacuate(n, 0)
            elif kind == "decay":
                decay_part(*index)
            elif kind == "square":
                n, = index
                i = 2 * n
                act.wait_ge(ld_x[i % XR], 16 * (i // XR + 1))
                if n >= 2:
                    act.wait_ge(ss_done, n - 1)
                act.activation(sq[:, n % 2], x[:, i % XR], ACT.Square).then_inc(sq_done, 1)
            elif kind == "norm":
                n, = index
                act.wait_ge(ss_done, n + 1)
                if n:
                    act.wait_ge(rn_done, n)
                act.activation(norm, ps_a, ACT.Sqrt, bias=g.eps[:]).then_inc(norm_done, 1)
            elif kind == "diff":
                t, = index
                act.wait_ge(diff_done, t + 1)
                if t:
                    act.wait_ge(tile_done, t)
                act.activation(decay.rearrange("p h i -> p (h i)"), ps_a, ACT.Exp).then_inc(exp_done, 1)
            elif kind == "u":
                t, half = index
                act.wait_ge(m_filled, m_no["u", t, half] + 1)
                act.activation(u[:, t % 2, half * HALF:(half + 1) * HALF], ps_m, ACT.Copy).then_inc(m_free, 1)
            elif kind == "w":
                t, = index
                act.wait_ge(m_filled, m_no["w", t] + 1)
                act.activation(w_t[:, t % 2], ps_m.rearrange("p (b n) -> p b n", b=4), ACT.Copy).then_inc(m_free, 1)
            elif kind == "mod":
                i, = index
                act.wait_ge(m_filled, m_no["mod", i] + 1)
                act.activation(g.mod[:, (3 + i) * KD:(4 + i) * KD], ps_m[:, 0:KD], ACT.Copy).then_inc(m_free, 1)
            elif kind == "write" and index[0] % 2:
                t = index[0] // 2
                act.wait_ge(o_done, t + 1)
                if t:
                    act.wait_ge(sum_done, t)
                if t >= 2:
                    act.wait_ge(m_filled, m_no["out", t - 2, 1] + 1)
                for dst, func in ((o[:, t % 2], ACT.Copy), (o_sq, ACT.Square)):
                    act.activation(dst.rearrange("p (b r v) -> p b r v", b=4, r=2), ps_o.rearrange(by_head, r=2, b=4), func)\
                       .then_inc(o_copied, 1)
            elif kind == "root":
                t, = index
                act.wait_ge(sum_done, t + 1)
                act.activation(std[:], ss[:], ACT.Sqrt, scale=1.0 / DV, bias=g.eps[:]).then_inc(std_done, 1)
        evacuate(BLOCKS - 1, 1)

    @block.gpsimd
    def _(pool):
        incl_h = g.const[:, C_INCL:C_INCL + P].unsqueeze(1).to_broadcast([P, HEADS, P])

        def low(n):
            pool.wait_ge(hi_done, n + 1)
            pool.tensor_tensor(w_lo[:, n % 2], raw[:, n % 2].rearrange("p (k m) -> p k m", k=KD),
                               as_f32(w_hi[:, n % 2]), ALU.subtract).then_inc(lo_done, 1)

        def spread(t):
            if t:
                pool.wait_ge(diff_done, t)
            g_t = g_tok[:, t * HEADS:(t + 1) * HEADS]
            pool.tensor_tensor(gu, incl_h, g_t.unsqueeze(2).to_broadcast([P, HEADS, P]), ALU.mult).then_inc(gu_done, 1)

        low(0)
        for kind, *index in ORDER:
            if kind == "dense":
                n, q = index
                if q == 0 and n + 1 < BLOCKS:
                    low(n + 1)
            elif kind == "diff":
                t, = index
                pool.wait_ge(exp_done, t + 1)
                pool.tensor_tensor(decay, decay, incl_h, ALU.mult).then_inc(mask_done, 1)
                if t + 1 < TILES:
                    spread(t + 1)
            elif kind == "turn" and index[0] == NQK - 1:
                pool.wait_ge(a_step, 11)
                pool.wait_ge(v_step, 14)
                spread(0)
            elif kind == "solve":
                pool.wait_ge(tile_done, TILES)
                for s in range(2):
                    pool.memset(inv[:, s], 0.0).then_inc(zeroed, 1)
                pool.wait_ge(solve_step, 3)
            elif kind == "solve_late":
                j, = index
                c, i = j + 1 - LATE, CHUNK - 1 - j
                out = part_late[:, 0:c * i].rearrange("p (c i) -> p c i", c=c)
                if j > LATE:
                    pool.wait_ge(late_step, 2 * (j - LATE))
                pool.tensor_tensor(out, r[:, LATE:j + 1, j:j + 1].to_broadcast([P, c, i]),
                                   lt[:, j:j + 1, j + 1:CHUNK].to_broadcast([P, c, i]), ALU.mult).then_inc(late_step, 1)
                pool.wait_ge(late_step, 2 * (j - LATE) + 1)
                pool.tensor_tensor(r[:, LATE:j + 1, j + 1:CHUNK], r[:, LATE:j + 1, j + 1:CHUNK], out, ALU.subtract)\
                    .then_inc(late_step, 1)
            elif kind == "solved":
                pool.wait_ge(solve_step, SOLVE_STEPS)
                pool.wait_ge(late_step, LATE_STEPS)
                pool.memset(state, 0.0).then_inc(zeroed, 1)
                pool.wait_ge(zeroed, 3)
            elif kind == "read":
                n, = index
                if n:
                    pool.wait_ge(s_done, n)
                by = chunk_decay[:, n % 2, n // 2].unsqueeze(2).to_broadcast([P, 4, DV])
                pool.tensor_tensor(kept, state, by, ALU.mult).then_inc(kept_done, 1)
            elif kind == "scale":
                t, = index
                pool.wait_ge(rstd_done, t + 1)
                o_h = o[:, t % 2].rearrange("p (h v) -> p h v", h=HEADS)
                pool.tensor_tensor(o_h, o_h, rstd[:].unsqueeze(2).to_broadcast([P, HEADS, DV]), ALU.mult)\
                    .then_inc(on_done, 1)

    @block.vector
    def _(dve):
        done = {v_step: 0, solve_step: 0}

        def then(ins, signal=v_step):
            done[signal] += 1
            ins.then_inc(signal, 1)
            dve.wait_ge(signal, done[signal])

        def ring_slot(key):
            no = ring_no[key]
            if no >= RING:
                dve.wait_ge(st_r[no % RING], stored(no % RING, no))
            return ring[:, no % RING]

        def decay_part(i):
            row = rows
            if i == 0:
                dve.wait_ge(ld_d, 64)
                then(dve.tensor_scalar(row["a"], row["a"], g.small["dn_head"][:, 1:2], None, ALU.add))
            elif i == 1:
                dve.wait_ge(a_step, 5)
                then(dve.tensor_scalar(row["u"], row["e"], 1.0, None, ALU.add))
                then(dve.tensor_scalar(row["resid"], row["u"], -1.0, None, ALU.add))
                then(dve.tensor_tensor(row["resid"], row["e"], row["resid"], ALU.subtract))
                then(dve.reciprocal(row["rec"], row["u"]))
                then(dve.tensor_tensor(row["resid"], row["resid"], row["rec"], ALU.mult))
            elif i == 2:
                dve.wait_ge(a_step, 6)
                then(dve.tensor_tensor(row["resid"], row["resid"], row["lnu"], ALU.add))
                then(dve.scalar_tensor_tensor(row["gl"], row["a"], 0.0, row["resid"], ALU.max, ALU.add))
                then(dve.tensor_scalar(row["gl"], row["gl"], neg_a[:], -1.0, ALU.mult, ALU.mult))
                then(dve.tensor_tensor_scan(row["gcum"], row["reset"], row["gl"], 0.0, ALU.mult, ALU.add))
            elif i == 4:
                dve.wait_ge(tr_done, 1)
                then(dve.tensor_copy(tok, ps_tok))
                dve.tensor_copy(g_tok[:], tok[:, 0]).then_inc(v_step, 1)
                dve.tensor_copy(beta_tok[:], tok[:, 1]).then_inc(v_step, 1)
                dve.wait_ge(a_step, 8)
                dve.tensor_tensor(beta_eg_tok[:], tok[:, 1], eg_tok, ALU.mult).then_inc(v_step, 1)

        for kind, *index in ORDER:
            if kind == "decay":
                decay_part(*index)
            elif kind == "norm":
                n, = index
                i, b = 2 * n, n // 2
                dve.wait_ge(norm_done, n + 1)
                if n:
                    dve.wait_ge(n_done, n)
                dve.reciprocal(rn, norm).then_inc(rn_done, 1)
                dve.wait_ge(rn_done, n + 1)
                if n % 2 == 0:
                    dve.scalar_tensor_tensor(q_n[:, b], x[:, i % XR], DK ** -0.5, rn, ALU.mult, ALU.mult)\
                       .then_inc(n_done, 1)
                else:
                    dve.tensor_tensor(k_n[:, b], x[:, i % XR], rn, ALU.mult).then_inc(n_done, 1)
            elif kind == "value":
                h, = index
                dve.wait_ge(vt_done, h + 1)
                dve.wait_ge(v_step, 14)
                by = beta_tok[:].rearrange("p (t h) -> p t h", h=HEADS)[:, :, h:h + 1]
                ps_v, used = ((ps_c, c_used), (ps_b, b_used))[h % 2]
                dst = ring_slot(("value", h)).rearrange("p (t v) -> p t v", t=TILES)
                dve.tensor_tensor(dst, ps_v.rearrange("p (t v) -> p t v", t=TILES), by.to_broadcast([P, TILES, DV]),
                                  ALU.mult).then_inc(used, 1)
                dve.wait_ge(used, h + 1)
                dve.sem_inc(ring_full, 1)
            elif kind == "turn":
                n, = index
                b = n // 2
                if n % 2 == 0:
                    dve.wait_ge(n_done, n + 1)
                    dve.wait_ge(bc_done, b + 1)
                    dve.tensor_tensor(ring_slot(("q", b)), q_n[:, b], ps_b, ALU.mult).then_inc(b_used, 1)
                    dve.wait_ge(b_used, n + 1)
                    dve.sem_inc(ring_full, 1)
                else:
                    dve.wait_ge(kt_done, b + 1)
                    if b == 0:
                        dve.wait_ge(a_step, 11)
                    k_tok = ps_c.rearrange("p (t h k) -> p t h k", t=TILES, h=2)
                    for name, by in (("k_beta", beta_eg_tok), ("k_rest", rest_tok)):
                        by = by[:].rearrange("p (t h) -> p t h", h=HEADS)[:, :, 2 * b:2 * b + 2]
                        dst = ring_slot((name, b)).rearrange("p (t h k) -> p t h k", t=TILES, h=2)
                        dve.tensor_tensor(dst, k_tok, by.unsqueeze(3).to_broadcast([P, TILES, 2, DK]), ALU.mult)\
                           .then_inc(ring_full, 1)
                    dve.wait_ge(ring_full, ring_no["k_rest", b] + 1)
                    dve.sem_inc(c_used, 1)
            elif kind == "weights":
                t, = index
                dve.wait_ge(mask_done, t + 1)
                dve.wait_ge(prod_done, t + 1)
                for name, src in (("system", ps_b), ("intra", ps_c)):
                    dst = ring_slot((name, t)).rearrange("p (h i) -> p h i", h=HEADS)
                    for par in range(2):
                        prod = src[:, par * HALF:(par + 1) * HALF].rearrange("p (h i) -> p h i", h=4)
                        ins = dve.tensor_tensor(dst[:, par::2], prod, decay[:, par::2], ALU.mult)
                    ins.then_inc(ring_full, 1)
                dve.wait_ge(ring_full, ring_no["intra", t] + 1)
                dve.sem_inc(tile_done, 1)
            elif kind == "solve":
                then(dve.memset(r, 0.0), solve_step)
                then(dve.memset(r.rearrange("p c i -> p (c i)")[:, 0:CHUNK * CHUNK:CHUNK + 1], 1.0), solve_step)
                dve.wait_ge(ld_s, 16)
                then(dve.tensor_tensor(lt, lt, beta_sys[:].unsqueeze(1).to_broadcast([P, CHUNK, CHUNK]), ALU.mult),
                     solve_step)
                for j in range(CHUNK - 1):
                    c, i = min(j + 1, LATE), CHUNK - 1 - j
                    out = part[:, 0:c * i].rearrange("p (c i) -> p c i", c=c)
                    then(dve.tensor_tensor(out, r[:, 0:c, j:j + 1].to_broadcast([P, c, i]),
                                           lt[:, j:j + 1, j + 1:CHUNK].to_broadcast([P, c, i]), ALU.mult), solve_step)
                    then(dve.tensor_tensor(r[:, 0:c, j + 1:CHUNK], r[:, 0:c, j + 1:CHUNK], out, ALU.subtract),
                         solve_step)
            elif kind == "read":
                n, = index
                t, c = n // 2, n % 2
                half = slice(c * CHUNK, (c + 1) * CHUNK)
                dve.wait_ge(ws_done, n + 1)
                if t >= 2:
                    dve.wait_ge(o_done, t - 1)
                natural = lambda ap: ap.rearrange("p (b r v) -> p b r v", b=4, r=2)
                dve.tensor_tensor(natural(v_new[half, t % 2]), natural(u[half, t % 2]),
                                  ps_ws[half].rearrange(by_head, r=2, b=4), ALU.subtract).then_inc(vn_done, 1)
            elif kind == "write":
                n, = index
                dve.wait_ge(kv_done, n + 1)
                dve.wait_ge(kept_done, n + 1)
                dve.tensor_tensor(state, kept, ps_kv.rearrange("p (b v) -> p b v", b=4), ALU.add).then_inc(s_done, 1)
            elif kind == "ada":
                i, = index
                c_k = g.c_act[:, i % KD:i % KD + 1]
                dve.wait_ge(ld_a[i % 2], 16 * (i // 2 + 1))
                if i % KD == 0:
                    if i:
                        dve.wait_ge(m_free, m_no["mod", i // KD - 1] + 1)
                    ins = dve.tensor_scalar(acc[:], wa[:, i % 2], c_k, None, ALU.mult)
                else:
                    dve.wait_ge(ada_done, i)
                    ins = dve.scalar_tensor_tensor(acc[:], wa[:, i % 2], c_k, acc[:], ALU.mult, ALU.add)
                ins.then_inc(ada_done, 1)
            elif kind == "root":
                t, = index
                dve.wait_ge(o_copied, 2 * t + 2)
                if t:
                    dve.wait_ge(std_done, t)
                dve.tensor_reduce(ss[:], o_sq.rearrange("p (h v) -> p h v", h=HEADS), AX.X, ALU.add)\
                   .then_inc(sum_done, 1)
            elif kind == "scale":
                t, = index
                dve.wait_ge(std_done, t + 1)
                if t:
                    dve.wait_ge(on_done, t)
                dve.reciprocal(rstd[:], std[:]).then_inc(rstd_done, 1)
            elif kind == "out":
                t, half = index
                s = t % 2
                dve.wait_ge(m_filled, m_no["out", t, half] + 1)
                dve.wait_ge(ld_z[s], 16 * (t // 2 + 1))
                if t >= 2:
                    dve.wait_ge(st_o[s], 16 * (t // 2))
                heads = slice(4 * half, 4 * half + 4)
                dve.scalar_tensor_tensor(o_t[:, s, heads], ps_m.rearrange("p (h n) -> p h n", h=4),
                                         g.small["dn_norm"][:], z[:, s, heads], ALU.mult, ALU.mult)\
                   .then_inc(m_free, 1)
        dve.wait_ge(m_free, m_no["mod", 2] + 1)
        dve.tensor_tensor(g.mod[:, 3 * KD:6 * KD], g.mod[:, 3 * KD:6 * KD], g.small["b_ada"][:, 3 * KD:6 * KD], ALU.add)\
           .then_inc(mod_step, 1)
        dve.wait_ge(mod_step, 1)
        dve.scalar_tensor_tensor(g.mod[:, 4 * KD:5 * KD], g.mod[:, 4 * KD:5 * KD], 1.0,
                                 g.small["norms"][:, KD:2 * KD], ALU.add, ALU.mult).then_inc(mod_step, 1)

    @block.tensor
    def _(pe):
        def dense(n, q):
            half, k = q // KD, q % KD
            if q == 0:
                pe.wait_ge(lo_done, n + 1)
            if k == 0 and n:
                pe.wait_ge(out_done, 2 * (n - 1) + half + 1)
            cols = slice(half * HALF, (half + 1) * HALF)
            for i, (w, h) in enumerate(three(w_hi[:, n % 2, k], w_lo[:, n % 2, k], g.h_hi[:, k, cols], g.h_lo[:, k, cols])):
                mm = pe.matmul(ps[half][:], w, h, start=k == 0 and i == 0, stop=k == KD - 1 and i == 2)
            if k == KD - 1:
                mm.then_inc(mm_done, 1)

        def take_m(key):
            if m_no[key]:
                pe.wait_ge(m_free, m_no[key])

        for kind, *index in ORDER:
            if kind == "dense":
                dense(*index)
            elif kind == "decay" and index[0] == 4:
                pe.wait_ge(a_step, 1)
                pe.wait_ge(v_step, 10)
                ident8 = g.const[0:HEADS, C_IDENT:C_IDENT + HEADS]
                for i, name in enumerate(("gl", "beta", "gcum")):
                    for t in range(TILES):
                        mm = pe.transpose(ps_tok[:, i, t * HEADS:(t + 1) * HEADS], rows[name][:, t * P:(t + 1) * P], ident8)
                mm.then_inc(tr_done, 1)
            elif kind == "decay" and index[0] == 5:
                pe.wait_ge(v_step, 11)
                for i, table in enumerate((C_STRICT, C_EVEN, C_ODD)):
                    mm = pe.matmul(ps_sum[:, i], g.const[:, table:table + P], tok[:, 0], start=True, stop=True)
                mm.then_inc(total_done, 1)
            elif kind == "norm":
                n, = index
                pe.wait_ge(sq_done, n + 1)
                if n:
                    pe.wait_ge(norm_done, n)
                for t in range(2):
                    cols = slice(t * HALF, (t + 1) * HALF)
                    mm = pe.matmul(ps_a[:, cols], g.const[:, C_ONES64:C_ONES64 + P], sq[:, n % 2, cols], start=True, stop=True)
                mm.then_inc(ss_done, 1)
            elif kind == "value":
                h, = index
                i = 2 * h + 1
                pe.wait_ge(ld_x[i % XR], 16 * (i // XR + 1))
                if h:
                    pe.wait_ge((c_used, b_used)[h % 2], h)
                else:
                    pe.wait_ge(a_step, 11)
                for t in range(TILES):
                    mm = pe.transpose((ps_c, ps_b)[h % 2][:, t * P:(t + 1) * P], x[:, i % XR, t * P:(t + 1) * P], ident)
                mm.then_inc(vt_done, 1)
            elif kind == "turn":
                n, = index
                b = n // 2
                if n % 2 == 0:
                    if b:
                        pe.wait_ge(b_used, n)
                    for t in range(2):
                        cols = slice(t * HALF, (t + 1) * HALF)
                        mm = pe.matmul(ps_b[:, cols], g.const[0:HEADS, C_SEL + b * P:C_SEL + (b + 1) * P],
                                       eg_row[:, cols], start=True, stop=True)
                    mm.then_inc(bc_done, 1)
                else:
                    pe.wait_ge(n_done, n + 1)
                    pe.wait_ge(c_used, n)
                    for t in range(TILES):
                        mm = pe.transpose(ps_c[:, t * P:(t + 1) * P], k_n[:, b, t * P:(t + 1) * P], ident)
                    mm.then_inc(kt_done, 1)
            elif kind == "diff":
                t, = index
                pe.wait_ge(gu_done, t + 1)
                pe.wait_ge(*((exp_done, t) if t else (norm_done, NQK)))
                for i in range(2):
                    mm = pe.matmul(ps_a[:, i * HALF:(i + 1) * HALF], g.const[:, C_STRICT:C_STRICT + P],
                                   gu[:, 4 * i:4 * i + 4], start=True, stop=True)
                mm.then_inc(diff_done, 1)
            elif kind == "weights":
                t, = index
                if t:
                    pe.wait_ge(tile_done, t)
                else:
                    pe.wait_ge(b_used, NQK)
                    pe.wait_ge(c_used, NQK)
                cols = slice(t * P, (t + 1) * P)
                for dst, rhs in ((ps_b, k_n), (ps_c, q_n)):
                    for b in range(4):
                        for par in range(2):
                            half = slice(par * DK, (par + 1) * DK)
                            to = par * HALF + b * P
                            mm = pe.matmul(dst[:, to:to + P], k_n[half, b, cols], rhs[half, b, cols], start=True, stop=True)
                mm.then_inc(prod_done, 1)
            elif kind == "u":
                t, half = index
                take_m((kind, *index))
                pe.wait_ge(ld_t[t % 2], 112 * (t // 2 + 1))
                for h in range(4 * half, 4 * half + 4):
                    mm = pe.matmul(ps_m[:, h % 4 * DV:(h % 4 + 1) * DV], inv[:, t % 2, h], u[:, t % 2, h * DV:(h + 1) * DV],
                                   start=True, stop=True)
                mm.then_inc(m_filled, 1)
            elif kind == "w":
                t, = index
                take_m((kind, t))
                for h in range(HEADS):
                    half = slice(h % 2 * DK, h % 2 * DK + DK)
                    mm = pe.matmul(ps_m[half, h // 2 * P:(h // 2 + 1) * P], k_beta[:, t % 2, h * DK:(h + 1) * DK],
                                   inv[:, t % 2, h], start=True, stop=True)
                mm.then_inc(m_filled, 1)
            elif kind == "mod":
                take_m((kind, *index))
                pe.wait_ge(tile_done, TILES)
                pe.wait_ge(ada_done, KD * (index[0] + 1))
                for m in range(KD):
                    mm = pe.matmul(ps_m[:, m:m + 1], acc[:, m * P:(m + 1) * P], g.const[:, C_ONES:C_ONES + 1],
                                   start=True, stop=True)
                mm.then_inc(m_filled, 1)
            elif kind == "out":
                t, half = index
                take_m((kind, *index))
                pe.wait_ge(on_done, t + 1)
                for h in range(4 * half, 4 * half + 4):
                    mm = pe.transpose(ps_m[:, h % 4 * P:(h % 4 + 1) * P], o[:, t % 2, h * DV:(h + 1) * DV], ident)
                mm.then_inc(m_filled, 1)
            elif kind == "read":
                n, = index
                t, c = n // 2, n % 2
                to = slice(c * CHUNK, (c + 1) * CHUNK)
                pe.wait_ge(m_free, m_no["w", t] + 1)
                if n:
                    pe.wait_ge(s_done, n)
                else:
                    pe.wait_ge(zeroed, 3)
                for h in range(HEADS):
                    half = slice(h % 2 * DK, h % 2 * DK + DK)
                    mm = pe.matmul(ps_ws[to, head_at(h)], w_t[half, t % 2, h // 2, to], state[half, h // 2],
                                   start=True, stop=True)
                mm.then_inc(ws_done, 1)
                if t:
                    pe.wait_ge(o_copied, 2 * t)
                for h in range(HEADS):
                    half = slice(h % 2 * DK, h % 2 * DK + DK)
                    pe.matmul(ps_o[to, head_at(h)], q_decayed[half, t % 2, h // 2, to], state[half, h // 2],
                              start=h < 2, stop=False, skip_group_check=True)
            elif kind == "write":
                n, = index
                t, c = n // 2, n % 2
                frm = slice(c * CHUNK, (c + 1) * CHUNK)
                pe.wait_ge(vn_done, n + 1)
                for h in range(HEADS):
                    half = slice(h % 2 * DK, h % 2 * DK + DK)
                    mm = pe.matmul(ps_kv[half, h // 2 * DV:(h // 2 + 1) * DV], k_rest[frm, t % 2, h * DK:(h + 1) * DK],
                                   v_new[frm, t % 2, h * DV:(h + 1) * DV], start=True, stop=True)
                mm.then_inc(kv_done, 1)
                if c == 1:
                    for h in range(HEADS):
                        mm = pe.matmul(ps_o[:, head_at(h)], intra[:, t % 2, h], v_new[:, t % 2, h * DV:(h + 1) * DV],
                                       start=False, stop=True, skip_group_check=True)
                    mm.then_inc(o_done, 1)

    ph.close()


def merge(nc, g, d):
    ph = Scope(nc, "merge")
    KA, KB = HEADS // 2, KD
    K = KA + KB
    raw = ph.sb("raw", [P, 2, K * P])
    w_hi, w_lo = ph.sb("w_hi", [P, 2, K, P], F32R), ph.sb("w_lo", [P, 2, K, P], F32R)
    o_raw = ph.sb("o_raw", [P, 2, S])
    o_hi, o_lo = ph.sb("o_hi", [P, K, S], F32R), ph.sb("o_lo", [P, K, S], F32R)
    gates = ph.sb("gates", [P, 2, 2, S])
    ps = [[ph.ps(f"s{s}_{i}", [P, S]) for i in range(2)] for s in range(2)]
    ld, ld_g, ld_o = ph.sems("ld", 2), ph.sems("ld_g", 2), ph.sems("ld_o", 2)
    oh_done, ol_done, hi_done, lo_done, mm_done, part_done, out_done = (
        ph.sem(n) for n in ("oh_done", "ol_done", "hi_done", "lo_done", "mm_done", "part_done", "out_done"))
    block = ph.stack.enter_context(nc.Block())

    @block.sync
    def _(sp):
        def load_w(m):
            if m >= 2:
                sp.wait_ge(lo_done, m - 1)
            sp.dma_start(raw[:, m % 2], d["w_merge"][m]).then_inc(ld[m % 2], 16)

        def load_gates(m):
            if m >= 2:
                sp.wait_ge(out_done, m - 1)
            for i in range(2):
                sp.dma_start(gates[:, m % 2, i], d["proj"][B_GATE + i * KD + m]).then_inc(ld_g[m % 2], 16)

        load_w(0)
        for k in range(K):
            if k >= 2:
                sp.wait_ge(ol_done, k - 1)
            src = d["o_a"][k] if k < KA else d["o_b"][k - KA]
            sp.dma_start(o_raw[:, k % 2], src).then_inc(ld_o[k % 2], 16)
        load_w(1)
        load_gates(0)
        load_gates(1)
        for m in range(2, KD):
            load_w(m)
            load_gates(m)

    @block.scalar
    def _(act):
        def split(m):
            act.wait_ge(ld[m % 2], 16 * (m // 2 + 1))
            if m >= 2:
                act.wait_ge(mm_done, m - 1)
            act.activation(w_hi[:, m % 2].rearrange("p k n -> p (k n)"), raw[:, m % 2], ACT.Copy).then_inc(hi_done, 1)

        split(0)
        for k in range(K):
            act.wait_ge(ld_o[k % 2], 16 * (k // 2 + 1))
            act.activation(o_hi[:, k], o_raw[:, k % 2], ACT.Copy).then_inc(oh_done, 1)
        for m in range(1, KD):
            split(m)

    @block.gpsimd
    def _(pool):
        def low(m):
            pool.wait_ge(hi_done, m + 1)
            pool.tensor_tensor(w_lo[:, m % 2].rearrange("p k n -> p (k n)"), raw[:, m % 2],
                               as_f32(w_hi[:, m % 2].rearrange("p k n -> p (k n)")), ALU.subtract).then_inc(lo_done, 1)

        low(0)
        for m in range(1, KD):
            low(m)
            pool.wait_ge(part_done, 2 * m)
            pool.tensor_tensor(g.merged[:, m - 1], gates[:, (m - 1) % 2, 0], gates[:, (m - 1) % 2, 1], ALU.add)\
                .then_inc(out_done, 1)
        pool.wait_ge(part_done, 2 * KD)
        pool.tensor_tensor(g.merged[:, KD - 1], gates[:, (KD - 1) % 2, 0], gates[:, (KD - 1) % 2, 1], ALU.add)\
            .then_inc(out_done, 1)

    @block.vector
    def _(dve):
        for k in range(K):
            dve.wait_ge(oh_done, k + 1)
            dve.tensor_tensor(o_lo[:, k], o_raw[:, k % 2], as_f32(o_hi[:, k]), ALU.subtract).then_inc(ol_done, 1)
        for m in range(KD):
            dve.wait_ge(mm_done, m + 1)
            dve.wait_ge(ld_g[m % 2], 32 * (m // 2 + 1))
            for i in range(2):
                gate = gates[:, m % 2, i]
                dve.tensor_tensor(gate, ps[m % 2][i][:], gate, ALU.mult).then_inc(part_done, 1)

    @block.tensor
    def _(pe):
        for m in range(KD):
            s = m % 2
            pe.wait_ge(lo_done, m + 1)
            if m >= 2:
                pe.wait_ge(part_done, 2 * (m - 1))
            for k in range(K):
                if m == 0:
                    pe.wait_ge(ol_done, k + 1)
                branch, first, last = (0, 0, KA - 1) if k < KA else (1, KA, K - 1)
                for i, (w, x) in enumerate(three(w_hi[:, s, k], w_lo[:, s, k], o_hi[:, k], o_lo[:, k])):
                    for t in range(2):
                        cols = slice(t * HALF, (t + 1) * HALF)
                        mm = pe.matmul(ps[s][branch][:, cols], w, x[:, cols], start=k == first and i == 0,
                                       stop=k == last and i == 2)
            mm.then_inc(mm_done, 1)

    ph.close()


def output(nc, g, d):
    ph = Scope(nc, "out")
    raw = ph.sb("raw", [P, 2, KD * P])
    w_hi, w_lo = ph.sb("w_hi", [P, 2, KD, P], F32R), ph.sb("w_lo", [P, 2, KD, P], F32R)
    hi, lo = g.h_hi, g.h_lo
    x2 = ph.sb("x2", [P, KD, S])
    sq, total = ph.sb("sq", [P, S]), ph.sb("total", [P, S])
    hf = ph.sb("hf", [P, 2, S])
    ps = [ph.ps(f"s{s}", [P, S]) for s in range(2)]
    ps_ss = ph.ps("ss", [P, S])
    ld, ld_x, st = ph.sems("ld", 2), ph.sems("ld_x", KD), ph.sem("st")
    mh_done, ml_done, hi_done, lo_done, mm_done, x2_done = (
        ph.sem(n) for n in ("mh_done", "ml_done", "hi_done", "lo_done", "mm_done", "x2_done"))
    sq_done, add_done, ss_done, std_done, rstd_done = (
        ph.sem(n) for n in ("sq_done", "add_done", "ss_done", "std_done", "rstd_done"))
    xn_done, h_done, hh_done, hl_done = (ph.sem(n) for n in ("xn_done", "h_done", "hh_done", "hl_done"))
    block = ph.stack.enter_context(nc.Block())

    @block.sync
    def _(sp):
        for m in range(KD):
            if m >= 2:
                sp.wait_ge(lo_done, m - 1)
            sp.dma_start(raw[:, m % 2], d["w_out"][m]).then_inc(ld[m % 2], 16)
            sp.dma_start(x2[:, m], d["xT"][m]).then_inc(ld_x[m], 16)
        for m in range(KD):
            sp.wait_ge(x2_done, m + 1)
            sp.dma_start(d["x2"][m], x2[:, m]).then_inc(st, 16)
        sp.wait_ge(st, 16 * KD)

    @block.scalar
    def _(act):
        def split(m):
            act.wait_ge(ld[m % 2], 16 * (m // 2 + 1))
            if m >= 2:
                act.wait_ge(mm_done, m - 1)
            act.activation(w_hi[:, m % 2].rearrange("p k n -> p (k n)"), raw[:, m % 2], ACT.Copy).then_inc(hi_done, 1)

        split(0)
        for k in range(KD):
            act.activation(hi[:, k], g.merged[:, k], ACT.Copy).then_inc(mh_done, 1)
        for m in range(KD):
            if m + 1 < KD:
                split(m + 1)
            act.wait_ge(x2_done, m + 1)
            if m:
                act.wait_ge(add_done, m + 1)
            act.activation(sq[:], x2[:, m], ACT.Square).then_inc(sq_done, 1)
        act.wait_ge(ss_done, 1)
        act.activation(sq[:], ps_ss[:], ACT.Sqrt, scale=1.0 / D, bias=g.eps[:]).then_inc(std_done, 1)
        for k in range(KD):
            act.wait_ge(xn_done, k + 1)
            if k >= 2:
                act.wait_ge(hl_done, k - 1)
            act.activation(hf[:, k % 2], hf[:, k % 2], ACT.Identity, scale=g.mod[:, 4 * KD + k:4 * KD + k + 1],
                           bias=g.mod[:, 3 * KD + k:3 * KD + k + 1]).then_inc(h_done, 1)
            act.wait_ge(h_done, k + 1)
            act.activation(g.h_hi[:, k], hf[:, k % 2], ACT.Copy).then_inc(hh_done, 1)

    @block.gpsimd
    def _(pool):
        def low(m):
            pool.wait_ge(hi_done, m + 1)
            pool.tensor_tensor(w_lo[:, m % 2].rearrange("p k n -> p (k n)"), raw[:, m % 2],
                               as_f32(w_hi[:, m % 2].rearrange("p k n -> p (k n)")), ALU.subtract).then_inc(lo_done, 1)

        pool.memset(total[:], 0.0).then_inc(add_done, 1)
        low(0)
        for m in range(KD):
            if m + 1 < KD:
                low(m + 1)
            pool.wait_ge(sq_done, m + 1)
            pool.wait_ge(add_done, m + 1)
            pool.tensor_tensor(total[:], total[:], sq[:], ALU.add).then_inc(add_done, 1)
        pool.wait_ge(rstd_done, 1)
        for k in range(KD):
            if k >= 2:
                pool.wait_ge(hl_done, k - 1)
            pool.tensor_tensor(hf[:, k % 2], x2[:, k], total[:], ALU.mult).then_inc(xn_done, 1)

    @block.vector
    def _(dve):
        for k in range(KD):
            dve.wait_ge(mh_done, k + 1)
            dve.tensor_tensor(lo[:, k], g.merged[:, k], as_f32(hi[:, k]), ALU.subtract).then_inc(ml_done, 1)
        for m in range(KD):
            dve.wait_ge(mm_done, m + 1)
            dve.wait_ge(ld_x[m], 16)
            dve.scalar_tensor_tensor(x2[:, m], ps[m % 2][:], g.mod[:, 2 * KD + m:2 * KD + m + 1], x2[:, m],
                                     ALU.mult, ALU.add).then_inc(x2_done, 1)
        dve.wait_ge(std_done, 1)
        dve.reciprocal(total[:], sq[:]).then_inc(rstd_done, 1)
        for k in range(KD):
            dve.wait_ge(hh_done, k + 1)
            dve.tensor_tensor(g.h_lo[:, k], hf[:, k % 2], as_f32(g.h_hi[:, k]), ALU.subtract).then_inc(hl_done, 1)

    @block.tensor
    def _(pe):
        for m in range(KD):
            s = m % 2
            pe.wait_ge(lo_done, m + 1)
            if m >= 2:
                pe.wait_ge(x2_done, m - 1)
            for k in range(KD):
                if m == 0:
                    pe.wait_ge(ml_done, k + 1)
                for i, (w, x) in enumerate(three(w_hi[:, s, k], w_lo[:, s, k], hi[:, k], lo[:, k])):
                    for t in range(2):
                        cols = slice(t * HALF, (t + 1) * HALF)
                        mm = pe.matmul(ps[s][:, cols], w, x[:, cols], start=k == 0 and i == 0,
                                       stop=k == KD - 1 and i == 2)
            mm.then_inc(mm_done, 1)
        pe.wait_ge(add_done, KD + 1)
        for t in range(2):
            cols = slice(t * HALF, (t + 1) * HALF)
            mm = pe.matmul(ps_ss[:, cols], g.const[:, C_ONES:C_ONES + P], total[:, cols], start=True, stop=True)
        mm.then_inc(ss_done, 1)

    ph.close()


def ffn_up(nc, g, d):
    ph = Scope(nc, "up")
    raw = ph.sb("raw", [P, 2, BLK])
    w_hi, w_lo = ph.sb("w_hi", [P, 2, KD, P], F32R), ph.sb("w_lo", [P, 2, KD, P], F32R)
    taps = ph.sb("taps", [P, 2, W_EXTRA])
    u = ph.sb("u", [P, 2, S])
    ps = [ph.ps(f"s{s}", [P, S]) for s in range(2)]
    ld = ph.sems("ld", 2)
    hi_done, lo_done, mm_done, scaled, conv, gate_done, y_done = (
        ph.sem(n) for n in ("hi_done", "lo_done", "mm_done", "scaled", "conv", "gate_done", "y_done"))
    block = ph.stack.enter_context(nc.Block())

    @block.sync
    def _(sp):
        def load(n, s):
            src = d["w_up"][n] if isinstance(n, int) else d["w_up"][bass.ds(n, 1)].rearrange("o p n -> p (o n)")
            sp.dma_start(raw[:, s], src).then_inc(ld[s], 16)

        load(0, 0)
        load(1, 1)
        with sp.Fori(0, KF - 1) as j:
            for s in range(2):
                sp.wait_ge(lo_done, 2 * j + s + 1)
                load(2 * j + s + 2, s)

    @block.scalar
    def _(act):
        def split(j, s, first=False):
            act.wait_ge(ld[s], 16 * j + 16)
            if not first:
                act.wait_ge(mm_done, 2 * j + s - 1)
            act.activation(w_hi[:, s], raw[:, s, 0:KD * P].rearrange("p (k m) -> p k m", k=KD), ACT.Copy)\
               .then_inc(hi_done, 1)

        def scale(j, s, first=False):
            act.wait_ge(mm_done, 2 * j + s + 1)
            if not first:
                act.wait_ge(y_done, j)
            act.activation(u[:, s], ps[s][:], ACT.Identity, scale=taps[:, s, 2:3], bias=taps[:, s, 3:4])\
               .then_inc(scaled, 1)

        def silu(j):
            act.wait_ge(conv, 4 * j + 2)
            act.activation(u[:, 0], u[:, 0], ACT.Silu).then_inc(gate_done, 1)

        split(0, 0, True)
        split(0, 1, True)
        scale(0, 0, True)
        split(1, 0)
        silu(0)
        scale(0, 1, True)
        with act.Fori(1, KF - 1) as j:
            split(j, 1)
            scale(j, 0)
            split(j + 1, 0)
            silu(j)
            scale(j, 1)
        split(KF - 1, 1)
        scale(KF - 1, 0)
        silu(KF - 1)
        scale(KF - 1, 1)

    @block.gpsimd
    def _(pool):
        def low(j, s, first=False):
            pool.wait_ge(hi_done, 2 * j + s + 1)
            if not first:
                pool.wait_ge(conv, 4 * (j - 1) + 2 * s + 2)
            pool.tensor_tensor(w_lo[:, s], raw[:, s, 0:KD * P].rearrange("p (k m) -> p k m", k=KD),
                               as_f32(w_hi[:, s]), ALU.subtract)
            pool.tensor_copy(taps[:, s], raw[:, s, KD * P:BLK]).then_inc(lo_done, 1)

        low(0, 0, True)
        low(0, 1, True)
        with pool.Fori(1, KF) as j:
            low(j, 0)
            low(j, 1)

    @block.vector
    def _(dve):
        with dve.Fori(0, KF) as j:
            for s in range(2):
                dve.wait_ge(scaled, 2 * j + s + 1)
                for back in (1, 2):
                    if back == 2:
                        dve.wait_ge(conv, 4 * j + 2 * s + 1)
                    dve.scalar_tensor_tensor(u[:, s, back:S], ps[s][:, 0:S - back], taps[:, s, 2 - back:3 - back],
                                             u[:, s, back:S], ALU.mult, ALU.add).then_inc(conv, 1)
            dve.wait_ge(conv, 4 * j + 4)
            dve.wait_ge(gate_done, j + 1)
            dve.tensor_tensor(g.y[:, bass.ds(j, 1)], u[:, 0:1], u[:, 1:2], ALU.mult).then_inc(y_done, 1)

    @block.tensor
    def _(pe):
        def product(j, s, first=False):
            pe.wait_ge(lo_done, 2 * j + s + 1)
            if not first:
                pe.wait_ge(conv, 4 * (j - 1) + 2 * s + 2)
            for k in range(KD):
                for i, (w, x) in enumerate(three(w_hi[:, s, k], w_lo[:, s, k], g.h_hi[:, k], g.h_lo[:, k])):
                    for t in range(2):
                        cols = slice(t * HALF, (t + 1) * HALF)
                        mm = pe.matmul(ps[s][:, cols], w, x[:, cols], start=k == 0 and i == 0,
                                       stop=k == KD - 1 and i == 2)
            mm.then_inc(mm_done, 1)

        product(0, 0, True)
        product(0, 1, True)
        with pe.Fori(1, KF) as j:
            product(j, 0)
            product(j, 1)

    ph.close()


def ffn_down(nc, g, d):
    ph = Scope(nc, "down")
    MB = 4
    W = MB * P
    raw = ph.sb("raw", [P, 2, W])
    w_hi, w_lo = ph.sb("w_hi", [P, 2, W], F32R), ph.sb("w_lo", [P, 2, W], F32R)
    y_hi, y_lo = ph.sb("y_hi", [P, 2, S], F32R), ph.sb("y_lo", [P, 2, S], F32R)
    x3 = ph.sb("x3", [P, KD, S])
    sq, total, rstd = ph.sb("sq", [P, S]), ph.sb("total", [P, S]), ph.sb("rstd", [P, S])
    ps = [ph.ps(f"m{m}", [P, S]) for m in range(MB)]
    ld, ld_x, st = ph.sems("ld", 2), ph.sem("ld_x"), ph.sem("st")
    wh_done, wl_done, yh_done, yl_done, mm_done, last_done, x3_done = (
        ph.sem(n) for n in ("wh_done", "wl_done", "yh_done", "yl_done", "mm_done", "last_done", "x3_done"))
    sq_done, add_done, ss_done, std_done, rstd_done, out_done = (
        ph.sem(n) for n in ("sq_done", "add_done", "ss_done", "std_done", "rstd_done", "out_done"))
    block = ph.stack.enter_context(nc.Block())
    STEPS = 2 * KF

    @block.sync
    def _(sp):
        w = d["w_down"].rearrange("g k p n -> (g k) p n")

        def load(n, s):
            src = w[n] if isinstance(n, int) else w[bass.ds(n, 1)].rearrange("o p n -> p (o n)")
            sp.dma_start(raw[:, s], src).then_inc(ld[s], 16)

        load(0, 0)
        load(1, 1)
        sp.dma_start(x3[:], d["x2"].rearrange("m p n -> p m n")).then_inc(ld_x, 16)
        with sp.Fori(0, KF - 1) as j:
            for s in range(2):
                sp.wait_ge(wl_done, 2 * j + s + 1)
                load(2 * j + s + 2, s)
        for m in range(KD):
            sp.wait_ge(out_done, m + 1)
            sp.dma_start(d["out"][m], x3[:, m]).then_inc(st, 16)
        sp.wait_ge(st, 16 * KD)

    @block.scalar
    def _(act):
        def split(n, s, y_n, read=None):
            act.wait_ge(ld[s], 8 * (n - s) + 16)
            if read:
                act.wait_ge(*read)
            act.activation(w_hi[:, s], raw[:, s], ACT.Copy).then_inc(wh_done, 1)
            act.activation(y_hi[:, s:s + 1], g.y[:, bass.ds(y_n, 1)], ACT.Copy).then_inc(yh_done, 1)

        def square(m):
            act.wait_ge(x3_done, m + 1)
            if m:
                act.wait_ge(add_done, m + 1)
            act.activation(sq[:], x3[:, m], ACT.Square).then_inc(sq_done, 1)

        split(0, 0, 0)
        split(1, 1, 1)
        with act.Fori(1, KF // 2) as j:
            for s in range(2):
                split(2 * j + s, s, 2 * j + s, (mm_done, 2 * j + s - 1))
        split(KF, 0, 0, (mm_done, KF - 1))
        split(KF + 1, 1, 1, (last_done, MB))
        with act.Fori(KF // 2 + 1, KF) as j:
            for s in range(2):
                split(2 * j + s, s, 2 * j + s - KF, (mm_done, 2 * j + s - 2))
        for m in range(KD):
            square(m)
        act.wait_ge(ss_done, 1)
        act.activation(sq[:], ps[0][:], ACT.Sqrt, scale=1.0 / D, bias=g.eps[:]).then_inc(std_done, 1)

    @block.gpsimd
    def _(pool):
        pool.memset(total[:], 0.0).then_inc(add_done, 1)
        with pool.Fori(0, KF) as j:
            for s in range(2):
                pool.wait_ge(wh_done, 2 * j + s + 1)
                pool.tensor_tensor(w_lo[:, s], raw[:, s], as_f32(w_hi[:, s]), ALU.subtract).then_inc(wl_done, 1)
        for m in range(KD):
            pool.wait_ge(sq_done, m + 1)
            pool.wait_ge(add_done, m + 1)
            pool.tensor_tensor(total[:], total[:], sq[:], ALU.add).then_inc(add_done, 1)

    @block.vector
    def _(dve):
        def low(n, s, y_n):
            dve.wait_ge(yh_done, n + 1)
            dve.tensor_tensor(y_lo[:, s:s + 1], g.y[:, bass.ds(y_n, 1)], as_f32(y_hi[:, s:s + 1]), ALU.subtract)\
               .then_inc(yl_done, 1)

        def residual(grp):
            for m in range(MB):
                n = grp * MB + m
                dve.wait_ge(last_done, n + 1)
                if n == 0:
                    dve.wait_ge(ld_x, 16)
                dve.scalar_tensor_tensor(x3[:, n], ps[m][:], g.mod[:, 5 * KD + n:5 * KD + n + 1], x3[:, n],
                                         ALU.mult, ALU.add).then_inc(x3_done, 1)

        with dve.Fori(0, KF // 2) as j:
            for s in range(2):
                low(2 * j + s, s, 2 * j + s)
        low(KF, 0, 0)
        residual(0)
        low(KF + 1, 1, 1)
        with dve.Fori(KF // 2 + 1, KF) as j:
            for s in range(2):
                low(2 * j + s, s, 2 * j + s - KF)
        residual(1)
        dve.wait_ge(std_done, 1)
        dve.reciprocal(rstd[:], sq[:]).then_inc(rstd_done, 1)
        dve.wait_ge(rstd_done, 1)
        for m in range(KD):
            dve.scalar_tensor_tensor(x3[:, m], x3[:, m], g.small["norms"][:, 2 * KD + m:2 * KD + m + 1], rstd[:],
                                     ALU.mult, ALU.mult).then_inc(out_done, 1)

    @block.tensor
    def _(pe):
        def step(n, s, grp, first=False, last=False):
            pe.wait_ge(wl_done, n + 1)
            pe.wait_ge(yl_done, n + 1)
            for m in range(MB):
                if first and grp:
                    pe.wait_ge(x3_done, m + 1)
                cut = slice(m * P, (m + 1) * P)
                for i, (w, x) in enumerate(three(w_hi[:, s, cut], w_lo[:, s, cut], y_hi[:, s], y_lo[:, s])):
                    for t in range(2):
                        cols = slice(t * HALF, (t + 1) * HALF)
                        mm = pe.matmul(ps[m][:, cols], w, x[:, cols], start=first and i == 0, stop=last and i == 2)
                if last:
                    mm.then_inc(last_done, 1)
                elif m == MB - 1:
                    mm.then_inc(mm_done, 1)

        for grp in range(2):
            n0 = grp * KF
            step(n0, 0, grp, first=True)
            step(n0 + 1, 1, grp)
            with pe.Fori(grp * KF // 2 + 1, (grp + 1) * KF // 2 - 1) as j:
                for s in range(2):
                    step(2 * j + s, s, grp)
            step(n0 + KF - 2, 0, grp)
            step(n0 + KF - 1, 1, grp, last=True)
        pe.wait_ge(add_done, KD + 1)
        for t in range(2):
            cols = slice(t * HALF, (t + 1) * HALF)
            mm = pe.matmul(ps[0][:, cols], g.const[:, C_ONES:C_ONES + P], total[:, cols], start=True, stop=True)
        mm.then_inc(ss_done, 1)

    ph.close()

SCRATCH = {"proj": (N_PROJ, P, S), "systems": (SOLVES, CHUNK, CHUNK), "solved": (SOLVES, CHUNK, CHUNK),
           "q_decayed": (HEADS // 2, P, S), "k_beta": (P, TILES, HEADS * DK), "k_rest": (P, TILES, HEADS * DK),
           "value": (P, TILES, HEADS * DV), "intra": (TILES, P, HEADS * P),
           "o_a": (HEADS // 2, P, S), "o_b": (HEADS, P, S), "x2": (KD, P, S), "out": (KD, P, S)}
OUT = ("out",)


def finish(r):
    return r["out"].reshape(D, S).T.reshape(1, S, D)


class Shared:
    pass


def build(nc, d):
    with ExitStack() as stack:
        sb = lambda name, shape, dt=F32: stack.enter_context(nc.sbuf_tensor(name, shape, dt))
        g = Shared()
        g.const = sb("const", [P, C_RESET])
        g.eps = sb("eps", [P, 1])
        g.c_act = sb("c_act", [P, KD])
        g.mod = sb("mod", [P, 6 * KD])
        g.small = {"b_ada": sb("b_ada", [P, 6 * KD]), "norms": sb("norms", [P, 3 * KD]),
                   "dn_norm": sb("dn_norm", [P, 1]), "dn_head": sb("dn_head", [HEADS, 2])}
        def hidden(scope, n):
            g.h_hi = scope.sb(f"{n}_hi", [P, KD, S], F32R)
            g.h_lo = scope.sb(f"{n}_lo", [P, KD, S], F32R)

        scope = Scope(nc, "h1")
        hidden(scope, "h1")
        project_a(nc, g, d)
        project_b(nc, g, d)
        scope.close()
        stick(nc, g, d)
        merged = Scope(nc, "merged")
        g.merged = merged.sb("merged", [P, KD, S])
        merge(nc, g, d)
        h2 = Scope(nc, "h2", side="right")
        hidden(h2, "h2")
        output(nc, g, d)
        merged.close()
        mlp = Scope(nc, "mlp")
        g.y = mlp.sb("y", [P, KF, S])
        ffn_up(nc, g, d)
        h2.close()
        ffn_down(nc, g, d)
        mlp.close()


def constants():
    import numpy as np

    t = np.zeros((P, C_END), np.float32)
    i, j = np.arange(P)[:, None], np.arange(P)[None]
    chunk = i // 64 == j // 64
    t[:, C_IDENT:C_IDENT + P] = i == j
    t[:, C_ONES:C_ONES + P] = 1
    t[:, C_ONES64:C_ONES64 + P] = chunk
    t[:, C_INCL:C_INCL + P] = chunk & (j >= i)
    t[:, C_STRICT:C_STRICT + P] = chunk & (i > j)
    for h in range(HEADS):
        t[h, C_SEL + h // 2 * P + h % 2 * 64:C_SEL + h // 2 * P + h % 2 * 64 + 64] = 1
    t[:, C_NEG:C_NEG + P] = np.where(j >= i, NEG, 0)
    t[:64, C_EVEN:C_EVEN + P] = 1
    t[64:, C_ODD:C_ODD + P] = 1
    t[:, C_RESET:C_RESET + S] = (np.arange(S) % 64 != 0)[None]
    return t


def kernel(x, c, w_ada, b_ada, norm1_w, w_in, dn_conv_w, dn_A_log, dn_dt_bias, dn_norm_w,
           w_proj_sb, w_proj_dn, w_out, norm2_w, w_ffn_in, ffn_conv_w, ffn_conv_b, w_ffn_out,
           final_norm_w):
    import numpy as np
    import concourse.bacc as bacc
    from concourse.bass_utils import run_bass_kernel_spmd

    def column(v):
        return np.asarray(v).reshape(-1, P).T

    def blocks(w, cols, extra=None, pad=0):
        out = []
        for b, c0 in enumerate(cols):
            part = w[:, c0:c0 + P].reshape(-1, P, P).transpose(1, 0, 2).reshape(P, -1)
            tail = np.zeros((P, pad), np.float32) if extra is None or extra[b] is None else extra[b]
            out.append(np.concatenate([part, tail], 1))
        return np.stack(out)

    sb, ab = 12 * P, 36 * P
    cols = [ab] + [sb + b * P for b in range(24)] + [b * P for b in range(12)] + [ab + 16 + b * P for b in range(16)]
    conv = np.asarray(dn_conv_w)[0].T.reshape(16, P, W_EXTRA)
    taps = [None] * B_DN + list(conv) + [None] * (N_PROJ - B_Z)
    ffn_cols, ffn_taps = [], []
    fcw = np.asarray(ffn_conv_w)[0].T.reshape(2 * KF, P, 3)
    fcb = np.asarray(ffn_conv_b)[0].reshape(2 * KF, P, 1)
    for b in range(KF):
        for half in range(2):
            ffn_cols.append((half * KF + b) * P)
            ffn_taps.append(np.concatenate([fcw[half * KF + b], fcb[half * KF + b]], 1))
    m_cols = [b * P for b in range(KD)]
    ins = {
        "xT": np.asarray(x)[0].T.reshape(KD, P, S),
        "c": column(c[0]),
        "w_ada": np.asarray(w_ada)[0].reshape(2, 4, P, 6, D).transpose(3, 0, 2, 1, 4),
        "b_ada": column(b_ada[0]),
        "norms": np.concatenate([column(norm1_w[0]), column(norm2_w[0]), column(final_norm_w)], 1),
        "w_in": blocks(np.asarray(w_in)[0], cols, taps, W_EXTRA),
        "dn_norm": np.asarray(dn_norm_w)[0].reshape(P, 1),
        "dn_head": np.stack([np.asarray(dn_A_log)[0], np.asarray(dn_dt_bias)[0]], 1),
        "w_merge": np.concatenate([blocks(np.asarray(w_proj_sb)[0], m_cols),
                                   blocks(np.asarray(w_proj_dn)[0], m_cols)], 2),
        "w_out": blocks(np.asarray(w_out)[0], m_cols),
        "w_up": blocks(np.asarray(w_ffn_in)[0], ffn_cols, ffn_taps, W_EXTRA),
        "w_down": np.asarray(w_ffn_out)[0].reshape(KF, P, 2, 4 * P).transpose(2, 0, 1, 3),
        "const": constants(),
    }
    ins = {k + "_dram": np.ascontiguousarray(v) for k, v in ins.items()}
    nc = bacc.Bacc("TRN2", target_bir_lowering=False, num_devices=1)
    d = {k[:-5]: nc.dram_tensor(k, v.shape, F32, kind="ExternalInput").ap() for k, v in ins.items()}
    d["reset"] = d["const"][0:HEADS, C_RESET:C_END]
    d["const"] = d["const"][:, 0:C_RESET]
    for name, shape in SCRATCH.items():
        d[name] = nc.dram_tensor(name + "_dram", shape, F32, kind="ExternalOutput" if name in OUT else "Internal").ap()
    build(nc, d)
    r = run_bass_kernel_spmd(nc, [ins], core_ids=[0])
    return finish({name: r.results[0][name + "_dram"] for name in OUT})
```

```python
import concourse.bass as bass
from concourse import mybir
from contextlib import ExitStack

F32 = mybir.dt.float32
F32R = mybir.dt.float32r
BF16 = mybir.dt.bfloat16
ALU = mybir.AluOpType
ACT = mybir.ActivationFunctionType
AX = mybir.AxisListType

P = 128
D = 1024
S = 1024
KD = D // P
HALF = 512
EPS = 1e-6
HEADS = 8
N_PROJ = 53
B_DN, B_Z, B_SB, B_GATE = 1, 17, 25, 37
DOWN = 4
W_EXTRA = 4
BLK = KD * P + W_EXTRA
D_FF = 2816
KF = D_FF // P
NEG = -1e30

C_IDENT, C_ONES, C_ONES64, C_INCL, C_STRICT, C_SEL = 0, 128, 256, 384, 512, 640
C_NEG = 640 + 512
C_EVEN, C_ODD = C_NEG + 128, C_NEG + 256
C_RESET = C_NEG + 384
C_END = C_RESET + 1024


def three(hi_w, lo_w, hi_x, lo_x):
    return ((hi_w, hi_x), (hi_w, lo_x), (lo_w, hi_x))


def as_f32(ap):
    return ap.bitcast(F32)


class Scope:

    def __init__(self, nc, name, side="left"):
        self.nc, self.name, self.side, self.stack = nc, name, side, ExitStack()
        self.signals = []

    def sb(self, name, shape, dt=F32):
        return self.stack.enter_context(self.nc.sbuf_tensor(f"{self.name}_{name}", shape, dt, side=self.side))

    def ps(self, name, shape, dt=F32):
        return self.stack.enter_context(self.nc.psum_tensor(f"{self.name}_ps_{name}", shape, dt))

    def sem(self, name):
        signal = self.stack.enter_context(self.nc.semaphore(f"{self.name}_{name}"))
        self.signals.append(signal)
        return signal

    def sems(self, name, n):
        return [self.sem(f"{name}{i}") for i in range(n)]

    def close(self):
        self.stack.close()
        for signal in self.signals:
            self.nc.sync.sem_clear(signal)


def project_a(nc, g, d):
    ph = Scope(nc, "pa")
    PIECE = 4
    xT = ph.sb("xT", [P, KD, S])
    wa, acc = ph.sb("wa", [P, 2, PIECE, D]), ph.sb("acc", [P, 2, D])
    sq, std, rstd = ph.sb("sq", [P, 2, S]), ph.sb("std", [P, S]), ph.sb("rstd", [P, S])
    hf = ph.sb("hf", [P, 2, S])
    c_in = ph.sb("c_in", [P, KD])
    raw = ph.sb("raw", [P, 2, BLK])
    w_hi = ph.sb("w_hi", [P, 2, KD, P], F32R)
    w_lo = ph.sb("w_lo", [P, 2, KD, P], F32R)
    taps = ph.sb("taps", [P, 2, W_EXTRA])
    stage = ph.sb("stage", [P, 2, S])
    ps = [ph.ps(f"s{i}", [P, S]) for i in range(2)]
    ps_ss, ps_mod = ph.ps("ss", [P, S]), ph.ps("mod", [P, 3 * KD])
    ld_small, ld_c, ld_x, ld_a = ph.sem("ld_small"), ph.sem("ld_c"), ph.sems("ld_x", KD), ph.sems("ld_a", 2)
    ld_ones, ld_const, ld_last = ph.sem("ld_ones"), ph.sem("ld_const"), ph.sems("ld_last", PIECE)
    ld, st = ph.sems("ld", 2), ph.sems("st", 2)
    c_done, acc_free, acc_done, eps_set = (ph.sem(n) for n in ("c_done", "acc_free", "acc_done", "eps_set"))
    sq_done, ss_done, std_done, rstd_done = (ph.sem(n) for n in ("sq_done", "ss_done", "std_done", "rstd_done"))
    mod_done, step, xn_done = (ph.sem(n) for n in ("mod_done", "step", "xn_done"))
    hf_done, hh_done, hl_dve, hl_pool = (ph.sem(n) for n in ("hf_done", "hh_done", "hl_dve", "hl_pool"))
    hi_done, lo_done, mm_done, out_done = (ph.sem(n) for n in ("hi_done", "lo_done", "mm_done", "out_done"))
    scaled, conv = ph.sem("scaled"), ph.sem("conv")
    block = ph.stack.enter_context(nc.Block())
    N = B_Z
    PEEL = 9

    def at(tensor, n):
        return tensor[n] if isinstance(n, int) else tensor[bass.ds(n, 1)].rearrange("o p n -> p (o n)")


    @block.sync
    def _(sp):
        def load_piece(n):
            if n >= 2:
                sp.wait_ge(acc_free, n - 1)
            sp.dma_start(wa[:, n % 2], d["w_ada"][n // 2, n % 2]).then_inc(ld_a[n % 2], 16)

        def block_io(j, s, load=True):
            n = 2 * j + s
            if load:
                sp.wait_ge(lo_done, n + 1)
                sp.dma_start(raw[:, s], at(d["w_in"], n + 2)).then_inc(ld[s], 16)
            sp.wait_ge(out_done, n + 1)
            sp.dma_start(at(d["proj"], n), stage[:, s]).then_inc(st[s], 16)

        sp.dma_start(c_in[:], d["c"]).then_inc(ld_c, 16)
        ones_cols = slice(C_ONES, C_ONES + P)
        sp.dma_start(g.const[:, ones_cols], d["const"][:, ones_cols]).then_inc(ld_ones, 16)
        for name in ("b_ada", "norms", "dn_norm", "dn_head"):
            sp.dma_start(g.small[name][:], d[name]).then_inc(ld_small, 16)
        for k in range(KD):
            sp.dma_start(xT[:, k, :], d["xT"][k]).then_inc(ld_x[k], 16)
        for n in range(3):
            load_piece(n)
        sp.wait_ge(acc_free, 2)
        for k in range(PIECE):
            sp.dma_start(wa[:, 1, k], d["w_ada"][1, 1][:, k]).then_inc(ld_last[k], 16)
        for s in range(2):
            sp.dma_start(raw[:, s], d["w_in"][s]).then_inc(ld[s], 16)
        for cols in (slice(0, C_ONES), slice(C_ONES + P, C_RESET)):
            sp.dma_start(g.const[:, cols], d["const"][:, cols]).then_inc(ld_const, 16)
        for n in range(PEEL + 1):
            block_io(n // 2, n % 2)
            if n in (0, 4):
                load_piece(4 + n // 4)
        with sp.Fori((PEEL + 1) // 2, N // 2 - 1) as j:
            for s in range(2):
                block_io(j, s)
        block_io(N // 2 - 1, 0)
        block_io(N // 2 - 1, 1, load=False)
        block_io(N // 2, 0, load=False)
        for s in range(2):
            sp.dma_start(g.next_raw[:, s], d["w_in"][B_Z + s][:, 0:KD * P]).then_inc(g.next_ld[s], 16)
        sp.wait_ge(ld_const, 32)
        sp.wait_ge(st[0], 16 * (N // 2 + 1))
        sp.wait_ge(st[1], 16 * (N // 2))

    @block.scalar
    def _(act):
        def split(j, s):
            n = 2 * j + s
            act.wait_ge(ld[s], 16 * (j + 1))
            if not (isinstance(n, int) and n < 2):
                act.wait_ge(mm_done, n - 1)
            act.activation(w_hi[:, s], raw[:, s, 0:KD * P].rearrange("p (k m) -> p k m", k=KD), ACT.Copy)\
               .then_inc(hi_done, 1)

        def evacuate(j, s):
            n = 2 * j + s
            act.wait_ge(mm_done, n + 1)
            if not (isinstance(n, int) and n < 2):
                act.wait_ge(st[s], 16 * j)
            act.activation(stage[:, s], ps[s][:], ACT.Copy, scale=taps[:, s, 3:4]).then_inc(scaled, 1)
            act.wait_ge(conv, 3 * n)
            act.activation(stage[:, s], stage[:, s], ACT.Silu).then_inc(out_done, 1)

        act.wait_ge(ld_c, 16)
        act.activation(g.c_act[:], c_in[:], ACT.Silu).then_inc(c_done, 1)
        for k in range(KD):
            act.wait_ge(ld_x[k], 16)
            if k >= 2:
                act.wait_ge(ss_done, k - 1)
            act.activation(sq[:, k % 2], xT[:, k], ACT.Square).then_inc(sq_done, 1)
        act.wait_ge(ss_done, KD)
        act.wait_ge(eps_set, 1)
        act.activation(std[:], ps_ss[:], ACT.Sqrt, scale=1.0 / D, bias=g.eps[:]).then_inc(std_done, 1)
        split(0, 0)
        split(0, 1)
        act.wait_ge(step, 2)
        for k in range(KD):
            act.wait_ge(xn_done, k + 1)
            act.activation(g.h_hi[:, k], xT[:, k], ACT.Identity, scale=g.mod[:, KD + k:KD + k + 1],
                           bias=g.mod[:, k:k + 1]).then_inc(hh_done, 1)
        act.wait_ge(mm_done, 1)
        act.activation(stage[:, 0], ps[0][:], ACT.Copy).then_inc(out_done, 1)
        split(1, 0)
        evacuate(0, 1)
        with act.Fori(1, N // 2) as j:
            split(j, 1)
            evacuate(j, 0)
            split(j + 1, 0)
            evacuate(j, 1)
        evacuate(N // 2, 0)

    @block.gpsimd
    def _(pool):
        def low(j, s):
            n = 2 * j + s
            pool.wait_ge(hi_done, n + 1)
            if not (isinstance(n, int) and n < 2):
                pool.wait_ge(out_done, n - 1)
            pool.tensor_tensor(w_lo[:, s], raw[:, s, 0:KD * P].rearrange("p (k m) -> p k m", k=KD),
                               as_f32(w_hi[:, s]), ALU.subtract)
            pool.tensor_copy(taps[:, s], raw[:, s, KD * P:BLK]).then_inc(lo_done, 1)

        pool.memset(g.eps[:], EPS).then_inc(eps_set, 1)
        pool.wait_ge(rstd_done, 1)
        for k in range(KD):
            pool.tensor_tensor(xT[:, k], xT[:, k], rstd[:], ALU.mult).then_inc(xn_done, 1)
        low(0, 0)
        for k in range(1, KD, 2):
            pool.wait_ge(hh_done, k + 1)
            pool.wait_ge(hf_done, k + 1)
            pool.tensor_tensor(g.h_lo[:, k], hf[:, 1], as_f32(g.h_hi[:, k]), ALU.subtract).then_inc(hl_pool, 1)
        low(0, 1)
        with pool.Fori(1, N // 2) as j:
            for s in range(2):
                low(j, s)
        low(N // 2, 0)

    @block.vector
    def _(dve):
        def condition(grp, k):
            n = 2 * grp + k // PIECE
            dst, c_k = acc[:, grp % 2], g.c_act[:, k:k + 1]
            if n == 3:
                dve.wait_ge(ld_last[k - PIECE], 16)
            elif k % PIECE == 0:
                dve.wait_ge(ld_a[n % 2], 16 * (n // 2 + (n < 4 or n % 2 == 0)))
            if k == 0:
                if grp == 2:
                    dve.wait_ge(mod_done, 1)
                ins = dve.tensor_scalar(dst, wa[:, 0, 0], c_k, None, ALU.mult)
            else:
                dve.wait_ge(acc_done, grp * KD + k)
                ins = dve.scalar_tensor_tensor(dst, wa[:, n % 2, k % PIECE], c_k, dst, ALU.mult, ALU.add)
            ins.then_inc(acc_done, 1)
            if k % PIECE == PIECE - 1:
                dve.wait_ge(acc_done, PIECE * n + PIECE)
                dve.sem_inc(acc_free, 1)

        def convolve(n, s):
            dve.wait_ge(scaled, n)
            for back in (1, 2, 3):
                if back > 1:
                    dve.wait_ge(conv, 3 * (n - 1) + back - 1)
                dve.scalar_tensor_tensor(stage[:, s, back:S], ps[s][:, 0:S - back], taps[:, s, 3 - back:4 - back],
                                         stage[:, s, back:S], ALU.mult, ALU.add).then_inc(conv, 1)

        dve.wait_ge(c_done, 1)
        for k in range(PIECE):
            condition(0, k)
        dve.wait_ge(std_done, 1)
        dve.reciprocal(rstd[:], std[:]).then_inc(rstd_done, 1)
        for k in range(PIECE, KD):
            condition(0, k)
        for k in range(KD):
            condition(1, k)
        dve.wait_ge(ld_small, 16 * 4)
        dve.wait_ge(mod_done, 2)
        dve.tensor_tensor(g.mod[:, 0:2 * KD], ps_mod[:, 0:2 * KD], g.small["b_ada"][:, 0:2 * KD], ALU.add)\
           .then_inc(step, 1)
        dve.wait_ge(step, 1)
        dve.scalar_tensor_tensor(g.mod[:, KD:2 * KD], g.mod[:, KD:2 * KD], 1.0, g.small["norms"][:, 0:KD],
                                 ALU.add, ALU.mult).then_inc(step, 1)
        dve.wait_ge(step, 2)
        for k in range(KD):
            dve.wait_ge(xn_done, k + 1)
            if k >= 2:
                dve.wait_ge((hl_dve, hl_pool)[k % 2], k // 2)
            dve.tensor_scalar(hf[:, k % 2], xT[:, k], g.mod[:, KD + k:KD + k + 1], g.mod[:, k:k + 1],
                              ALU.mult, ALU.add).then_inc(hf_done, 1)
            if k % 2 == 0:
                dve.wait_ge(hh_done, k + 1)
                dve.wait_ge(hf_done, k + 1)
                dve.tensor_tensor(g.h_lo[:, k], hf[:, 0], as_f32(g.h_hi[:, k]), ALU.subtract).then_inc(hl_dve, 1)
        for n in range(1, PEEL):
            convolve(n, n % 2)
            condition(2, n - 1)
        with dve.Fori(PEEL // 2, N // 2) as j:
            for s in (1, 2):
                convolve(2 * j + s, s % 2)
        dve.wait_ge(mod_done, 3)
        dve.tensor_tensor(g.mod[:, 2 * KD:3 * KD], ps_mod[:, 2 * KD:3 * KD], g.small["b_ada"][:, 2 * KD:3 * KD], ALU.add)\
           .then_inc(step, 1)

    @block.tensor
    def _(pe):
        ones = g.const[:, C_ONES:C_ONES + P]

        def product(n, s, first=False):
            pe.wait_ge(lo_done, n + 1)
            if not first:
                pe.wait_ge(out_done, n - 1)
            for k in range(KD):
                if isinstance(n, int) and n == 0:
                    pe.wait_ge((hl_dve, hl_pool)[k % 2], k // 2 + 1)
                hi, lo = w_hi[:, s, k], w_lo[:, s, k]
                for i, (w, x) in enumerate(three(hi, lo, g.h_hi[:, k], g.h_lo[:, k])):
                    for t in range(2):
                        mm = pe.matmul(ps[s][:, t * HALF:(t + 1) * HALF], w, x[:, t * HALF:(t + 1) * HALF],
                                       start=k == 0 and i == 0, stop=k == KD - 1 and i == 2)
            mm.then_inc(mm_done, 1)

        def columns(grp):
            pe.wait_ge(acc_done, KD * (grp + 1))
            for m in range(KD):
                mm = pe.matmul(ps_mod[:, grp * KD + m:grp * KD + m + 1], acc[:, grp % 2, m * P:(m + 1) * P],
                               ones[:, 0:1], start=True, stop=True)
            mm.then_inc(mod_done, 1)

        pe.wait_ge(ld_ones, 16)
        for k in range(KD):
            pe.wait_ge(sq_done, k + 1)
            for t in range(2):
                mm = pe.matmul(ps_ss[:, t * HALF:(t + 1) * HALF], ones, sq[:, k % 2, t * HALF:(t + 1) * HALF],
                               start=k == 0, stop=k == KD - 1)
            mm.then_inc(ss_done, 1)
        columns(0)
        columns(1)
        for n in range(PEEL):
            product(n, n % 2, first=n < 2)
        product(PEEL, PEEL % 2)
        product(PEEL + 1, (PEEL + 1) % 2)
        columns(2)
        with pe.Fori(PEEL // 2 + 1, N // 2) as j:
            for s in (1, 2):
                product(2 * j + s, s % 2)

    ph.close()


def stick(nc, g, d):
    ph = Scope(nc, "stick")
    PAIRS, TILES, UNITS = HEADS // 2, S // P, 16
    ALL = PAIRS * UNITS
    AHEAD, SLOTS = 3, 3
    q_raw, k_raw = ph.sb("q_raw", [P, 2, S]), ph.sb("k_raw", [P, 2, S])
    v_raw = ph.sb("v_raw", [P, S])
    q_both = ph.sb("q_both", [P, 2, 2, S], F32R)
    k_hi, k_lo = ph.sb("k_hi", [P, 2, 2, S], F32R), ph.sb("k_lo", [P, 2, 2, S], F32R)
    v_hi, v_lo = (ph.sb(n, [P, 2, TILES, 2, P], F32R) for n in ("v_hi", "v_lo"))
    a_hi, a_lo = (ph.sb(n, [P, 2, TILES, HALF], F32R) for n in ("a_hi", "a_lo"))
    beta = ph.sb("beta", [P, SLOTS, S])
    rest = ph.sb("rest", [P, SLOTS, S + 1])
    o_out = ph.sb("o_out", [P, 2, HALF])
    ident_b, mask_b = ph.sb("ident_b", [P, P], BF16), ph.sb("mask_b", [P, P], BF16)
    ps_z = [ph.ps(f"z{i}", [P, S]) for i in range(2)]
    ps_t = [ph.ps(f"t{i}", [P, 4, P]) for i in range(2)]
    ps_o = [ph.ps(f"o{i}", [P, HALF]) for i in range(2)]
    ld_qk, ld_v, st = ph.sems("ld_qk", 2), ph.sem("ld_v"), ph.sems("st", 2)
    setup, high_done, low_done, bf_done = (ph.sem(n) for n in ("setup", "high_done", "low_done", "bf_done"))
    z_done, rest_done, beta_done, scan_done, w_done = (ph.sem(n) for n in ("z_done", "rest_done", "beta_done", "scan_done", "w_done"))
    t_done, hi_done, lo_done, av_done, o_done = (ph.sem(n) for n in ("t_done", "hi_done", "lo_done", "av_done", "o_done"))
    block = ph.stack.enter_context(nc.Block())
    SCALE = 64 ** -0.5
    ident = g.const[:, C_IDENT:C_IDENT + P]

    def where(n):
        u = n % UNITS
        return u // 8, u // 4 % 2, 4 * (u // 8) + u % 4

    def start(n):
        return S - (where(n)[2] + 1) * P

    V_UNIT = (4, 5)
    QK_UNIT = 2
    groups = []
    for n in range(ALL):
        groups += [("a", n, j0) for j0 in range(0, where(n)[2] + 1, 4)]
        if n < 2:
            groups.append(("v", 0, n))
        if n % UNITS in V_UNIT and n // UNITS + 1 < PAIRS:
            groups.append(("v", n // UNITS + 1, V_UNIT.index(n % UNITS)))
    group_no = {key: i for i, key in enumerate(groups)}

    def last_group(n):
        return max(i for i, key in enumerate(groups) if key[0] == "a" and key[1] == n)

    def group_tiles(n):
        last = where(n)[2]
        return [(group_no["a", n, j0], j0, min(4, last + 1 - j0)) for j0 in range(0, last + 1, 4)]

    @block.sync
    def _(sp):
        def load(p):
            for h in range(2):
                for raw, b in ((q_raw, B_SB + p), (k_raw, B_SB + PAIRS + p)):
                    for copy in range(2):
                        sp.dma_start(raw[copy * 64:copy * 64 + 64, h], d["proj"][b][h * 64:h * 64 + 64])\
                          .then_inc(ld_qk[h], 16)
                if h == 0:
                    sp.dma_start(v_raw[:], d["proj"][B_SB + 2 * PAIRS + p]).then_inc(ld_v, 16)

        def load_next(p):
            sp.wait_ge(low_done, 4 * p + 4)
            sp.wait_ge(t_done, group_no["v", p, 1] + 1)
            load(p + 1)

        load(0)
        load_next(0)
        for p in range(PAIRS):
            if p + 2 < PAIRS:
                load_next(p + 1)
            for half in range(2):
                sp.wait_ge(o_done, 2 * p + half + 1)
                cols = slice(half * HALF, half * HALF + HALF)
                sp.dma_start(d["o_a"][p][:, cols], o_out[:, half]).then_inc(st[half], 16)
        sp.dma_start(g.merge_raw[:], d["w_merge"][0]).then_inc(g.merge_ld, 16)
        for half in range(2):
            sp.wait_ge(st[half], 16 * PAIRS)

    @block.scalar
    def _(act):
        def split_qk(p, heads=(0, 1)):
            if p >= 2:
                act.wait_ge(z_done, UNITS * (p - 1))
            for h in heads:
                act.wait_ge(ld_qk[h], 64 * p + 64)
                act.activation(q_both[:, p % 2, h], q_raw[:, h], ACT.Copy).then_inc(high_done, 1)
                act.activation(k_hi[:, p % 2, h], k_raw[:, h], ACT.Copy).then_inc(high_done, 1)

        def split_v(p, i):
            n = group_no["v", p, i]
            act.wait_ge(t_done, n + 1)
            act.wait_ge(setup, 2 if p == 0 else 5)
            if p >= 2:
                act.wait_ge(av_done, 4 * (p - 1))
            for h in range(2):
                cols = slice(h * 64, h * 64 + 64)
                ins = act.activation(v_hi[:, p % 2, 4 * i:4 * i + 4, h, cols], ps_t[n % 2][:, :, cols], ACT.Copy)
            ins.then_inc(hi_done, 1)

        def sigmoids(n):
            s, o = n % SLOTS, start(n)
            act.wait_ge(z_done, n + 1)
            if n >= SLOTS:
                act.wait_ge(t_done, last_group(n - SLOTS) + 1)
            z = ps_z[n % 2][:, 0:S - o]
            act.activation(rest[:, s, o:S], z, ACT.Sigmoid, scale=-SCALE).then_inc(rest_done, 1)
            act.activation(beta[:, s, o:S], z, ACT.Sigmoid, scale=SCALE).then_inc(beta_done, 1)

        def high(n):
            h, t0 = where(n)[1], n % 4 * P
            if n % 4 == 0 and n >= 8:
                act.wait_ge(av_done, n // 4 - 1)
            for no, j0, w in group_tiles(n):
                act.wait_ge(t_done, no + 1)
                act.activation(a_hi[:, h, j0:j0 + w, t0:t0 + P], ps_t[no % 2][:, 0:w], ACT.Copy).then_inc(hi_done, 1)

        def out(p, half):
            act.wait_ge(av_done, 4 * p + 2 * half + 2)
            if p:
                act.wait_ge(st[half], 16 * p)
            act.activation(o_out[:, half], ps_o[half][:], ACT.Copy).then_inc(o_done, 1)

        split_qk(0, (0,))
        for n in range(AHEAD):
            sigmoids(n)
            if n == 0:
                split_qk(0, (1,))
        for n in range(ALL):
            p, u = n // UNITS, n % UNITS
            high(n)
            if n + AHEAD < ALL:
                sigmoids(n + AHEAD)
            if n < 2:
                split_v(0, n)
            if u in V_UNIT and p + 1 < PAIRS:
                split_v(p + 1, V_UNIT.index(u))
            if u == QK_UNIT and p + 1 < PAIRS:
                split_qk(p + 1)
            if u == 10:
                out(p, 0)
            if u == 1 and p:
                out(p - 1, 1)
        out(PAIRS - 1, 1)

    @block.gpsimd
    def _(pool):
        pool.memset(as_f32(v_hi[:, 0]), 0.0).then_inc(setup, 1)
        pool.memset(as_f32(v_lo[:, 0]), 0.0).then_inc(setup, 1)
        pool.memset(rest[:, :, S:S + 1], 1.0).then_inc(setup, 1)
        for n in range(ALL):
            s, o = n % SLOTS, start(n)
            pool.wait_ge(beta_done, n + 1)
            pool.wait_ge(scan_done, n + 1)
            if n < 1:
                pool.wait_ge(setup, 3)
            pool.tensor_tensor(beta[:, s, o:S], beta[:, s, o:S], rest[:, s, o + 1:S + 1], ALU.mult)\
                .then_inc(w_done, 1)
            if n == 0:
                pool.memset(as_f32(v_hi[:, 1]), 0.0).then_inc(setup, 1)
            if n == 1:
                pool.memset(as_f32(v_lo[:, 1]), 0.0).then_inc(setup, 1)

    @block.vector
    def _(dve):
        def low_qk(p, heads=(0, 1)):
            for h in heads:
                dve.wait_ge(high_done, 4 * p + 2 * h + 1)
                dve.tensor_tensor(q_both[64:P, p % 2, h], q_raw[64:P, h], as_f32(q_both[64:P, p % 2, h]), ALU.subtract)\
                   .then_inc(low_done, 1)
                dve.wait_ge(high_done, 4 * p + 2 * h + 2)
                dve.tensor_tensor(k_lo[:, p % 2, h], k_raw[:, h], as_f32(k_hi[:, p % 2, h]), ALU.subtract)\
                   .then_inc(low_done, 1)

        def low_v(p, i):
            n = group_no["v", p, i]
            dve.wait_ge(hi_done, n + 1)
            for h in range(2):
                cols = slice(h * 64, h * 64 + 64)
                ins = dve.tensor_tensor(v_lo[:, p % 2, 4 * i:4 * i + 4, h, cols], ps_t[n % 2][:, :, cols],
                                        as_f32(v_hi[:, p % 2, 4 * i:4 * i + 4, h, cols]), ALU.subtract)
            ins.then_inc(lo_done, 1)

        def scan(n):
            s, o = n % SLOTS, start(n)
            dve.wait_ge(rest_done, n + 1)
            factor = rest[:, s, o:S][:, ::-1]
            dve.tensor_tensor_scan(factor, factor, factor, 1.0, ALU.mult, ALU.bypass)\
               .then_inc(scan_done, 1)

        def low(n):
            h, t0 = where(n)[1], n % 4 * P
            for no, j0, w in group_tiles(n):
                dve.wait_ge(hi_done, no + 1)
                dve.tensor_tensor(a_lo[:, h, j0:j0 + w, t0:t0 + P], ps_t[no % 2][:, 0:w],
                                  as_f32(a_hi[:, h, j0:j0 + w, t0:t0 + P]), ALU.subtract).then_inc(lo_done, 1)

        dve.tensor_copy(ident_b[:], ident).then_inc(bf_done, 1)
        dve.tensor_copy(mask_b[:], g.const[:, C_NEG:C_NEG + P]).then_inc(bf_done, 1)
        low_qk(0, (0,))
        for n in range(AHEAD):
            scan(n)
            if n == 0:
                low_qk(0, (1,))
        for n in range(ALL):
            p, u = n // UNITS, n % UNITS
            low(n)
            if n + AHEAD < ALL:
                scan(n + AHEAD)
            if n < 2:
                low_v(0, n)
            if u in V_UNIT and p + 1 < PAIRS:
                low_v(p + 1, V_UNIT.index(u))
            if u == QK_UNIT and p + 1 < PAIRS:
                low_qk(p + 1)

    @block.tensor
    def _(pe):
        def transposes_v(p, i):
            n = group_no["v", p, i]
            pe.wait_ge(ld_v, 16 * p + 16)
            if n >= 2:
                pe.wait_ge(lo_done, n - 1)
            for j in range(4):
                mm = pe.transpose(ps_t[n % 2][:, j], v_raw[:, (4 * i + j) * P:(4 * i + j) * P + P], ident)
            mm.then_inc(t_done, 1)

        def logits(n):
            (_, h, i), s, pair = where(n), n % 2, n // UNITS
            if n % UNITS in (0, 4):
                pe.wait_ge(low_done, 4 * pair + 2 * h + 2)
            if n >= 2:
                pe.wait_ge(beta_done, n - 1)
            w = (i + 1) * P
            q_t = q_both[:, pair % 2, h, i * P:i * P + P]
            for c0 in range(0, w, HALF):
                c1 = min(w, c0 + HALF)
                pe.matmul(ps_z[s][:, c0:c1], q_t, k_hi[:, pair % 2, h, c0:c1], start=True, stop=False)
                mm = pe.matmul(ps_z[s][:, c0:c1], q_t, k_lo[:, pair % 2, h, c0:c1], start=False, stop=c1 < w)
            mm = pe.matmul(ps_z[s][:, w - P:w], ident_b[:], mask_b[:], start=False, stop=True)
            mm.then_inc(z_done, 1)

        def transposes(n):
            s, o = n % SLOTS, start(n)
            pe.wait_ge(w_done, n + 1)
            for no, j0, w in group_tiles(n):
                if no >= 2:
                    pe.wait_ge(lo_done, no - 1)
                for j in range(j0, j0 + w):
                    mm = pe.transpose(ps_t[no % 2][:, j - j0], beta[:, s, o + j * P:o + j * P + P], ident)
                mm.then_inc(t_done, 1)

        def values(a):
            half, h, _ = where(4 * a)
            pair = a // 4
            pe.wait_ge(lo_done, last_group(4 * a + 3) + 1)
            if h == 0 and pair:
                pe.wait_ge(o_done, 2 * (pair - 1) + half + 1)
            last = 4 * half + 3
            for j in range(last + 1):
                t0 = max(0, j - 4 * half) * P
                v = v_hi[:, pair % 2, j, h], v_lo[:, pair % 2, j, h]
                for i, (w, x) in enumerate(three(*v, a_hi[:, h, j, t0:HALF], a_lo[:, h, j, t0:HALF])):
                    mm = pe.matmul(ps_o[half][:, t0:HALF], w, x, start=h == 0 and j == 0 and i == 0,
                                   stop=h == 1 and j == last and i == 2)
            mm.then_inc(av_done, 1)

        pe.wait_ge(bf_done, 2)
        for n in range(AHEAD):
            logits(n)
        for n in range(ALL):
            p, u = n // UNITS, n % UNITS
            transposes(n)
            if n + AHEAD < ALL:
                logits(n + AHEAD)
            if n < 2:
                transposes_v(0, n)
            if u in V_UNIT and p + 1 < PAIRS:
                transposes_v(p + 1, V_UNIT.index(u))
            if u % 4 == 0 and n:
                values(n // 4 - 1)
        values(ALL // 4 - 1)

    ph.close()


CHUNK = 64
TILES = S // P
DK, DV = 64, 128
SOLVES = HEADS * S // CHUNK
NQK = 8
SLICES = 2 * KD


def schedule():
    order, ticks = [], iter([(n, q) for n in range(N_PROJ - B_Z) for q in range(SLICES)])

    def dense(count):
        for _, (n, q) in zip(range(count), ticks):
            order.append(("dense", n, q))

    def side(kind, *index):
        order.append((kind, *index))

    dense(2)
    for i, count in enumerate((6, 8, 6, 8, 6, 4)):
        side("decay", i)
        dense(count)
    side("square", 0)
    side("square", 1)
    for n in range(NQK):
        before, between, behind = (3, 4, 5) if n % 2 == 0 else (5, 8, 3)
        side("norm", n)
        dense(before)
        if n:
            side("ship", n - 1)
            if n + 1 < NQK:
                side("square", n + 1)
        side("value", n)
        dense(between)
        side("turn", n)
        dense(behind)
    side("ship", NQK - 1)
    for t in range(TILES):
        side("diff", t)
        dense(4)
        if t:
            side("ship_tile", t - 1)
        side("weights", t)
        side("ada", t)
        dense(5)
    side("ship_tile", TILES - 1)
    dense(1)
    side("solve")
    dense(16)
    side("preload", 0)
    dense(16)
    side("preload", 1)
    dense(SOLVE_TICKS - 32)
    for j in range(LATE, CHUNK - 1):
        side("solve_late", j)
        dense(3)
    side("solved")
    dense(8)
    side("mod", 0)
    dense(8)
    side("u", 0, 0)
    dense(2)
    side("u", 0, 1)
    dense(2)
    side("w", 0)
    dense(2)
    for t in range(TILES):
        side("read", 2 * t)
        dense(2)
        side("write", 2 * t)
        side("ada", KD + 2 * t)
        dense(2)
        if t:
            side("root", t - 1)
        dense(2)
        if t:
            side("std", t - 1)
        dense(1)
        side("read", 2 * t + 1)
        if t:
            side("scale", t - 1)
        dense(2)
        side("write", 2 * t + 1)
        side("ada", KD + 2 * t + 1)
        dense(1)
        if t + 2 < TILES:
            side("load", t + 2)
        if t:
            side("out", t - 1, 0)
            dense(1)
            side("out", t - 1, 1)
            dense(1)
            side("ship_out", t - 1)
        if t + 1 < TILES:
            for step in (("u", t + 1, 0), ("u", t + 1, 1), ("w", t + 1)):
                side(*step)
                dense(2)
        if t == TILES // 2 - 1:
            side("mod", 1)
            dense(1)
    dense(2)
    side("root", TILES - 1)
    dense(2)
    side("std", TILES - 1)
    dense(3)
    side("mod", 2)
    side("scale", TILES - 1)
    dense(8)
    side("out", TILES - 1, 0)
    dense(2)
    side("out", TILES - 1, 1)
    dense(2)
    side("ship_out", TILES - 1)
    dense(1 << 20)
    return order


SOLVE_TICKS = 58
LATE = 26


def project_b(nc, g, d):
    ph = Scope(nc, "pb")
    BLOCKS = N_PROJ - B_Z
    ORDER = schedule()
    TH = TILES * HEADS
    raw, ld = g.next_raw, g.next_ld
    w_hi = ph.sb("w_hi", [P, 2, KD, P], F32R)
    w_lo = ph.sb("w_lo", [P, 2, KD, P], F32R)
    stage = ph.sb("stage", [P, 2, HALF])
    ps = [ph.ps(f"s{i}", [P, HALF]) for i in range(2)]
    st = ph.sems("st", 2)
    hi_done, lo_done, mm_done, out_done = (ph.sem(n) for n in ("hi_done", "lo_done", "mm_done", "out_done"))

    beta_sys = ph.sb("beta_sys", [P, CHUNK])
    eg_row = ph.sb("eg_row", [HEADS, S])
    g_tok, beta_tok, beta_eg_tok, rest_tok = (ph.sb(n, [P, TH]) for n in ("g_tok", "beta_tok", "beta_eg_tok", "rest_tok"))
    chunk_decay = ph.sb("chunk_decay", [P, 2, TILES, 4])
    neg_a, eps_q = ph.sb("neg_a", [HEADS, 1]), ph.sb("eps_q", [P, 1])
    AREAS = 22
    arena = ph.sb("arena", [P, AREAS * S])

    def area(first, pattern=None, count=1, **dims):
        cols = arena[:, int(first * S):int((first + count) * S)]
        return cols.rearrange(pattern, **dims) if pattern else cols

    rows = {name: area(8 + i)[0:HEADS] for i, name in enumerate(
        ("a", "b", "reset", "mag", "e", "u", "lnu", "resid", "rec", "gl", "gcum", "beta"))}
    tok = area(20, "p (k n) -> p k n", k=4, count=0.25)[:, 0:3]
    eg_tok = area(20.25)[:, 0:TH]
    XR, RING = 4, 4
    x = area(0, "p (s n) -> p s n", count=XR, s=XR)
    sq = area(4, "p (s n) -> p s n", count=2, s=2)
    norm, rn = area(6), area(7)
    q_n, k_n = (area(a, "p (b n) -> p b n", count=4, b=4) for a in (8, 12))
    ring = area(16, "p (s n) -> p s n", count=RING, s=RING)
    gu, decay = (area(a, "p (h n) -> p h n", h=HEADS) for a in (20, 21))
    lt = area(8, "p (j i) -> p j i", count=4, j=CHUNK)
    r = area(12, "p (c i) -> p c i", count=4, c=CHUNK)
    part, part_late = area(20), area(21)
    inv = area(0, "p (s h n) -> p s h n", count=2, s=2, h=HEADS)
    w_t = area(2, "p (s b n) -> p s b n", s=2, b=4)
    u = area(3, "p (s n) -> p s n", count=2, s=2)
    k_beta, k_rest = (area(a, "p (s n) -> p s n", s=2) for a in (5, 6))
    q_decayed = area(7, "p (s b n) -> p s b n", s=2, b=4)
    intra = area(16, "p (s h n) -> p s h n", count=2, s=2, h=HEADS)
    state, kept = (area(a, "p (b v) -> p b v", count=0.5, b=4) for a in (10, 10.5))
    v_new = area(11, "p (s n) -> p s n", count=2, s=2)
    o = area(13, "p (s n) -> p s n", count=2, s=2)
    o_sq = area(15)
    z = area(18, "p (s h n) -> p s h n", count=2, s=2, h=HEADS)
    o_t = area(8, "p (s h n) -> p s h n", count=2, s=2, h=HEADS)
    wa, acc = ph.sb("wa", [P, 2, D]), ph.sb("acc", [P, D])
    ss, std, rstd = ph.sb("ss", [P, HEADS]), ph.sb("std", [P, HEADS]), ph.sb("rstd", [P, HEADS])

    side_ps = ph.ps("side", [P, 3, S])
    ps_a, ps_b, ps_c = (side_ps[:, i] for i in range(3))
    ps_tok = side_ps[:, 0, 0:4 * TH].rearrange("p (k n) -> p k n", k=4)[:, 0:3]
    ps_sum = side_ps[:, 1, 0:4 * TH].rearrange("p (k n) -> p k n", k=4)[:, 0:3]
    ps_ws, ps_o = side_ps[:, 0], side_ps[:, 1]
    by_head = "p (r b v) -> p b r v"
    head_at = lambda h: slice(h % 2 * HALF + h // 2 * DV, h % 2 * HALF + h // 2 * DV + DV)
    ps_kv, ps_m = side_ps[:, 2, 0:HALF], side_ps[:, 2, HALF:S]

    ld_d, a_step, v_step, tr_done, total_done = (ph.sem(n) for n in ("ld_d", "a_step", "v_step", "tr_done", "total_done"))
    ld_x, st_r = ph.sems("ld_x", XR), ph.sems("st_r", RING)
    sq_done, ss_done, norm_done, rn_done, n_done = (ph.sem(n) for n in ("sq_done", "ss_done", "norm_done", "rn_done", "n_done"))
    bc_done, kt_done, vt_done, b_used, c_used, ring_full = (
        ph.sem(n) for n in ("bc_done", "kt_done", "vt_done", "b_used", "c_used", "ring_full"))
    gu_done, diff_done, exp_done, mask_done, prod_done, tile_done = (
        ph.sem(n) for n in ("gu_done", "diff_done", "exp_done", "mask_done", "prod_done", "tile_done"))
    eps_set = ph.sem("eps_set")
    ld_s, st_s, solve_step, late_step = (ph.sem(n) for n in ("ld_s", "st_s", "solve_step", "late_step"))
    ld_a, ada_done, mod_step = ph.sems("ld_a", 2), ph.sem("ada_done"), ph.sem("mod_step")
    ld_t, ld_z, st_o = ph.sems("ld_t", 2), ph.sems("ld_z", 2), ph.sems("st_o", 2)
    zeroed, m_filled, m_free = ph.sem("zeroed"), ph.sem("m_filled"), ph.sem("m_free")
    ws_done, vn_done, kept_done, kv_done, s_done = (ph.sem(n) for n in ("ws_done", "vn_done", "kept_done", "kv_done", "s_done"))
    o_done, o_copied, sum_done, std_done, rstd_done, on_done = (
        ph.sem(n) for n in ("o_done", "o_copied", "sum_done", "std_done", "rstd_done", "on_done"))
    block = ph.stack.enter_context(nc.Block())
    ident = g.const[:, C_IDENT:C_IDENT + P]
    SOLVE_STEPS, LATE_STEPS = 3 + 2 * (CHUNK - 1), 2 * (CHUNK - 1 - LATE)

    ring_uses = []
    for n in range(NQK):
        ring_uses += [("value", n)] + ([("k_beta", n // 2), ("k_rest", n // 2)] if n % 2 else [("q", n // 2)])
    for t in range(TILES):
        ring_uses += [("system", t), ("intra", t)]
    ring_no = {key: n for n, key in enumerate(ring_uses)}

    def stored(slot, before):
        return sum(32 if key[0] == "system" else 16 for n, key in enumerate(ring_uses) if n < before and n % RING == slot)

    m_no = {key: n for n, key in enumerate([s for s in ORDER if s[0] in ("u", "w", "out", "mod")])}

    @block.sync
    def _(sp):
        def load_x(i):
            n = i // 2
            b = B_DN + 8 + n if i % 2 else B_DN + n // 2 + 4 * (n % 2)
            sp.dma_start(x[:, i % XR], d["proj"][b]).then_inc(ld_x[i % XR], 16)

        def ship(kind, n):
            no = ring_no[kind, n]
            src = ring[:, no % RING]
            sp.wait_ge(ring_full, no + 1)
            if kind == "system":
                dst = d["systems"].rearrange("(h t c) j i -> t c j h i", h=HEADS, c=2)[n]
                src = src.rearrange("p (h i) -> p h i", h=HEADS)
                for c in range(2):
                    half = slice(c * CHUNK, (c + 1) * CHUNK)
                    sp.dma_start(dst[c], src[half, :, half]).then_inc(st_r[no % RING], 16)
                return
            if kind == "q":
                dst = d["q_decayed"][n]
            elif kind == "intra":
                dst = d["intra"][n]
            else:
                dst = d[kind][:, :, n * P:(n + 1) * P]
                src = src.rearrange("p (t k) -> p t k", t=TILES)
            sp.dma_start(dst, src).then_inc(st_r[no % RING], 16)

        def load_inv(t):
            for c in range(2):
                half = slice(c * CHUNK, (c + 1) * CHUNK)
                src = d["solved"].rearrange("(h t c) j i -> t c j h i", h=HEADS, c=2)[t, c]
                sp.dma_start(inv[half, t % 2, :, half], src).then_inc(ld_t[t % 2], 16)

        def load_tile(t):
            s = t % 2
            sp.dma_start(u[:, s], d["value"][:, t]).then_inc(ld_t[s], 16)
            sp.dma_start(k_beta[:, s], d["k_beta"][:, t]).then_inc(ld_t[s], 16)
            sp.dma_start(k_rest[:, s], d["k_rest"][:, t]).then_inc(ld_t[s], 16)
            src = d["q_decayed"].rearrange("b p n -> p b n")[:, :, t * P:(t + 1) * P]
            sp.dma_start(q_decayed[:, s], src).then_inc(ld_t[s], 16)
            src = d["intra"][t].rearrange("p (h n) -> p h n", h=HEADS)
            sp.dma_start(intra[:, s], src).then_inc(ld_t[s], 16)

        def load_z(t):
            src = d["proj"][B_Z:B_SB].rearrange("h v n -> v h n")[:, :, t * P:(t + 1) * P]
            sp.dma_start(z[:, t % 2], src).then_inc(ld_z[t % 2], 16)

        def store_half(n, half):
            sp.wait_ge(out_done, 2 * n + half + 1)
            sp.dma_start(d["proj"][B_Z + n][:, half * HALF:(half + 1) * HALF], stage[:, half]).then_inc(st[half], 16)

        def load_ada(i):
            if i >= 2:
                sp.wait_ge(ada_done, i - 1)
            sp.dma_start(wa[:, i % 2], d["w_ada"][3 + i // KD, i % KD // 4][:, i % 4]).then_inc(ld_a[i % 2], 16)

        ab = d["proj"][0]
        for dst, src in ((rows["b"], ab[0:HEADS]), (rows["a"], ab[HEADS:2 * HEADS]),
                         (beta_sys[:], ab[0:HEADS].rearrange("h (c i) -> (h c) i", i=CHUNK)), (rows["reset"], d["reset"])):
            sp.dma_start(dst, src).then_inc(ld_d, 16)
        for i in range(XR):
            load_x(i)
        load_ada(0)
        load_ada(1)
        for kind, *index in ORDER:
            if kind == "dense":
                n, q = index
                if q == 0:
                    if n:
                        store_half(n - 1, 1)
                    if n + 2 < BLOCKS:
                        sp.wait_ge(lo_done, n + 1)
                        sp.dma_start(raw[:, n % 2], d["w_in"][B_Z + n + 2][:, 0:KD * P]).then_inc(ld[n % 2], 16)
                elif q == KD:
                    store_half(n, 0)
            elif kind == "ship":
                n, = index
                if 2 * n + XR < 2 * NQK:
                    sp.wait_ge(n_done, n + 1)
                    load_x(2 * n + XR)
                    sp.wait_ge(vt_done, n + 1)
                    load_x(2 * n + XR + 1)
                ship("value", n)
                for name in ("k_beta", "k_rest") if n % 2 else ("q",):
                    ship(name, n // 2)
            elif kind == "ada":
                if index[0] >= 1 and index[0] + 1 < 3 * KD:
                    load_ada(index[0] + 1)
            elif kind == "ship_tile":
                ship("system", *index)
                ship("intra", *index)
            elif kind == "solve":
                for s in range(RING):
                    sp.wait_ge(st_r[s], stored(s, len(ring_uses)))
                sp.wait_ge(tile_done, TILES)
                sp.dma_start(lt, d["systems"]).then_inc(ld_s, 16)
            elif kind == "preload":
                for s in range(2):
                    sp.wait_ge(st[s], 16 * (B_SB - B_Z))
                load_tile(*index)
                load_z(*index)
            elif kind == "solved":
                sp.wait_ge(solve_step, SOLVE_STEPS)
                sp.wait_ge(late_step, LATE_STEPS)
                sp.dma_start(d["solved"], r).then_inc(st_s, 16)
                sp.wait_ge(zeroed, 2)
                sp.wait_ge(st_s, 16)
                for t in range(2):
                    load_inv(t)
            elif kind == "load":
                t, = index
                sp.wait_ge(o_done, t - 1)
                load_inv(t)
                load_tile(t)
            elif kind == "ship_out":
                t, = index
                sp.wait_ge(m_free, m_no["out", t, 1] + 1)
                sp.dma_start(d["o_b"].rearrange("h v n -> v h n")[:, :, t * P:(t + 1) * P], o_t[:, t % 2])\
                  .then_inc(st_o[t % 2], 16)
                if t + 2 < TILES:
                    load_z(t + 2)
        store_half(BLOCKS - 1, 1)
        for s in range(2):
            sp.wait_ge(st_o[s], 16 * TILES // 2)
            sp.wait_ge(st[s], 16 * BLOCKS)

    @block.scalar
    def _(act):
        def split(n):
            act.wait_ge(ld[n % 2], 16 * (n // 2 + 1))
            if n >= 2:
                act.wait_ge(mm_done, 2 * (n - 1))
            act.activation(w_hi[:, n % 2], raw[:, n % 2].rearrange("p (k m) -> p k m", k=KD), ACT.Copy)\
               .then_inc(hi_done, 1)

        def evacuate(n, half):
            func = ACT.Silu if n < B_SB - B_Z else ACT.Copy if n < B_GATE - B_Z else ACT.Sigmoid
            act.wait_ge(mm_done, 2 * n + half + 1)
            if n:
                act.wait_ge(st[half], 16 * n)
            act.activation(stage[:, half], ps[half][:], func).then_inc(out_done, 1)

        def decay_part(i):
            if i == 0:
                act.wait_ge(ld_d, 64)
                act.activation(rows["beta"], rows["b"], ACT.Sigmoid).then_inc(a_step, 1)
                act.activation(beta_sys[:], beta_sys[:], ACT.Sigmoid).then_inc(a_step, 1)
            elif i == 1:
                act.wait_ge(v_step, 1)
                act.activation(rows["mag"], rows["a"], ACT.Abs).then_inc(a_step, 1)
                act.wait_ge(a_step, 3)
                act.activation(rows["e"], rows["mag"], ACT.Exp, scale=-1.0).then_inc(a_step, 1)
                act.activation(neg_a[:], g.small["dn_head"][:, 0:1], ACT.Exp).then_inc(a_step, 1)
            elif i == 2:
                act.wait_ge(v_step, 2)
                act.activation(rows["lnu"], rows["u"], ACT.Ln).then_inc(a_step, 1)
            elif i == 4:
                act.wait_ge(v_step, 10)
                act.activation(eg_row[:], rows["gcum"], ACT.Exp).then_inc(a_step, 1)
            elif i == 5:
                act.wait_ge(v_step, 11)
                act.activation(eg_tok, tok[:, 2], ACT.Exp).then_inc(a_step, 1)
                act.wait_ge(total_done, 1)
                act.activation(rest_tok[:], ps_sum[:, 0], ACT.Exp).then_inc(a_step, 1)
                for par in range(2):
                    half = slice(par * DK, (par + 1) * DK)
                    src = ps_sum[half, 1:3].rearrange("p c (t h) -> p c t h", h=HEADS)[:, :, :, par::2]
                    act.activation(chunk_decay[half], src, ACT.Exp).then_inc(a_step, 1)

        split(0)
        for kind, *index in ORDER:
            if kind == "dense":
                n, q = index
                if q == 0:
                    if n:
                        evacuate(n - 1, 1)
                    if n + 1 < BLOCKS:
                        split(n + 1)
                elif q == KD:
                    evacuate(n, 0)
            elif kind == "decay":
                decay_part(*index)
            elif kind == "square":
                n, = index
                i = 2 * n
                act.wait_ge(ld_x[i % XR], 16 * (i // XR + 1))
                if n >= 2:
                    act.wait_ge(ss_done, n - 1)
                act.activation(sq[:, n % 2], x[:, i % XR], ACT.Square).then_inc(sq_done, 1)
            elif kind == "norm":
                n, = index
                act.wait_ge(ss_done, n + 1)
                if n:
                    act.wait_ge(rn_done, n)
                if n % 2 == 0:
                    act.wait_ge(eps_set, 1)
                    act.activation(norm, ps_a, ACT.Sqrt, scale=float(DK), bias=eps_q[:]).then_inc(norm_done, 1)
                else:
                    act.activation(norm, ps_a, ACT.Sqrt, bias=g.eps[:]).then_inc(norm_done, 1)
            elif kind == "diff":
                t, = index
                act.wait_ge(diff_done, t + 1)
                if t:
                    act.wait_ge(tile_done, t)
                act.activation(decay.rearrange("p h i -> p (h i)"), ps_a, ACT.Exp).then_inc(exp_done, 1)
            elif kind == "u":
                t, half = index
                act.wait_ge(m_filled, m_no["u", t, half] + 1)
                act.activation(u[:, t % 2, half * HALF:(half + 1) * HALF], ps_m, ACT.Copy).then_inc(m_free, 1)
            elif kind == "w":
                t, = index
                act.wait_ge(m_filled, m_no["w", t] + 1)
                act.activation(w_t[:, t % 2], ps_m.rearrange("p (b n) -> p b n", b=4), ACT.Copy).then_inc(m_free, 1)
            elif kind == "mod":
                i, = index
                act.wait_ge(m_filled, m_no["mod", i] + 1)
                act.activation(g.mod[:, (3 + i) * KD:(4 + i) * KD], ps_m[:, 0:KD], ACT.Copy).then_inc(m_free, 1)
            elif kind == "write" and index[0] % 2:
                t = index[0] // 2
                act.wait_ge(o_done, t + 1)
                if t:
                    act.wait_ge(sum_done, t)
                if t >= 2:
                    act.wait_ge(m_filled, m_no["out", t - 2, 1] + 1)
                for dst, func in ((o[:, t % 2], ACT.Copy), (o_sq, ACT.Square)):
                    act.activation(dst.rearrange("p (b r v) -> p b r v", b=4, r=2), ps_o.rearrange(by_head, r=2, b=4), func)\
                       .then_inc(o_copied, 1)
            elif kind == "std":
                t, = index
                act.wait_ge(sum_done, t + 1)
                act.activation(std[:], ss[:], ACT.Sqrt, scale=1.0 / DV, bias=g.eps[:]).then_inc(std_done, 1)
        evacuate(BLOCKS - 1, 1)

    @block.gpsimd
    def _(pool):
        incl_h = g.const[:, C_INCL:C_INCL + P].unsqueeze(1).to_broadcast([P, HEADS, P])

        def low(n):
            pool.wait_ge(hi_done, n + 1)
            pool.tensor_tensor(w_lo[:, n % 2], raw[:, n % 2].rearrange("p (k m) -> p k m", k=KD),
                               as_f32(w_hi[:, n % 2]), ALU.subtract).then_inc(lo_done, 1)

        def spread(t):
            if t:
                pool.wait_ge(diff_done, t)
            g_t = g_tok[:, t * HEADS:(t + 1) * HEADS]
            pool.tensor_tensor(gu, incl_h, g_t.unsqueeze(2).to_broadcast([P, HEADS, P]), ALU.mult).then_inc(gu_done, 1)

        pool.memset(eps_q[:], DK * EPS).then_inc(eps_set, 1)
        low(0)
        for kind, *index in ORDER:
            if kind == "dense":
                n, q = index
                if q == 0 and n + 1 < BLOCKS:
                    low(n + 1)
            elif kind == "diff":
                t, = index
                pool.wait_ge(exp_done, t + 1)
                pool.tensor_tensor(decay, decay, incl_h, ALU.mult).then_inc(mask_done, 1)
                if t + 1 < TILES:
                    spread(t + 1)
            elif kind == "norm":
                n, = index
                pool.wait_ge(rn_done, n + 1)
                pool.tensor_tensor((q_n, k_n)[n % 2][:, n // 2], x[:, 2 * n % XR], rn, ALU.mult).then_inc(n_done, 1)
            elif kind == "turn" and index[0] == NQK - 1:
                pool.wait_ge(a_step, 11)
                pool.wait_ge(v_step, 14)
                spread(0)
            elif kind == "solve":
                pool.wait_ge(tile_done, TILES)
                for s in range(2):
                    pool.memset(inv[:, s], 0.0).then_inc(zeroed, 1)
                pool.wait_ge(solve_step, 3)
            elif kind == "solve_late":
                j, = index
                c, i = j + 1 - LATE, CHUNK - 1 - j
                out = part_late[:, 0:c * i].rearrange("p (c i) -> p c i", c=c)
                if j > LATE:
                    pool.wait_ge(late_step, 2 * (j - LATE))
                pool.tensor_tensor(out, r[:, LATE:j + 1, j:j + 1].to_broadcast([P, c, i]),
                                   lt[:, j:j + 1, j + 1:CHUNK].to_broadcast([P, c, i]), ALU.mult).then_inc(late_step, 1)
                pool.wait_ge(late_step, 2 * (j - LATE) + 1)
                pool.tensor_tensor(r[:, LATE:j + 1, j + 1:CHUNK], r[:, LATE:j + 1, j + 1:CHUNK], out, ALU.subtract)\
                    .then_inc(late_step, 1)
            elif kind == "solved":
                pool.wait_ge(solve_step, SOLVE_STEPS)
                pool.wait_ge(late_step, LATE_STEPS)
                pool.memset(state, 0.0).then_inc(zeroed, 1)
                pool.wait_ge(zeroed, 3)
            elif kind == "read":
                n, = index
                if n:
                    pool.wait_ge(s_done, n)
                by = chunk_decay[:, n % 2, n // 2].unsqueeze(2).to_broadcast([P, 4, DV])
                pool.tensor_tensor(kept, state, by, ALU.mult).then_inc(kept_done, 1)
            elif kind == "scale":
                t, = index
                pool.wait_ge(rstd_done, t + 1)
                o_h = o[:, t % 2].rearrange("p (h v) -> p h v", h=HEADS)
                pool.tensor_tensor(o_h, o_h, rstd[:].unsqueeze(2).to_broadcast([P, HEADS, DV]), ALU.mult)\
                    .then_inc(on_done, 1)

    @block.vector
    def _(dve):
        done = {v_step: 0, solve_step: 0}

        def then(ins, signal=v_step):
            done[signal] += 1
            ins.then_inc(signal, 1)
            dve.wait_ge(signal, done[signal])

        def ring_slot(key):
            no = ring_no[key]
            if no >= RING:
                dve.wait_ge(st_r[no % RING], stored(no % RING, no))
            return ring[:, no % RING]

        def decay_part(i):
            row = rows
            if i == 0:
                dve.wait_ge(ld_d, 64)
                then(dve.tensor_scalar(row["a"], row["a"], g.small["dn_head"][:, 1:2], None, ALU.add))
            elif i == 1:
                dve.wait_ge(a_step, 5)
                then(dve.tensor_scalar(row["u"], row["e"], 1.0, None, ALU.add))
                then(dve.tensor_scalar(row["resid"], row["u"], -1.0, None, ALU.add))
                then(dve.tensor_tensor(row["resid"], row["e"], row["resid"], ALU.subtract))
                then(dve.reciprocal(row["rec"], row["u"]))
                then(dve.tensor_tensor(row["resid"], row["resid"], row["rec"], ALU.mult))
            elif i == 2:
                dve.wait_ge(a_step, 6)
                then(dve.tensor_tensor(row["resid"], row["resid"], row["lnu"], ALU.add))
                then(dve.scalar_tensor_tensor(row["gl"], row["a"], 0.0, row["resid"], ALU.max, ALU.add))
                then(dve.tensor_scalar(row["gl"], row["gl"], neg_a[:], -1.0, ALU.mult, ALU.mult))
                then(dve.tensor_tensor_scan(row["gcum"], row["reset"], row["gl"], 0.0, ALU.mult, ALU.add))
            elif i == 4:
                dve.wait_ge(tr_done, 1)
                then(dve.tensor_copy(tok, ps_tok))
                dve.tensor_copy(g_tok[:], tok[:, 0]).then_inc(v_step, 1)
                dve.tensor_copy(beta_tok[:], tok[:, 1]).then_inc(v_step, 1)
                dve.wait_ge(a_step, 8)
                dve.tensor_tensor(beta_eg_tok[:], tok[:, 1], eg_tok, ALU.mult).then_inc(v_step, 1)

        for kind, *index in ORDER:
            if kind == "decay":
                decay_part(*index)
            elif kind == "norm":
                n, = index
                dve.wait_ge(norm_done, n + 1)
                if n:
                    dve.wait_ge(n_done, n)
                dve.reciprocal(rn, norm).then_inc(rn_done, 1)
            elif kind == "value":
                h, = index
                dve.wait_ge(vt_done, h + 1)
                dve.wait_ge(v_step, 14)
                by = beta_tok[:].rearrange("p (t h) -> p t h", h=HEADS)[:, :, h:h + 1]
                ps_v, used = ((ps_c, c_used), (ps_b, b_used))[h % 2]
                dst = ring_slot(("value", h)).rearrange("p (t v) -> p t v", t=TILES)
                dve.tensor_tensor(dst, ps_v.rearrange("p (t v) -> p t v", t=TILES), by.to_broadcast([P, TILES, DV]),
                                  ALU.mult).then_inc(used, 1)
                dve.wait_ge(used, h + 1)
                dve.sem_inc(ring_full, 1)
            elif kind == "turn":
                n, = index
                b = n // 2
                if n % 2 == 0:
                    dve.wait_ge(n_done, n + 1)
                    dve.wait_ge(bc_done, b + 1)
                    dve.tensor_tensor(ring_slot(("q", b)), q_n[:, b], ps_b, ALU.mult).then_inc(b_used, 1)
                    dve.wait_ge(b_used, n + 1)
                    dve.sem_inc(ring_full, 1)
                else:
                    dve.wait_ge(kt_done, b + 1)
                    if b == 0:
                        dve.wait_ge(a_step, 11)
                    k_tok = ps_c.rearrange("p (t h k) -> p t h k", t=TILES, h=2)
                    for name, by in (("k_beta", beta_eg_tok), ("k_rest", rest_tok)):
                        by = by[:].rearrange("p (t h) -> p t h", h=HEADS)[:, :, 2 * b:2 * b + 2]
                        dst = ring_slot((name, b)).rearrange("p (t h k) -> p t h k", t=TILES, h=2)
                        dve.tensor_tensor(dst, k_tok, by.unsqueeze(3).to_broadcast([P, TILES, 2, DK]), ALU.mult)\
                           .then_inc(ring_full, 1)
                    dve.wait_ge(ring_full, ring_no["k_rest", b] + 1)
                    dve.sem_inc(c_used, 1)
            elif kind == "weights":
                t, = index
                dve.wait_ge(mask_done, t + 1)
                dve.wait_ge(prod_done, t + 1)
                for name, src in (("system", ps_b), ("intra", ps_c)):
                    dst = ring_slot((name, t)).rearrange("p (h i) -> p h i", h=HEADS)
                    for par in range(2):
                        prod = src[:, par * HALF:(par + 1) * HALF].rearrange("p (h i) -> p h i", h=4)
                        ins = dve.tensor_tensor(dst[:, par::2], prod, decay[:, par::2], ALU.mult)
                    ins.then_inc(ring_full, 1)
                dve.wait_ge(ring_full, ring_no["intra", t] + 1)
                dve.sem_inc(tile_done, 1)
            elif kind == "solve":
                then(dve.memset(r, 0.0), solve_step)
                then(dve.memset(r.rearrange("p c i -> p (c i)")[:, 0:CHUNK * CHUNK:CHUNK + 1], 1.0), solve_step)
                dve.wait_ge(ld_s, 16)
                then(dve.tensor_tensor(lt, lt, beta_sys[:].unsqueeze(1).to_broadcast([P, CHUNK, CHUNK]), ALU.mult),
                     solve_step)
                for j in range(CHUNK - 1):
                    c, i = min(j + 1, LATE), CHUNK - 1 - j
                    out = part[:, 0:c * i].rearrange("p (c i) -> p c i", c=c)
                    then(dve.tensor_tensor(out, r[:, 0:c, j:j + 1].to_broadcast([P, c, i]),
                                           lt[:, j:j + 1, j + 1:CHUNK].to_broadcast([P, c, i]), ALU.mult), solve_step)
                    then(dve.tensor_tensor(r[:, 0:c, j + 1:CHUNK], r[:, 0:c, j + 1:CHUNK], out, ALU.subtract),
                         solve_step)
            elif kind == "read":
                n, = index
                t, c = n // 2, n % 2
                half = slice(c * CHUNK, (c + 1) * CHUNK)
                dve.wait_ge(ws_done, n + 1)
                if t >= 2:
                    dve.wait_ge(o_done, t - 1)
                natural = lambda ap: ap.rearrange("p (b r v) -> p b r v", b=4, r=2)
                dve.tensor_tensor(natural(v_new[half, t % 2]), natural(u[half, t % 2]),
                                  ps_ws[half].rearrange(by_head, r=2, b=4), ALU.subtract).then_inc(vn_done, 1)
            elif kind == "write":
                n, = index
                dve.wait_ge(kv_done, n + 1)
                dve.wait_ge(kept_done, n + 1)
                dve.tensor_tensor(state, kept, ps_kv.rearrange("p (b v) -> p b v", b=4), ALU.add).then_inc(s_done, 1)
            elif kind == "ada":
                i, = index
                c_k = g.c_act[:, i % KD:i % KD + 1]
                dve.wait_ge(ld_a[i % 2], 16 * (i // 2 + 1))
                if i % KD == 0:
                    if i:
                        dve.wait_ge(m_free, m_no["mod", i // KD - 1] + 1)
                    ins = dve.tensor_scalar(acc[:], wa[:, i % 2], c_k, None, ALU.mult)
                else:
                    dve.wait_ge(ada_done, i)
                    ins = dve.scalar_tensor_tensor(acc[:], wa[:, i % 2], c_k, acc[:], ALU.mult, ALU.add)
                ins.then_inc(ada_done, 1)
            elif kind == "root":
                t, = index
                dve.wait_ge(o_copied, 2 * t + 2)
                if t:
                    dve.wait_ge(std_done, t)
                dve.tensor_reduce(ss[:], o_sq.rearrange("p (h v) -> p h v", h=HEADS), AX.X, ALU.add)\
                   .then_inc(sum_done, 1)
            elif kind == "std":
                t, = index
                dve.wait_ge(std_done, t + 1)
                if t:
                    dve.wait_ge(on_done, t)
                dve.reciprocal(rstd[:], std[:]).then_inc(rstd_done, 1)
            elif kind == "out":
                t, half = index
                s = t % 2
                dve.wait_ge(m_filled, m_no["out", t, half] + 1)
                dve.wait_ge(ld_z[s], 16 * (t // 2 + 1))
                if t >= 2:
                    dve.wait_ge(st_o[s], 16 * (t // 2))
                heads = slice(4 * half, 4 * half + 4)
                dve.scalar_tensor_tensor(o_t[:, s, heads], ps_m.rearrange("p (h n) -> p h n", h=4),
                                         g.small["dn_norm"][:], z[:, s, heads], ALU.mult, ALU.mult)\
                   .then_inc(m_free, 1)
        dve.wait_ge(m_free, m_no["mod", 2] + 1)
        dve.tensor_tensor(g.mod[:, 3 * KD:6 * KD], g.mod[:, 3 * KD:6 * KD], g.small["b_ada"][:, 3 * KD:6 * KD], ALU.add)\
           .then_inc(mod_step, 1)
        dve.wait_ge(mod_step, 1)
        dve.scalar_tensor_tensor(g.mod[:, 4 * KD:5 * KD], g.mod[:, 4 * KD:5 * KD], 1.0,
                                 g.small["norms"][:, KD:2 * KD], ALU.add, ALU.mult).then_inc(mod_step, 1)

    @block.tensor
    def _(pe):
        def dense(n, q):
            half, k = q // KD, q % KD
            if q == 0:
                pe.wait_ge(lo_done, n + 1)
            if k == 0 and n:
                pe.wait_ge(out_done, 2 * (n - 1) + half + 1)
            cols = slice(half * HALF, (half + 1) * HALF)
            for i, (w, h) in enumerate(three(w_hi[:, n % 2, k], w_lo[:, n % 2, k], g.h_hi[:, k, cols], g.h_lo[:, k, cols])):
                mm = pe.matmul(ps[half][:], w, h, start=k == 0 and i == 0, stop=k == KD - 1 and i == 2)
            if k == KD - 1:
                mm.then_inc(mm_done, 1)

        def take_m(key):
            if m_no[key]:
                pe.wait_ge(m_free, m_no[key])

        for kind, *index in ORDER:
            if kind == "dense":
                dense(*index)
            elif kind == "decay" and index[0] == 4:
                pe.wait_ge(a_step, 1)
                pe.wait_ge(v_step, 10)
                ident8 = g.const[0:HEADS, C_IDENT:C_IDENT + HEADS]
                for i, name in enumerate(("gl", "beta", "gcum")):
                    for t in range(TILES):
                        mm = pe.transpose(ps_tok[:, i, t * HEADS:(t + 1) * HEADS], rows[name][:, t * P:(t + 1) * P], ident8)
                mm.then_inc(tr_done, 1)
            elif kind == "decay" and index[0] == 5:
                pe.wait_ge(v_step, 11)
                for i, table in enumerate((C_STRICT, C_EVEN, C_ODD)):
                    mm = pe.matmul(ps_sum[:, i], g.const[:, table:table + P], tok[:, 0], start=True, stop=True)
                mm.then_inc(total_done, 1)
            elif kind == "norm":
                n, = index
                pe.wait_ge(sq_done, n + 1)
                if n:
                    pe.wait_ge(norm_done, n)
                for t in range(2):
                    cols = slice(t * HALF, (t + 1) * HALF)
                    mm = pe.matmul(ps_a[:, cols], g.const[:, C_ONES64:C_ONES64 + P], sq[:, n % 2, cols], start=True, stop=True)
                mm.then_inc(ss_done, 1)
            elif kind == "value":
                h, = index
                i = 2 * h + 1
                pe.wait_ge(ld_x[i % XR], 16 * (i // XR + 1))
                if h:
                    pe.wait_ge((c_used, b_used)[h % 2], h)
                else:
                    pe.wait_ge(a_step, 11)
                for t in range(TILES):
                    mm = pe.transpose((ps_c, ps_b)[h % 2][:, t * P:(t + 1) * P], x[:, i % XR, t * P:(t + 1) * P], ident)
                mm.then_inc(vt_done, 1)
            elif kind == "turn":
                n, = index
                b = n // 2
                if n % 2 == 0:
                    if b:
                        pe.wait_ge(b_used, n)
                    for t in range(2):
                        cols = slice(t * HALF, (t + 1) * HALF)
                        mm = pe.matmul(ps_b[:, cols], g.const[0:HEADS, C_SEL + b * P:C_SEL + (b + 1) * P],
                                       eg_row[:, cols], start=True, stop=True)
                    mm.then_inc(bc_done, 1)
                else:
                    pe.wait_ge(n_done, n + 1)
                    pe.wait_ge(c_used, n)
                    for t in range(TILES):
                        mm = pe.transpose(ps_c[:, t * P:(t + 1) * P], k_n[:, b, t * P:(t + 1) * P], ident)
                    mm.then_inc(kt_done, 1)
            elif kind == "diff":
                t, = index
                pe.wait_ge(gu_done, t + 1)
                pe.wait_ge(*((exp_done, t) if t else (norm_done, NQK)))
                for i in range(2):
                    mm = pe.matmul(ps_a[:, i * HALF:(i + 1) * HALF], g.const[:, C_STRICT:C_STRICT + P],
                                   gu[:, 4 * i:4 * i + 4], start=True, stop=True)
                mm.then_inc(diff_done, 1)
            elif kind == "weights":
                t, = index
                if t:
                    pe.wait_ge(tile_done, t)
                else:
                    pe.wait_ge(b_used, NQK)
                    pe.wait_ge(c_used, NQK)
                cols = slice(t * P, (t + 1) * P)
                for dst, rhs in ((ps_b, k_n), (ps_c, q_n)):
                    for b in range(4):
                        for par in range(2):
                            half = slice(par * DK, (par + 1) * DK)
                            to = par * HALF + b * P
                            mm = pe.matmul(dst[:, to:to + P], k_n[half, b, cols], rhs[half, b, cols], start=True, stop=True)
                mm.then_inc(prod_done, 1)
            elif kind == "u":
                t, half = index
                take_m((kind, *index))
                pe.wait_ge(ld_t[t % 2], 112 * (t // 2 + 1))
                for h in range(4 * half, 4 * half + 4):
                    mm = pe.matmul(ps_m[:, h % 4 * DV:(h % 4 + 1) * DV], inv[:, t % 2, h], u[:, t % 2, h * DV:(h + 1) * DV],
                                   start=True, stop=True)
                mm.then_inc(m_filled, 1)
            elif kind == "w":
                t, = index
                take_m((kind, t))
                for h in range(HEADS):
                    half = slice(h % 2 * DK, h % 2 * DK + DK)
                    mm = pe.matmul(ps_m[half, h // 2 * P:(h // 2 + 1) * P], k_beta[:, t % 2, h * DK:(h + 1) * DK],
                                   inv[:, t % 2, h], start=True, stop=True)
                mm.then_inc(m_filled, 1)
            elif kind == "mod":
                take_m((kind, *index))
                pe.wait_ge(tile_done, TILES)
                pe.wait_ge(ada_done, KD * (index[0] + 1))
                for m in range(KD):
                    mm = pe.matmul(ps_m[:, m:m + 1], acc[:, m * P:(m + 1) * P], g.const[:, C_ONES:C_ONES + 1],
                                   start=True, stop=True)
                mm.then_inc(m_filled, 1)
            elif kind == "out":
                t, half = index
                take_m((kind, *index))
                pe.wait_ge(on_done, t + 1)
                for h in range(4 * half, 4 * half + 4):
                    mm = pe.transpose(ps_m[:, h % 4 * P:(h % 4 + 1) * P], o[:, t % 2, h * DV:(h + 1) * DV], ident)
                mm.then_inc(m_filled, 1)
            elif kind == "read":
                n, = index
                t, c = n // 2, n % 2
                to = slice(c * CHUNK, (c + 1) * CHUNK)
                pe.wait_ge(m_free, m_no["w", t] + 1)
                if n:
                    pe.wait_ge(s_done, n)
                else:
                    pe.wait_ge(zeroed, 3)
                for h in range(HEADS):
                    half = slice(h % 2 * DK, h % 2 * DK + DK)
                    mm = pe.matmul(ps_ws[to, head_at(h)], w_t[half, t % 2, h // 2, to], state[half, h // 2],
                                   start=True, stop=True)
                mm.then_inc(ws_done, 1)
                if t:
                    pe.wait_ge(o_copied, 2 * t)
                for h in range(HEADS):
                    half = slice(h % 2 * DK, h % 2 * DK + DK)
                    pe.matmul(ps_o[to, head_at(h)], q_decayed[half, t % 2, h // 2, to], state[half, h // 2],
                              start=h < 2, stop=False, skip_group_check=True)
            elif kind == "write":
                n, = index
                t, c = n // 2, n % 2
                frm = slice(c * CHUNK, (c + 1) * CHUNK)
                pe.wait_ge(vn_done, n + 1)
                for h in range(HEADS):
                    half = slice(h % 2 * DK, h % 2 * DK + DK)
                    mm = pe.matmul(ps_kv[half, h // 2 * DV:(h // 2 + 1) * DV], k_rest[frm, t % 2, h * DK:(h + 1) * DK],
                                   v_new[frm, t % 2, h * DV:(h + 1) * DV], start=True, stop=True)
                mm.then_inc(kv_done, 1)
                if c == 1:
                    for h in range(HEADS):
                        mm = pe.matmul(ps_o[:, head_at(h)], intra[:, t % 2, h], v_new[:, t % 2, h * DV:(h + 1) * DV],
                                       start=False, stop=True, skip_group_check=True)
                    mm.then_inc(o_done, 1)

    ph.close()


def merge(nc, g, d):
    ph = Scope(nc, "merge")
    KA, KB = HEADS // 2, KD
    K = KA + KB
    raw = [g.merge_raw, ph.sb("raw", [P, K * P])]
    w_hi, w_lo = ph.sb("w_hi", [P, 2, K, P], F32R), ph.sb("w_lo", [P, 2, K, P], F32R)
    OR = 4
    o_raw = ph.sb("o_raw", [P, OR, S])
    o_hi, o_lo = ph.sb("o_hi", [P, K, S], F32R), ph.sb("o_lo", [P, K, S], F32R)
    gates = ph.sb("gates", [P, 2, 2, S])
    ps = [[ph.ps(f"s{s}_{i}", [P, S]) for i in range(2)] for s in range(2)]
    ld, ld_g, ld_o = [g.merge_ld, ph.sem("ld")], ph.sems("ld_g", 2), ph.sems("ld_o", OR)
    oh_done, ol_done, hi_done, lo_done, mm_done, part_done, out_done = (
        ph.sem(n) for n in ("oh_done", "ol_done", "hi_done", "lo_done", "mm_done", "part_done", "out_done"))
    block = ph.stack.enter_context(nc.Block())

    @block.sync
    def _(sp):
        def load_w(m):
            if m >= 2:
                sp.wait_ge(lo_done, m - 1)
            sp.dma_start(raw[m % 2][:], d["w_merge"][m]).then_inc(ld[m % 2], 16)

        def load_gates(m):
            if m >= 2:
                sp.wait_ge(out_done, m - 1)
            for i in range(2):
                sp.dma_start(gates[:, m % 2, i], d["proj"][B_GATE + i * KD + m]).then_inc(ld_g[m % 2], 16)

        for k in range(K):
            if k >= OR:
                sp.wait_ge(ol_done, k - OR + 1)
            src = d["o_a"][k] if k < KA else d["o_b"][k - KA]
            sp.dma_start(o_raw[:, k % OR], src).then_inc(ld_o[k % OR], 16)
            if k == KA - 1:
                load_w(1)
        load_gates(0)
        load_gates(1)
        sp.dma_start(g.out_raw[:, 0:KD * P], d["w_out"][0]).then_inc(g.out_ld, 16)
        for m in range(2, KD):
            load_w(m)
            load_gates(m)

    @block.scalar
    def _(act):
        def split(m):
            act.wait_ge(ld[m % 2], 16 * (m // 2 + 1))
            if m >= 2:
                act.wait_ge(mm_done, m - 1)
            act.activation(w_hi[:, m % 2].rearrange("p k n -> p (k n)"), raw[m % 2][:], ACT.Copy).then_inc(hi_done, 1)

        split(0)
        for k in range(K):
            act.wait_ge(ld_o[k % OR], 16 * (k // OR + 1))
            act.activation(o_hi[:, k], o_raw[:, k % OR], ACT.Copy).then_inc(oh_done, 1)
            if k == KA:
                split(1)
        for m in range(2, KD):
            split(m)

    @block.gpsimd
    def _(pool):
        def low(m):
            pool.wait_ge(hi_done, m + 1)
            pool.tensor_tensor(w_lo[:, m % 2].rearrange("p k n -> p (k n)"), raw[m % 2][:],
                               as_f32(w_hi[:, m % 2].rearrange("p k n -> p (k n)")), ALU.subtract).then_inc(lo_done, 1)

        low(0)
        for m in range(1, KD):
            low(m)
            pool.wait_ge(part_done, 2 * m)
            pool.tensor_tensor(g.y_a[:, m - 1], gates[:, (m - 1) % 2, 0], gates[:, (m - 1) % 2, 1], ALU.add)\
                .then_inc(out_done, 1)
        pool.wait_ge(part_done, 2 * KD)
        pool.tensor_tensor(g.y_a[:, KD - 1], gates[:, (KD - 1) % 2, 0], gates[:, (KD - 1) % 2, 1], ALU.add)\
            .then_inc(out_done, 1)

    @block.vector
    def _(dve):
        for k in range(K):
            dve.wait_ge(oh_done, k + 1)
            dve.tensor_tensor(o_lo[:, k], o_raw[:, k % OR], as_f32(o_hi[:, k]), ALU.subtract).then_inc(ol_done, 1)
        for m in range(KD):
            dve.wait_ge(mm_done, m + 1)
            dve.wait_ge(ld_g[m % 2], 32 * (m // 2 + 1))
            for i in range(2):
                gate = gates[:, m % 2, i]
                dve.tensor_tensor(gate, ps[m % 2][i][:], gate, ALU.mult).then_inc(part_done, 1)

    @block.tensor
    def _(pe):
        LAG = KA + 2
        order = []
        for k in range(K + LAG):
            order += [(0, k)] if k < K else []
            order += [(1, k - LAG)] if k >= LAG else []
        order += [(m, k) for m in range(2, KD) for k in range(K)]
        for m, k in order:
            s = m % 2
            if k == 0:
                pe.wait_ge(lo_done, m + 1)
                if m >= 2:
                    pe.wait_ge(part_done, 2 * (m - 1))
            if m == 0:
                pe.wait_ge(ol_done, k + 1)
            branch, first, last = (0, 0, KA - 1) if k < KA else (1, KA, K - 1)
            for i, (w, x) in enumerate(three(w_hi[:, s, k], w_lo[:, s, k], o_hi[:, k], o_lo[:, k])):
                for t in range(2):
                    cols = slice(t * HALF, (t + 1) * HALF)
                    mm = pe.matmul(ps[s][branch][:, cols], w, x[:, cols], start=k == first and i == 0,
                                   stop=k == last and i == 2)
            if k == K - 1:
                mm.then_inc(mm_done, 1)

    ph.close()


def output_and_up(nc, g, d):
    ph = Scope(nc, "up")
    raw = [g.out_raw, ph.sb("raw", [P, BLK])]
    w_hi, w_lo = ph.sb("w_hi", [P, 2, KD, P], F32R), ph.sb("w_lo", [P, 2, KD, P], F32R)
    taps = ph.sb("taps", [P, 2, W_EXTRA])
    u = ph.sb("u", [P, 2, S])
    hi, lo = g.h_hi, g.h_lo
    merged = g.y_a
    x2, xn = g.y_b[:, 0:KD], g.y_b[:, KD:KD + 3]
    sq, total = g.y_b[:, KD + 3], g.y_b[:, KD + 4]
    ps = [ph.ps(f"s{s}", [P, S]) for s in range(2)]
    ps_ss = ph.ps("ss", [P, S])
    ld, ld_x, st = [g.out_ld, ph.sem("ld")], ph.sems("ld_x", KD), ph.sem("st")
    mh_done, ml_done, x2_done, scaled_x = (ph.sem(n) for n in ("mh_done", "ml_done", "x2_done", "scaled_x"))
    sq_done, add_done, ss_done, std_done, rstd_done = (
        ph.sem(n) for n in ("sq_done", "add_done", "ss_done", "std_done", "rstd_done"))
    xn_pool, xn_dve, hh_done, hl_done = (ph.sem(n) for n in ("xn_pool", "xn_dve", "hh_done", "hl_done"))
    hi_done, lo_done, mm_done, scaled, conv, gate_done, y_done = (
        ph.sem(n) for n in ("hi_done", "lo_done", "mm_done", "scaled", "conv", "gate_done", "y_done"))
    block = ph.stack.enter_context(nc.Block())
    J0, J1 = KD // 2, KD // 2 + KF
    ON_DVE = (0, 3, 6)

    def normalised(k):
        return (xn_dve, ON_DVE.index(k) + 1) if k in ON_DVE else (xn_pool, k - sum(j < k for j in ON_DVE) + 1)

    @block.sync
    def _(sp):
        def load(n, s):
            src = d["w_up"][n - KD] if isinstance(n, int) else d["w_up"][bass.ds(n - KD, 1)].rearrange("o p n -> p (o n)")
            sp.dma_start(raw[s][:], src).then_inc(ld[s], 16)

        for m in range(KD):
            if m >= 2:
                sp.wait_ge(lo_done, m - 1)
            if m:
                sp.dma_start(raw[m % 2][:, 0:KD * P], d["w_out"][m]).then_inc(ld[m % 2], 16)
            sp.dma_start(x2[:, m], d["xT"][m]).then_inc(ld_x[m], 16)
        for s in range(2):
            sp.wait_ge(lo_done, KD - 1 + s)
            load(KD + s, s)
        for m in range(KD):
            sp.wait_ge(x2_done, m + 1)
            sp.dma_start(d["x2"][m], x2[:, m]).then_inc(st, 16)
        with sp.Fori(J0, J1 - 1) as j:
            for s in range(2):
                sp.wait_ge(lo_done, 2 * j + s + 1)
                load(2 * j + s + 2, s)
        sp.wait_ge(st, 16 * KD)
        for s in range(2):
            sp.dma_start(g.next_raw[:, s], d["w_down"][0, s]).then_inc(g.next_ld[s], 16)

    @block.scalar
    def _(act):
        def split(j, s, first=False):
            act.wait_ge(ld[s], 16 * j + 16)
            if not first:
                act.wait_ge(mm_done, 2 * j + s - 1)
            act.activation(w_hi[:, s], raw[s][:, 0:KD * P].rearrange("p (k m) -> p k m", k=KD), ACT.Copy)\
               .then_inc(hi_done, 1)

        def scale(j, s, first=False):
            act.wait_ge(mm_done, 2 * j + s + 1)
            if not first:
                act.wait_ge(y_done, j - J0)
            act.activation(u[:, s], ps[s][:], ACT.Identity, scale=taps[:, s, 2:3], bias=taps[:, s, 3:4])\
               .then_inc(scaled, 1)

        def silu(j):
            act.wait_ge(conv, 4 * (j - J0) + 2)
            act.activation(u[:, 0], u[:, 0], ACT.Silu).then_inc(gate_done, 1)

        split(0, 0, True)
        for k in range(KD):
            act.activation(hi[:, k], merged[:, k], ACT.Copy).then_inc(mh_done, 1)
        for m in range(KD):
            if m + 1 < KD:
                split((m + 1) // 2, (m + 1) % 2, m == 0)
            act.wait_ge(x2_done, m + 1)
            if m:
                act.wait_ge(add_done, m + 1)
            act.activation(sq, x2[:, m], ACT.Square).then_inc(sq_done, 1)
        split(J0, 0)
        act.wait_ge(ss_done, 1)
        act.activation(sq, ps_ss[:], ACT.Sqrt, scale=1.0 / D, bias=g.eps[:]).then_inc(std_done, 1)
        act.wait_ge(st, 16 * KD)
        for k in range(KD):
            act.activation(x2[:, k], x2[:, k], ACT.Copy, scale=g.mod[:, 4 * KD + k:4 * KD + k + 1]).then_inc(scaled_x, 1)
            if k == KD - 1:
                split(J0, 1)
            if k >= 3:
                high_h2 = k - 3
                act.wait_ge(*normalised(high_h2))
                act.activation(hi[:, high_h2], xn[:, high_h2 % 3], ACT.Identity, bias=g.mod[:, 3 * KD + high_h2:3 * KD + high_h2 + 1])\
                   .then_inc(hh_done, 1)
        for k in range(KD - 3, KD):
            act.wait_ge(*normalised(k))
            act.activation(hi[:, k], xn[:, k % 3], ACT.Identity, bias=g.mod[:, 3 * KD + k:3 * KD + k + 1])\
               .then_inc(hh_done, 1)
        scale(J0, 0, True)
        split(J0 + 1, 0)
        silu(J0)
        scale(J0, 1, True)
        with act.Fori(J0 + 1, J1 - 1) as j:
            split(j, 1)
            scale(j, 0)
            split(j + 1, 0)
            silu(j)
            scale(j, 1)
        split(J1 - 1, 1)
        scale(J1 - 1, 0)
        silu(J1 - 1)
        scale(J1 - 1, 1)

    @block.gpsimd
    def _(pool):
        def low(j, s):
            pool.tensor_tensor(w_lo[:, s], raw[s][:, 0:KD * P].rearrange("p (k m) -> p k m", k=KD),
                               as_f32(w_hi[:, s]), ALU.subtract)
            pool.tensor_copy(taps[:, s], raw[s][:, KD * P:BLK]).then_inc(lo_done, 1)

        def low_out(m):
            pool.wait_ge(hi_done, m + 1)
            pool.tensor_tensor(w_lo[:, m % 2], raw[m % 2][:, 0:KD * P].rearrange("p (k m) -> p k m", k=KD),
                               as_f32(w_hi[:, m % 2]), ALU.subtract).then_inc(lo_done, 1)

        pool.memset(total, 0.0).then_inc(add_done, 1)
        low_out(0)
        for m in range(KD):
            if m + 1 < KD:
                low_out(m + 1)
            if m < KD - 1:
                pool.wait_ge(sq_done, m + 1)
                pool.wait_ge(add_done, m + 1)
                pool.tensor_tensor(total, total, sq, ALU.add).then_inc(add_done, 1)
        pool.wait_ge(hi_done, KD + 1)
        low(J0, 0)
        pool.wait_ge(rstd_done, 1)
        for k in range(KD):
            if k in ON_DVE:
                continue
            if k >= 3:
                pool.wait_ge(hl_done, k - 2)
            pool.wait_ge(scaled_x, k + 1)
            pool.tensor_tensor(xn[:, k % 3], x2[:, k], total, ALU.mult).then_inc(xn_pool, 1)
        pool.wait_ge(hi_done, KD + 2)
        low(J0, 1)
        with pool.Fori(J0 + 1, J1) as j:
            for s in range(2):
                pool.wait_ge(hi_done, 2 * j + s + 1)
                pool.wait_ge(conv, 4 * (j - J0 - 1) + 2 * s + 2)
                low(j, s)

    @block.vector
    def _(dve):
        for k in range(KD):
            dve.wait_ge(mh_done, k + 1)
            dve.tensor_tensor(lo[:, k], merged[:, k], as_f32(hi[:, k]), ALU.subtract).then_inc(ml_done, 1)
        for m in range(KD):
            dve.wait_ge(mm_done, m + 1)
            dve.wait_ge(ld_x[m], 16)
            dve.scalar_tensor_tensor(x2[:, m], ps[m % 2][:], g.mod[:, 2 * KD + m:2 * KD + m + 1], x2[:, m],
                                     ALU.mult, ALU.add).then_inc(x2_done, 1)
        dve.wait_ge(std_done, 1)
        dve.reciprocal(total, sq).then_inc(rstd_done, 1)
        dve.wait_ge(rstd_done, 1)

        def normalise(k):
            if k >= 3:
                dve.wait_ge(hl_done, k - 2)
            dve.wait_ge(scaled_x, k + 1)
            dve.tensor_tensor(xn[:, k % 3], x2[:, k], total, ALU.mult).then_inc(xn_dve, 1)

        normalise(0)
        for k in range(KD):
            dve.wait_ge(hh_done, k + 1)
            dve.scalar_tensor_tensor(lo[:, k], xn[:, k % 3], g.mod[:, 3 * KD + k:3 * KD + k + 1], as_f32(hi[:, k]),
                                     ALU.add, ALU.subtract).then_inc(hl_done, 1)
            if k + 3 in ON_DVE:
                normalise(k + 3)

        def gated(j, y):
            for s in range(2):
                dve.wait_ge(scaled, 2 * (j - J0) + s + 1)
                for back in (1, 2):
                    if back == 2:
                        dve.wait_ge(conv, 4 * (j - J0) + 2 * s + 1)
                    dve.scalar_tensor_tensor(u[:, s, back:S], ps[s][:, 0:S - back], taps[:, s, 2 - back:3 - back],
                                             u[:, s, back:S], ALU.mult, ALU.add).then_inc(conv, 1)
            dve.wait_ge(conv, 4 * (j - J0) + 4)
            dve.wait_ge(gate_done, j - J0 + 1)
            dve.tensor_tensor(y, u[:, 0:1], u[:, 1:2], ALU.mult).then_inc(y_done, 1)

        with dve.Fori(J0, J0 + KD) as j:
            gated(j, g.y_a[:, bass.ds(j - J0, 1)])
        with dve.Fori(J0 + KD, J1) as j:
            gated(j, g.y_b[:, bass.ds(j - (J0 + KD), 1)])

    @block.tensor
    def _(pe):
        def product(n, s, ready=None):
            for k in range(KD):
                if ready is not None:
                    pe.wait_ge(ready, k + 1)
                for i, (w, x) in enumerate(three(w_hi[:, s, k], w_lo[:, s, k], g.h_hi[:, k], g.h_lo[:, k])):
                    for t in range(2):
                        cols = slice(t * HALF, (t + 1) * HALF)
                        mm = pe.matmul(ps[s][:, cols], w, x[:, cols], start=k == 0 and i == 0,
                                       stop=k == KD - 1 and i == 2)
            mm.then_inc(mm_done, 1)

        for m in range(KD):
            pe.wait_ge(lo_done, m + 1)
            if m >= 2:
                pe.wait_ge(x2_done, m - 1)
            product(m, m % 2, ml_done if m == 0 else None)
        for i, (part, ready) in enumerate(((total, add_done), (sq, sq_done))):
            pe.wait_ge(ready, KD)
            for t in range(2):
                cols = slice(t * HALF, (t + 1) * HALF)
                mm = pe.matmul(ps_ss[:, cols], g.const[:, C_ONES:C_ONES + P], part[:, cols], start=i == 0, stop=i == 1)
        mm.then_inc(ss_done, 1)
        for s in range(2):
            pe.wait_ge(lo_done, KD + s + 1)
            pe.wait_ge(x2_done, KD - 1 + s)
            product(KD + s, s, hl_done if s == 0 else None)
        with pe.Fori(J0 + 1, J1) as j:
            for s in range(2):
                pe.wait_ge(lo_done, 2 * j + s + 1)
                pe.wait_ge(conv, 4 * (j - J0 - 1) + 2 * s + 2)
                product(2 * j + s, s)

    ph.close()


def ffn_down(nc, g, d):
    ph = Scope(nc, "down")
    MB = DOWN
    W = MB * P
    raw, ld = g.next_raw, g.next_ld
    w_hi, w_lo = ph.sb("w_hi", [P, 2, W], F32R), ph.sb("w_lo", [P, 2, W], F32R)
    y_hi, y_lo = ph.sb("y_hi", [P, 2, S], F32R), ph.sb("y_lo", [P, 2, S], F32R)
    x3 = ph.sb("x3", [P, KD, S])
    sq, total = ph.sb("sq", [P, 2, S]), ph.sb("total", [P, S])
    std, rstd = ph.sb("std", [P, S]), ph.sb("rstd", [P, S])
    ps = [ph.ps(f"m{m}", [P, S]) for m in range(MB)]
    ld_x, st = ph.sem("ld_x"), ph.sem("st")
    wh_done, wl_done, yh_done, yl_done, mm_done, last_done, x3_done = (
        ph.sem(n) for n in ("wh_done", "wl_done", "yh_done", "yl_done", "mm_done", "last_done", "x3_done"))
    sq_done, add_done, ss_done, std_done, rstd_done = (
        ph.sem(n) for n in ("sq_done", "add_done", "ss_done", "std_done", "rstd_done"))
    weighted, out_dve, out_pool = (ph.sem(n) for n in ("weighted", "out_dve", "out_pool"))
    ON_DVE, ON_POOL = (0, 1, 3, 4, 6), (2, 5, 7)
    block = ph.stack.enter_context(nc.Block())
    parts = ((0, KD // 2, g.y_a, 0), (KD // 2, KF // 2, g.y_b, KD))

    @block.sync
    def _(sp):
        w = d["w_down"].rearrange("g k p n -> (g k) p n")

        def load(n, s):
            src = w[n] if isinstance(n, int) else w[bass.ds(n, 1)].rearrange("o p n -> p (o n)")
            sp.dma_start(raw[:, s], src).then_inc(ld[s], 16)

        sp.dma_start(x3[:], d["x2"].rearrange("m p n -> p m n")).then_inc(ld_x, 16)
        with sp.Fori(0, KF - 1) as j:
            for s in range(2):
                sp.wait_ge(wl_done, 2 * j + s + 1)
                load(2 * j + s + 2, s)
        for m in range(KD):
            done, own = (out_dve, ON_DVE) if m in ON_DVE else (out_pool, ON_POOL)
            sp.wait_ge(done, own.index(m) + 1)
            sp.dma_start(d["out"][m], x3[:, m]).then_inc(st, 16)
        sp.wait_ge(st, 16 * KD)

    @block.scalar
    def _(act):
        def split(n, s, y, read=None):
            act.wait_ge(ld[s], 8 * (n - s) + 16)
            if read:
                act.wait_ge(*read)
            act.activation(w_hi[:, s], raw[:, s], ACT.Copy).then_inc(wh_done, 1)
            act.activation(y_hi[:, s:s + 1], y, ACT.Copy).then_inc(yh_done, 1)

        def square(m):
            act.wait_ge(x3_done, m + 1)
            if m >= 2:
                act.wait_ge(*((add_done, m) if m - 2 < MB else (ss_done, m - 1 - MB)))
            act.activation(sq[:, m % 2], x3[:, m], ACT.Square).then_inc(sq_done, 1)
            act.wait_ge(sq_done, m + 1)
            if m < KD - 1:
                weigh(m)

        def weigh(m):
            act.activation(x3[:, m], x3[:, m], ACT.Copy, scale=g.small["norms"][:, 2 * KD + m:2 * KD + m + 1])\
               .then_inc(weighted, 1)

        split(0, 0, g.y_a[:, 0:1])
        split(1, 1, g.y_a[:, 1:2])
        for first, end, y, y0 in parts:
            with act.Fori(max(first, 1), end) as j:
                for s in range(2):
                    split(2 * j + s, s, y[:, bass.ds(2 * j + s - y0, 1)], (mm_done, 2 * j + s - 1))
        split(KF, 0, g.y_a[:, 0:1], (mm_done, KF - 1))
        split(KF + 1, 1, g.y_a[:, 1:2], (last_done, MB))
        for m in range(MB):
            square(m)
        for first, end, y, y0 in parts:
            with act.Fori(KF // 2 + max(first, 1), KF // 2 + end) as j:
                for s in range(2):
                    split(2 * j + s, s, y[:, bass.ds(2 * j + s - KF - y0, 1)], (mm_done, 2 * j + s - 2))
        for m in range(MB, KD):
            square(m)
        act.wait_ge(ss_done, MB)
        act.activation(std[:], ps[0][:], ACT.Sqrt, scale=1.0 / D, bias=g.eps[:]).then_inc(std_done, 1)
        weigh(KD - 1)

    @block.gpsimd
    def _(pool):
        pool.memset(total[:], 0.0).then_inc(add_done, 1)
        for first, end in ((0, KF // 2 + 1), (KF // 2 + 1, KF)):
            with pool.Fori(first, end) as j:
                for s in range(2):
                    pool.wait_ge(wh_done, 2 * j + s + 1)
                    pool.tensor_tensor(w_lo[:, s], raw[:, s], as_f32(w_hi[:, s]), ALU.subtract).then_inc(wl_done, 1)
            if first == 0:
                for m in range(MB):
                    pool.wait_ge(sq_done, m + 1)
                    pool.wait_ge(add_done, m + 1)
                    pool.tensor_tensor(total[:], total[:], sq[:, m % 2], ALU.add).then_inc(add_done, 1)
        pool.wait_ge(rstd_done, 1)
        for m in ON_POOL:
            pool.wait_ge(weighted, m + 1)
            pool.tensor_tensor(x3[:, m], x3[:, m], rstd[:], ALU.mult).then_inc(out_pool, 1)

    @block.vector
    def _(dve):
        def low(n, s, y):
            dve.wait_ge(yh_done, n + 1)
            dve.tensor_tensor(y_lo[:, s:s + 1], y, as_f32(y_hi[:, s:s + 1]), ALU.subtract)\
               .then_inc(yl_done, 1)

        def residual(grp):
            for m in range(MB):
                n = grp * MB + m
                dve.wait_ge(last_done, n + 1)
                if n == 0:
                    dve.wait_ge(ld_x, 16)
                dve.scalar_tensor_tensor(x3[:, n], ps[m][:], g.mod[:, 5 * KD + n:5 * KD + n + 1], x3[:, n],
                                         ALU.mult, ALU.add).then_inc(x3_done, 1)

        for first, end, y, y0 in parts:
            with dve.Fori(first, end) as j:
                for s in range(2):
                    low(2 * j + s, s, y[:, bass.ds(2 * j + s - y0, 1)])
        low(KF, 0, g.y_a[:, 0:1])
        residual(0)
        low(KF + 1, 1, g.y_a[:, 1:2])
        for first, end, y, y0 in parts:
            with dve.Fori(KF // 2 + max(first, 1), KF // 2 + end) as j:
                for s in range(2):
                    low(2 * j + s, s, y[:, bass.ds(2 * j + s - KF - y0, 1)])
        residual(1)
        dve.wait_ge(std_done, 1)
        dve.reciprocal(rstd[:], std[:]).then_inc(rstd_done, 1)
        dve.wait_ge(rstd_done, 1)
        for m in ON_DVE:
            dve.wait_ge(weighted, m + 1)
            dve.tensor_tensor(x3[:, m], x3[:, m], rstd[:], ALU.mult).then_inc(out_dve, 1)

    @block.tensor
    def _(pe):
        def step(n, s, grp, first=False, last=False):
            pe.wait_ge(wl_done, n + 1)
            pe.wait_ge(yl_done, n + 1)
            for m in range(MB):
                if first and grp:
                    pe.wait_ge(x3_done, m + 1)
                cut = slice(m * P, (m + 1) * P)
                for i, (w, x) in enumerate(three(w_hi[:, s, cut], w_lo[:, s, cut], y_hi[:, s], y_lo[:, s])):
                    for t in range(2):
                        cols = slice(t * HALF, (t + 1) * HALF)
                        mm = pe.matmul(ps[m][:, cols], w, x[:, cols], start=first and i == 0, stop=last and i == 2)
                if last:
                    mm.then_inc(last_done, 1)
                elif m == MB - 1:
                    mm.then_inc(mm_done, 1)

        for grp in range(2):
            n0 = grp * KF
            step(n0, 0, grp, first=True)
            step(n0 + 1, 1, grp)
            with pe.Fori(grp * KF // 2 + 1, (grp + 1) * KF // 2 - 1) as j:
                for s in range(2):
                    step(2 * j + s, s, grp)
            step(n0 + KF - 2, 0, grp)
            step(n0 + KF - 1, 1, grp, last=True)
        pe.wait_ge(add_done, MB + 1)
        pe.wait_ge(x3_done, MB + 1)
        for m in range(MB - 1, KD):
            if m >= MB:
                pe.wait_ge(sq_done, m + 1)
            for t in range(2):
                cols = slice(t * HALF, (t + 1) * HALF)
                part = total[:, cols] if m < MB else sq[:, m % 2, cols]
                mm = pe.matmul(ps[0][:, cols], g.const[:, C_ONES:C_ONES + P], part, start=m < MB, stop=m == KD - 1)
            if m >= MB:
                mm.then_inc(ss_done, 1)

    ph.close()

SCRATCH = {"proj": (N_PROJ, P, S), "systems": (SOLVES, CHUNK, CHUNK), "solved": (SOLVES, CHUNK, CHUNK),
           "q_decayed": (HEADS // 2, P, S), "k_beta": (P, TILES, HEADS * DK), "k_rest": (P, TILES, HEADS * DK),
           "value": (P, TILES, HEADS * DV), "intra": (TILES, P, HEADS * P),
           "o_a": (HEADS // 2, P, S), "o_b": (HEADS, P, S), "x2": (KD, P, S), "out": (KD, P, S)}
OUT = ("out",)


def finish(r):
    return r["out"].reshape(D, S).T.reshape(1, S, D)


class Shared:
    pass


def build(nc, d):
    with ExitStack() as stack:
        sb = lambda name, shape, dt=F32: stack.enter_context(nc.sbuf_tensor(name, shape, dt))
        g = Shared()
        g.const = sb("const", [P, C_RESET])
        g.eps = sb("eps", [P, 1])
        g.c_act = sb("c_act", [P, KD])
        g.mod = sb("mod", [P, 6 * KD])
        g.small = {"b_ada": sb("b_ada", [P, 6 * KD]), "norms": sb("norms", [P, 3 * KD]),
                   "dn_norm": sb("dn_norm", [P, 1]), "dn_head": sb("dn_head", [HEADS, 2])}
        def hidden(scope, n):
            g.h_hi = scope.sb(f"{n}_hi", [P, KD, S], F32R)
            g.h_lo = scope.sb(f"{n}_lo", [P, KD, S], F32R)

        scope = Scope(nc, "h1")
        hidden(scope, "h1")
        g.next_raw, g.next_ld = scope.sb("next_raw", [P, 2, KD * P]), scope.sems("next_ld", 2)
        project_a(nc, g, d)
        project_b(nc, g, d)
        scope.close()
        first = Scope(nc, "first")
        K_MERGE = HEADS // 2 + KD
        g.merge_raw, g.merge_ld = first.sb("merge_raw", [P, K_MERGE * P]), first.sem("merge_ld")
        stick(nc, g, d)
        mlp = Scope(nc, "mlp")
        g.y_a = mlp.sb("y_a", [P, KD, S])
        g.out_raw, g.out_ld = mlp.sb("out_raw", [P, BLK]), mlp.sem("out_ld")
        merge(nc, g, d)
        g.y_b = mlp.sb("y_b", [P, KF - KD, S])
        h2 = Scope(nc, "h2", side="right")
        hidden(h2, "h2")
        g.next_raw, g.next_ld = mlp.sb("next_raw", [P, 2, DOWN * P]), mlp.sems("next_ld", 2)
        output_and_up(nc, g, d)
        h2.close()
        ffn_down(nc, g, d)
        mlp.close()
        first.close()


def constants():
    import numpy as np

    t = np.zeros((P, C_END), np.float32)
    i, j = np.arange(P)[:, None], np.arange(P)[None]
    chunk = i // 64 == j // 64
    t[:, C_IDENT:C_IDENT + P] = i == j
    t[:, C_ONES:C_ONES + P] = 1
    t[:, C_ONES64:C_ONES64 + P] = chunk
    t[:, C_INCL:C_INCL + P] = chunk & (j >= i)
    t[:, C_STRICT:C_STRICT + P] = chunk & (i > j)
    for h in range(HEADS):
        t[h, C_SEL + h // 2 * P + h % 2 * 64:C_SEL + h // 2 * P + h % 2 * 64 + 64] = 1
    t[:, C_NEG:C_NEG + P] = np.where(j >= i, NEG, 0)
    t[:64, C_EVEN:C_EVEN + P] = 1
    t[64:, C_ODD:C_ODD + P] = 1
    t[:, C_RESET:C_RESET + S] = (np.arange(S) % 64 != 0)[None]
    return t


def kernel(x, c, w_ada, b_ada, norm1_w, w_in, dn_conv_w, dn_A_log, dn_dt_bias, dn_norm_w,
           w_proj_sb, w_proj_dn, w_out, norm2_w, w_ffn_in, ffn_conv_w, ffn_conv_b, w_ffn_out,
           final_norm_w):
    import numpy as np
    import concourse.bacc as bacc
    from concourse.bass_utils import run_bass_kernel_spmd

    def column(v):
        return np.asarray(v).reshape(-1, P).T

    def blocks(w, cols, extra=None, pad=0):
        out = []
        for b, c0 in enumerate(cols):
            part = w[:, c0:c0 + P].reshape(-1, P, P).transpose(1, 0, 2).reshape(P, -1)
            tail = np.zeros((P, pad), np.float32) if extra is None or extra[b] is None else extra[b]
            out.append(np.concatenate([part, tail], 1))
        return np.stack(out)

    sb, ab = 12 * P, 36 * P
    cols = [ab] + [sb + b * P for b in range(24)] + [b * P for b in range(12)] + [ab + 16 + b * P for b in range(16)]
    conv = np.asarray(dn_conv_w)[0].T.reshape(16, P, W_EXTRA)
    taps = [None] * B_DN + list(conv) + [None] * (N_PROJ - B_Z)
    ffn_cols, ffn_taps = [], []
    fcw = np.asarray(ffn_conv_w)[0].T.reshape(2 * KF, P, 3)
    fcb = np.asarray(ffn_conv_b)[0].reshape(2 * KF, P, 1)
    for b in range(KF):
        for half in range(2):
            ffn_cols.append((half * KF + b) * P)
            ffn_taps.append(np.concatenate([fcw[half * KF + b], fcb[half * KF + b]], 1))
    m_cols = [b * P for b in range(KD)]
    ins = {
        "xT": np.asarray(x)[0].T.reshape(KD, P, S),
        "c": column(c[0]),
        "w_ada": np.asarray(w_ada)[0].reshape(2, 4, P, 6, D).transpose(3, 0, 2, 1, 4),
        "b_ada": column(b_ada[0]),
        "norms": np.concatenate([column(norm1_w[0]), column(norm2_w[0]), column(final_norm_w)], 1),
        "w_in": blocks(np.asarray(w_in)[0], cols, taps, W_EXTRA),
        "dn_norm": np.asarray(dn_norm_w)[0].reshape(P, 1),
        "dn_head": np.stack([np.asarray(dn_A_log)[0], np.asarray(dn_dt_bias)[0]], 1),
        "w_merge": np.concatenate([blocks(np.asarray(w_proj_sb)[0], m_cols),
                                   blocks(np.asarray(w_proj_dn)[0], m_cols)], 2),
        "w_out": blocks(np.asarray(w_out)[0], m_cols),
        "w_up": blocks(np.asarray(w_ffn_in)[0], ffn_cols, ffn_taps, W_EXTRA),
        "w_down": np.asarray(w_ffn_out)[0].reshape(KF, P, 2, 4 * P).transpose(2, 0, 1, 3),
        "const": constants(),
    }
    ins = {k + "_dram": np.ascontiguousarray(v) for k, v in ins.items()}
    nc = bacc.Bacc("TRN2", target_bir_lowering=False, num_devices=1)
    d = {k[:-5]: nc.dram_tensor(k, v.shape, F32, kind="ExternalInput").ap() for k, v in ins.items()}
    d["reset"] = d["const"][0:HEADS, C_RESET:C_END]
    d["const"] = d["const"][:, 0:C_RESET]
    for name, shape in SCRATCH.items():
        d[name] = nc.dram_tensor(name + "_dram", shape, F32, kind="ExternalOutput" if name in OUT else "Internal").ap()
    build(nc, d)
    r = run_bass_kernel_spmd(nc, [ins], core_ids=[0])
    return finish({name: r.results[0][name + "_dram"] for name in OUT})
```
